# Optimizing a Trainium2 kernel written in Bass

```python
import jax, jax.numpy as jnp
from jax import lax
import numpy as np

D_MODEL = 1024
BATCH = 1
SEQ = 512
DEPTH = 1
DEC_BATCH = 8
DEC_SEQ = 8
PAST_LEN = 4096
PAGE_SIZE = 128

N_META = 16
D_RNN = D_MODEL
RG_BLOCKS = 16
RG_BS = D_RNN // RG_BLOCKS
CONV_W = 4
RG_C = 8.0
GLA_HEADS = 4
GLA_DK = D_MODEL // 2 // GLA_HEADS
GLA_DV = D_MODEL // GLA_HEADS
GLA_RANK = 16
GLA_TAU = 16.0
GLA_CHUNK = 16
PEER_HEADS = 8
PEER_NKEYS = 128
PEER_EXPERTS = PEER_NKEYS * PEER_NKEYS
PEER_TOPK = 16
PEER_DQ = 256
PEER_BLOCK = 256
EPS = 1e-6
IN_SIZES = (D_RNN, D_RNN, GLA_HEADS * GLA_DK, GLA_HEADS * GLA_DK, GLA_HEADS * GLA_DV, GLA_HEADS * GLA_DV, GLA_RANK, D_MODEL, D_MODEL)
D_IN = D_RNN * 2 + GLA_HEADS * GLA_DK * 2 + GLA_HEADS * GLA_DV * 2 + GLA_RANK + D_MODEL * 2

kernel_name = 'hawk_gla_peer_hybrid_step'

F32 = jnp.float32

def rmsnorm(x, g):
    xf = x.astype(F32)
    y = xf * lax.rsqrt(jnp.mean(xf * xf, axis=-1, keepdims=True) + EPS)
    return (y * g.astype(F32)).astype(x.dtype)

def split_in(z):
    outs, off = [], 0
    for s in IN_SIZES:
        outs.append(z[..., off:off + s])
        off += s
    return outs

def causal_conv(x, buf, w, b):
    T = x.shape[1]
    xp = jnp.concatenate([buf.astype(x.dtype), x], axis=1)
    y = b + xp[:, 0:T] * w[0]
    for j in range(1, CONV_W):
        y = y + xp[:, j:j + T] * w[j]
    return y, xp[:, -(CONV_W - 1):]

def rglru(x, h0, wa, ba, wx, bx, lam):
    B, T, _ = x.shape
    xf = x.astype(F32)
    xb = xf.reshape(B, T, RG_BLOCKS, RG_BS)
    r = jax.nn.sigmoid(jnp.einsum('btnc,ncd->btnd', xb, wa.astype(F32)).reshape(B, T, D_RNN) + ba.astype(F32))
    i = jax.nn.sigmoid(jnp.einsum('btnc,ncd->btnd', xb, wx.astype(F32)).reshape(B, T, D_RNN) + bx.astype(F32))
    log_a = -RG_C * r * jax.nn.softplus(-lam.astype(F32))
    a = jnp.exp(log_a)
    u = jnp.sqrt(-jnp.expm1(2.0 * log_a)) * (i * xf)

    def comb(lhs, rhs):
        a1, b1 = lhs
        a2, b2 = rhs
        return a1 * a2, a2 * b1 + b2

    a_cum, h = lax.associative_scan(comb, (a, u), axis=1)
    h = h + a_cum * h0.astype(F32)[:, None]
    return h.astype(x.dtype), h[:, -1].astype(h0.dtype)

def gla_scan(q, k, v, g, S0, front):
    B, T = q.shape[:2]
    end = (-(front + T)) % GLA_CHUNK
    pw = ((0, 0), (front, end), (0, 0), (0, 0))
    q, k, v, g = [jnp.pad(z.astype(F32), pw) for z in (q, k, v, g)]
    n = (front + T + end) // GLA_CHUNK

    def to_chunks(z):
        return jnp.moveaxis(z.reshape(B, n, GLA_CHUNK, z.shape[2], z.shape[3]), 1, 0)

    causal = jnp.tril(jnp.ones((GLA_CHUNK, GLA_CHUNK), bool))[None, :, :, None, None]

    def step(S, inp):
        qc, kc, vc, gc = inp
        b = jnp.cumsum(gc, axis=1)
        o = jnp.einsum('bthk,bhkv->bthv', qc * jnp.exp(b), S)
        decay = jnp.exp(jnp.where(causal, b[:, :, None] - b[:, None], -jnp.inf))
        A = jnp.einsum('btshk,bshk->bths', qc[:, :, None] * decay, kc)
        o = o + jnp.einsum('bths,bshv->bthv', A, vc)
        bl = b[:, -1]
        S = jnp.exp(bl)[..., None] * S + jnp.einsum('bshk,bshv->bhkv', kc * jnp.exp(bl[:, None] - b), vc)
        return S, o

    S, o = lax.scan(step, S0.astype(F32), (to_chunks(q), to_chunks(k), to_chunks(v), to_chunks(g)))
    o = jnp.moveaxis(o, 0, 1).reshape(B, n * GLA_CHUNK, GLA_HEADS, GLA_DV)[:, front:front + T]
    return o, S

def peer(h, wq, k1, k2, u, v):
    B, T, D = h.shape
    N = B * T
    pad = (-N) % PEER_BLOCK
    hb_all = jnp.pad(h.reshape(N, D), ((0, pad), (0, 0))).reshape(-1, PEER_BLOCK, D)
    half = PEER_DQ // 2

    def block(hb):
        q = (hb @ wq).reshape(PEER_BLOCK, PEER_HEADS, PEER_DQ).astype(F32)
        s1 = jnp.einsum('nhd,hkd->nhk', q[..., :half], k1.astype(F32))
        s2 = jnp.einsum('nhd,hkd->nhk', q[..., half:], k2.astype(F32))
        v1, i1 = lax.top_k(s1, PEER_TOPK)
        v2, i2 = lax.top_k(s2, PEER_TOPK)
        cand = (v1[..., :, None] + v2[..., None, :]).reshape(PEER_BLOCK, PEER_HEADS, PEER_TOPK * PEER_TOPK)
        cidx = (i1[..., :, None] * PEER_NKEYS + i2[..., None, :]).reshape(PEER_BLOCK, PEER_HEADS, PEER_TOPK * PEER_TOPK)
        sv, pos = lax.top_k(cand, PEER_TOPK)
        idx = jnp.take_along_axis(cidx, pos, axis=-1)
        gate = jax.nn.softmax(sv, axis=-1)
        act = jax.nn.gelu(jnp.einsum('nd,nhkd->nhk', hb.astype(F32), u[idx].astype(F32)), approximate=False)
        return jnp.einsum('nhk,nhkd->nd', (gate * act).astype(hb.dtype), v[idx])

    out = lax.map(block, hb_all)
    return out.reshape(-1, D)[:N].reshape(B, T, D)

def trunk_layer(x, conv_buf, h0, S0, front, norm1_g, w_in, conv_w, conv_b, rg_wa, rg_ba, rg_wx, rg_bx, rg_lam,
                gla_wg, gla_bg, gla_norm_g, w_pa, w_pb, w_out, norm2_g, peer_wq, peer_k1, peer_k2, peer_u, peer_v):
    B, T, _ = x.shape
    hn = rmsnorm(x, norm1_g)
    xa, ga, q, k, v, r, gl, za, zb = split_in(hn @ w_in)
    xc, conv_new = causal_conv(xa, conv_buf, conv_w, conv_b)
    ha, h_new = rglru(xc, h0, rg_wa, rg_ba, rg_wx, rg_bx, rg_lam)
    ya = jax.nn.gelu(ga, approximate=False) * ha
    log_alpha = jax.nn.log_sigmoid((gl @ gla_wg + gla_bg).astype(F32)) / GLA_TAU
    qh = q.reshape(B, T, GLA_HEADS, GLA_DK) * (GLA_DK ** -0.5)
    kh = k.reshape(B, T, GLA_HEADS, GLA_DK)
    vh = v.reshape(B, T, GLA_HEADS, GLA_DV)
    gh = log_alpha.reshape(B, T, GLA_HEADS, GLA_DK)
    o, S_new = gla_scan(qh, kh, vh, gh, S0, front)
    o = rmsnorm(o, gla_norm_g).astype(x.dtype).reshape(B, T, GLA_HEADS * GLA_DV)
    yb = o * jax.nn.silu(r)
    m = jax.nn.sigmoid(za) * (ya @ w_pa) + jax.nn.sigmoid(zb) * (yb @ w_pb)
    x = x + m @ w_out
    x = x + peer(rmsnorm(x, norm2_g), peer_wq, peer_k1, peer_k2, peer_u, peer_v)
    return x, conv_new, h_new, S_new.astype(S0.dtype)

def setup_inputs(seed: int = 0) -> dict:
    key = jax.random.key(seed)
    ks = jax.random.split(key, 32)
    nrm = lambda i, shape, s: jax.random.normal(ks[i], shape, F32) * s
    u_lam = jax.random.uniform(ks[12], (DEPTH, D_RNN), F32, 0.9, 0.999)
    return {
        'x_prompt': nrm(0, (BATCH, SEQ, D_MODEL), 1.0),
        'x_sample': nrm(1, (DEC_BATCH, DEC_SEQ, D_MODEL), 1.0),
        'state_conv': nrm(2, (DEPTH, DEC_BATCH, CONV_W - 1, D_RNN), 1.0),
        'state_rglru': nrm(3, (DEPTH, DEC_BATCH, D_RNN), 0.5),
        'state_gla': nrm(4, (DEPTH, DEC_BATCH, GLA_HEADS, GLA_DK, GLA_DV), 0.3),
        'meta': nrm(5, (N_META, D_MODEL), 1.0),
        'norm1_g': 1.0 + nrm(6, (DEPTH, D_MODEL), 0.02),
        'w_in': nrm(7, (DEPTH, D_MODEL, D_IN), D_MODEL ** -0.5),
        'conv_w': nrm(8, (DEPTH, CONV_W, D_RNN), CONV_W ** -0.5),
        'conv_b': nrm(9, (DEPTH, D_RNN), 0.02),
        'rg_wa': nrm(10, (DEPTH, RG_BLOCKS, RG_BS, RG_BS), RG_BS ** -0.5),
        'rg_ba': nrm(11, (DEPTH, D_RNN), 0.02),
        'rg_wx': nrm(13, (DEPTH, RG_BLOCKS, RG_BS, RG_BS), RG_BS ** -0.5),
        'rg_bx': nrm(14, (DEPTH, D_RNN), 0.02),
        'rg_lam': jnp.log(u_lam) - jnp.log1p(-u_lam),
        'gla_wg': nrm(15, (DEPTH, GLA_RANK, GLA_HEADS * GLA_DK), GLA_RANK ** -0.5),
        'gla_bg': nrm(16, (DEPTH, GLA_HEADS * GLA_DK), 0.5),
        'gla_norm_g': 1.0 + nrm(17, (DEPTH, GLA_DV), 0.02),
        'w_pa': nrm(18, (DEPTH, D_RNN, D_MODEL), D_RNN ** -0.5),
        'w_pb': nrm(19, (DEPTH, GLA_HEADS * GLA_DV, D_MODEL), (GLA_HEADS * GLA_DV) ** -0.5),
        'w_out': nrm(20, (DEPTH, D_MODEL, D_MODEL), D_MODEL ** -0.5),
        'norm2_g': 1.0 + nrm(21, (DEPTH, D_MODEL), 0.02),
        'peer_wq': nrm(22, (DEPTH, D_MODEL, PEER_HEADS * PEER_DQ), D_MODEL ** -0.5),
        'peer_k1': nrm(23, (DEPTH, PEER_HEADS, PEER_NKEYS, PEER_DQ // 2), (PEER_DQ // 2) ** -0.5),
        'peer_k2': nrm(24, (DEPTH, PEER_HEADS, PEER_NKEYS, PEER_DQ // 2), (PEER_DQ // 2) ** -0.5),
        'peer_u': nrm(25, (DEPTH, PEER_EXPERTS, D_MODEL), D_MODEL ** -0.5),
        'peer_v': nrm(26, (DEPTH, PEER_EXPERTS, D_MODEL), PEER_HEADS ** -0.5),
        'normf_g': 1.0 + nrm(27, (D_MODEL,), 0.02),
    }

def reference(x_prompt, x_sample, state_conv, state_rglru, state_gla, meta, norm1_g, w_in, conv_w, conv_b,
              rg_wa, rg_ba, rg_wx, rg_bx, rg_lam, gla_wg, gla_bg, gla_norm_g, w_pa, w_pb, w_out, norm2_g,
              peer_wq, peer_k1, peer_k2, peer_u, peer_v, normf_g):
    B = x_prompt.shape[0]
    xp = jnp.concatenate([jnp.broadcast_to(meta[None].astype(x_prompt.dtype), (B, N_META, D_MODEL)), x_prompt], axis=1)
    xs = x_sample
    front_p = (-N_META) % GLA_CHUNK
    cps, hps, sps, css, hss, sss = [], [], [], [], [], []
    for l in range(DEPTH):
        w = (norm1_g[l], w_in[l], conv_w[l], conv_b[l], rg_wa[l], rg_ba[l], rg_wx[l], rg_bx[l], rg_lam[l],
             gla_wg[l], gla_bg[l], gla_norm_g[l], w_pa[l], w_pb[l], w_out[l], norm2_g[l],
             peer_wq[l], peer_k1[l], peer_k2[l], peer_u[l], peer_v[l])
        conv0 = jnp.zeros((B, CONV_W - 1, D_RNN), xp.dtype)
        h0 = jnp.zeros((B, D_RNN), state_rglru.dtype)
        S0 = jnp.zeros((B, GLA_HEADS, GLA_DK, GLA_DV), state_gla.dtype)
        xp, cp, hp, sp = trunk_layer(xp, conv0, h0, S0, front_p, *w)
        xs, cs, hs, ss = trunk_layer(xs, state_conv[l], state_rglru[l], state_gla[l], 0, *w)
        cps.append(cp); hps.append(hp); sps.append(sp)
        css.append(cs); hss.append(hs); sss.append(ss)
    y_prompt = rmsnorm(xp, normf_g)[:, N_META:]
    y_sample = rmsnorm(xs, normf_g)
    return (y_prompt, y_sample, jnp.stack(cps), jnp.stack(hps), jnp.stack(sps), jnp.stack(css), jnp.stack(hss), jnp.stack(sss))


_drawn_inputs = setup_inputs


def setup_inputs(seed=0):
    import zlib

    import numpy as np

    out = dict(_drawn_inputs(seed))
    spreads = {}
    factors = {'rg_ba': 8.0, 'rg_bx': 7.768, 'gla_norm_g': 3.06, 'normf_g': 9.625, 'norm2_g': 2.903}
    for name, (base, spread) in spreads.items():
        noise = np.random.default_rng([zlib.crc32(name.encode()), seed]).standard_normal(out[name].shape)
        drawn = base * np.exp(spread * noise) if base else spread * noise
        out[name] = __import__('jax').numpy.asarray(drawn.astype(out[name].dtype))
    for name, factor in factors.items():
        out[name] = (out[name] * factor).astype(out[name].dtype)
    return out
```

```python
import numpy as np

import concourse.bass as bass
from concourse import mybir
from concourse.bass import ds

F32 = mybir.dt.float32
F32R = mybir.dt.float32r
U8 = mybir.dt.uint8
U32 = mybir.dt.uint32
ALU = mybir.AluOpType
ACT = mybir.ActivationFunctionType
AX = mybir.AxisListType.X

P = 128
D = 1024
KT = D // P
META, SEQ = 16, 512
NSEQ, DEC = 8, 8
TP = META + SEQ
T = TP + NSEQ * DEC
H2 = T // 2
EPS = 1e-6
HEADS, DK, DV, RANK = 4, 128, 256, 16
CT = (T + P - 1) // P
LAST = T - (CT - 1) * P
PREST = TP - (CT - 1) * P
HALF = [64, 32, 16, 8, 4, 2, 1]
PH, NK, TOPK = 8, 128, 16
GB = 16
NGB = T // GB
E1G = 8
NGRP = NK // E1G

N_Q, N_K, N_V, N_XA, N_GA, N_ZA, N_R, N_ZB, N_OUT, N_WQ, N_U, N_D, N_END = (
    0, 4, 8, 16, 24, 32, 48, 56, 72, 80, 96, 224, 352)

LOOP1 = 52
LOOP2 = (NGB - 1) // 2
assert N_U + LOOP1 + 4 * LOOP2 + 4 == N_D and NGB == 2 * LOOP2 + 1
CONSTS = 16 * 8


def level_span(lv):
    hs = HALF[lv - 1]
    return (CT - 1) * P if hs > DEC else TP if hs == DEC else T


def level_tiles(lv):
    last = LAST if lv == 0 else level_span(lv) - (CT - 1) * P
    return [(c, P) for c in range(CT - 1)] + ([(CT - 1, last)] if last else [])


def turns_to(lv):
    return sum(len(level_tiles(v)) for v in range(lv + 1))


TURNS = turns_to(len(HALF))


COLS = {}
_n = 0
for _name, _w in (("norm1", 8), ("cw0", 8), ("cw1", 8), ("cw2", 8), ("cw3", 8), ("cb", 8), ("ba", 8), ("bx", 8),
                  ("lam", 8), ("norm2", 8), ("normf", 8), ("bg", 4), ("gng", 2)):
    COLS[_name] = _n
    _n += _w
NCOL = _n


def build(nc, xT, trunk, up, down, cols, masks, ident, reset, segmask, iota, wgl, wg, gates, keys, conv0, h0,
          gla0, a_dram, g_dram, yT, conv_out, h_out, gla_p, gla_s):
    def sem(name):
        return nc.semaphore(name).__enter__()

    base = 16512
    TB = KT * T * 4

    def at(name, shape, dt, off):
        return nc.alloc_sbuf_tensor_at(name, shape, dt, offset=base + off)

    o_ring = 0
    w_raw = [at(f"w_raw{i}", [P, KT, P], F32, o_ring + 4096 * i) for i in range(4)]
    w_hi = [at(f"w_hi{i}", [P, KT, P], F32R, o_ring + 16384 + 4096 * i) for i in range(2)]
    w_lo = [at(f"w_lo{i}", [P, KT, P], F32R, o_ring + 24576 + 4096 * i) for i in range(2)]
    o_const = 32768
    col = at("col", [P, NCOL], F32, o_const)
    small = at("small", [P, 64], F32, o_const + 512)
    idt = at("idt", [P, P], F32, o_const + 1024)
    ones = at("ones", [P, P], F32, o_const + 1536)
    iot = at("iot", [P, P], F32, o_const + 2048)
    rstd = at("rstd", [P, T], F32, o_const + 2560)
    o_x = o_const + 2560 + 2368
    x = at("x", [P, KT, T], F32, o_x)
    o_h = o_x + TB
    h_hi = at("h_hi", [P, KT, T], F32R, o_h)
    h_lo = at("h_lo", [P, KT, T], F32R, o_h + TB)
    r3 = o_h + 2 * TB
    r4 = r3 + TB
    r5 = r4 + CT * D * 4
    r6 = r5 + TB
    XPW = 3 + TP + NSEQ * (3 + DEC)
    r7 = r6 + KT * XPW * 4 + 32
    hn_raw = at("hn_raw", [P, KT, T], F32, r3)
    qk = at("qk", [P, KT, T], F32, r3)
    y_hi = at("y_hi", [P, KT, T], F32R, r3)
    v_nat = at("v_nat", [P, CT, D], F32, r4)
    y_lo = at("y_lo", [P, KT, T], F32R, r4)
    vT = at("vT", [P, KT, T], F32, r5)
    zed = [at(f"zed{i}", [P, HEADS, T], F32, r5 + i * TB // 2) for i in range(2)]
    o = at("o", [P, KT, T], F32, r5)
    hn2_raw = at("hn2_raw", [P, KT, T], F32, r5)
    xpad = at("xpad", [P, KT, XPW], F32, r6)
    g7 = r7
    attn = at("attn", [P, CT, HEADS, P], F32, g7)
    gtmp = at("gtmp", [P, HEADS, T], F32, g7)
    cum = at("cum", [P, HEADS, T], F32, g7 + 10240)
    st_p = at("st_p", [P, HEADS, DV], F32, g7 + 19712)
    st_s = [at(f"st_s{i}", [P, HEADS, DV], F32, g7 + 23808 + 4096 * i) for i in range(2)]
    lmask_in = at("lmask_in", [P, 8, P], F32, r5)
    lmask = at("lmask", [P, 8, P], U8, g7 + 32000)
    k_nat = at("k_nat", [P, HEADS * DK], F32, g7 + 33024)
    k_seg = at("k_seg", [P, HEADS * DK], F32, g7 + 35072)
    end_cum = at("end_cum", [P, HEADS, 16], F32, g7 + 37120)
    segm = at("segm", [P, NSEQ], F32, g7 + 37376)
    assert base + g7 + 37408 < 229368, g7
    wgl_sb = at("wgl_sb", [P, KT, RANK], F32, g7 + 19712)
    wg_sb = at("wg_sb", [RANK, HEADS * DK], F32, g7 + 20224)
    glT = at("glT", [RANK, T], F32, g7 + 22272)
    rst = at("rst", [P, T], F32, g7 + 24640)
    sq = at("sq", [P, 2, T], F32, g7 + 27008)
    ga = at("ga", [P, KT, T], F32, r7)
    mix = at("mix", [P, KT, T], F32, r7)
    t7 = r7 + TB
    xc = at("xc", [P, T], F32, t7)
    rr = at("rr", [P, T], F32, t7 + 2368)
    ii = at("ii", [P, T], F32, t7 + 2 * 2368)
    aa = at("aa", [P, T], F32, t7 + 3 * 2368)
    sq_o = at("sq_o", [P, 2, T], F32, t7)
    sgate = [at(f"sgate{i}", [P, T], F32, t7 + 2368 * i) for i in range(2)]
    prod = at("prod", [P, T], F32, t7 + 2 * 2368)
    c0sb = at("c0sb", [P, KT, NSEQ, 3], F32, t7 + 9472)
    h0sb = at("h0sb", [P, KT, NSEQ], F32, t7 + 10240)
    hfin = at("hfin", [P, KT, 1 + NSEQ], F32, t7 + 10496)
    cfin = at("cfin", [P, KT, 1 + NSEQ, 3], F32, t7 + 10784)
    gate_w = at("gate_w", [P, 2, KT, P], F32, t7 + 11648)
    assert base + t7 + 19840 < 229368
    hh = rstd
    s3 = r3
    scores = at("scores", [P, CT, 16, NK], F32, s3)
    oh2 = [at(f"oh2{i}", [P, GB, NK], F32, s3 + 8192 * i) for i in range(2)]
    oh1 = [at(f"oh1{i}", [P, GB, NK], F32, s3 + 16384 + 8192 * i) for i in range(2)]
    gst = [at(f"gst{i}", [P, NK, GB], F32, s3 + 32768 + 8192 * i) for i in range(2)]
    s4 = s3 + 49152
    keys_sb = at("keys_sb", [P, PH, 2, NK], F32, s4)
    qh = [at(f"qh{i}", [P, 2, T], F32, s4 + 8192 + 4736 * i) for i in range(2)]
    work = at("work", [P, 16, NK], F32, s4)
    cand = at("cand", [P, PH, TOPK, TOPK], F32, s4 + 8192)
    pick = at("pick", [P, PH, TOPK, TOPK], F32, s4 + 16384)
    ast = [at(f"ast{i}", [P, T], F32, s4 + 24576 + 2368 * i) for i in range(4)]
    s5 = s4 + 24576 + 4 * 2368
    chosen = at("chosen", [P, CT, 3, P], F32, s5)
    chT = at("chT", [P, 3, T], F32, s5 + 7680)
    s6 = s5 + 7680 + 7104
    tv = at("tv", [P, 16, TOPK], F32, s6)
    ti = at("ti", [P, 16, TOPK], U32, s6 + 1024)
    tif = at("tif", [P, 16, TOPK], F32, s6 + 2048)
    cv = at("cv", [P, PH, TOPK], F32, s6 + 3072)
    ci = at("ci", [P, PH, TOPK], U32, s6 + 3584)
    ca = at("ca", [P, 2, PH, TOPK], U32, s6 + 4096)
    caf = at("caf", [P, 2, PH, TOPK], F32, s6 + 5120)
    sm = at("sm", [P, CT, PH], F32, s6 + 6144)
    assert base + s6 + 6304 < 229368
    c_act = [at(f"c_act{i}", [P, E1G, T], F32, o_h + i * TB) for i in range(2)]
    c_gate = [at(f"c_gate{i}", [P, NGB, E1G, GB], F32, o_h + (2 + i) * TB) for i in range(2)]
    c_hi = [at(f"c_hi{i}", [P, E1G, T], F32R, o_h + (4 + i) * TB) for i in range(2)]
    c_lo = [at(f"c_lo{i}", [P, E1G, T], F32R, o_h + (6 + i) * TB) for i in range(2)]
    assert base + o_h + 8 * TB < 229368
    yraw = at("yraw", [P, KT, T], F32, o_h)

    ps = nc.alloc_psum_tensor("ps", [P, 8, 512], F32)

    def pair(p):
        return ps[:, 2 * p:2 * p + 2, 0:H2]

    def halves(ap):
        return ap.rearrange("p (a b) -> p a b", a=2)

    def block(buf, m):
        return buf[:, ds(m, 1), :].rearrange("p o (a b) -> p (o a) b", a=2)

    def f(ap):
        return ap.bitcast(F32)

    def c_(name, k=0):
        j = COLS[name] + k
        return col[:, j:j + 1]

    x_in = sem("x_in")
    const_in = sem("const_in")
    rgw_in = sem("rgw_in")
    keys_in = sem("keys_in")
    raw_in = [sem(f"raw_in{i}") for i in range(4)]
    w_hi_done = sem("w_hi_done")
    w_split = sem("w_split")
    tile_done = sem("tile_done")
    pair_free = [sem(f"pair_free{i}") for i in range(2)]
    ones_set = sem("ones_set")
    masks_in = sem("masks_in")
    passed = sem("passed")
    sq_done, sq_used, rms_done, nrm_done, hi_done, lo_done = (
        sem(n) for n in ("sq_done", "sq_used", "rms_done", "nrm_done", "hi_done", "lo_done"))
    dve_step, act_step = sem("dve_step"), sem("act_step")
    gl_done, gl_copied, z_done, z_read, lsig, cum_done = (
        sem(n) for n in ("gl_done", "gl_copied", "z_done", "z_read", "lsig", "cum_done"))
    vt_done, vt_copied = sem("vt_done"), sem("vt_copied")
    diff_done, exp_done, zed_done, zed_used, a_done, a_copied = (
        sem(n) for n in ("diff_done", "exp_done", "zed_done", "zed_used", "a_done", "a_copied"))
    end_done, qe_exp, qe_done, kT_done, k_nat_done, o_done, o_copied, u_done, s_done, kseg_done, si_done = (
        sem(n) for n in ("end_done", "qe_exp", "qe_done", "kT_done", "k_nat_done", "o_done", "o_copied", "u_done",
                         "s_done", "kseg_done", "si_done"))
    gla_in = [sem(f"gla_in{i}") for i in range(2)]
    gla_out = [sem(f"gla_out{i}") for i in range(2)]
    glap_out = sem("glap_out")
    osq_done, osq_used, orms_done, o_norm = (sem(n) for n in ("osq_done", "osq_used", "orms_done", "o_norm"))
    tap0, conv_done, gates_done, ri_done, ae_done, w2_done, sq2_done, ya_done, yhi_done, ylo_done = (
        sem(n) for n in ("tap0", "conv_done", "gates_done", "ri_done", "ae_done", "w2_done", "sq2_done", "ya_done",
                         "yhi_done", "ylo_done"))
    states_done, mix_done, small_out = sem("states_done"), sem("mix_done"), sem("small_out")
    lam_abs, lam_exp = sem("lam_abs"), sem("lam_exp")
    sc_done, sc_copied = sem("sc_done"), sem("sc_copied")
    top_step, picked, gate_exp, chosen_done, ct_done, bank_read = (
        sem(n) for n in ("top_step", "picked", "gate_exp", "chosen_done", "ct_done", "bank_read"))
    a_stored = [sem(f"a_stored{i}") for i in range(4)]
    oh_done, ohg_done, g_mm = sem("oh_done"), sem("ohg_done"), sem("g_mm")
    g_stored = [sem(f"g_stored{i}") for i in range(2)]
    c_in = [sem(f"c_in{i}") for i in range(2)]
    c_raw, c_hi_done, c_lo_done = sem("c_raw"), sem("c_hi_done"), sem("c_lo_done")
    d_free = [sem(f"d_free{i}") for i in range(4)]
    y_done, y_out = sem("y_done"), sem("y_out")
    SQ = [sq, sq_o, sq]

    blk = nc.Block()
    with blk as b:

        @b.sync
        def _(sp):
            for i in range(2):
                sp.dma_start(x[:, 4 * i:4 * i + 4, :], xT[:, 4 * i:4 * i + 4, :]).then_inc(x_in, 16)

            def load(src, i, first, j):
                n = first + j if i is None else i * 4 + (first + j)
                if i is not None:
                    sp.wait_ge(w_split, n - 3)
                k = j if i is None else i * 4 + j
                sp.dma_start(w_raw[j][:, :, :], src[ds(k, 1), :, :].rearrange("o p (k m) -> p (o k) m", m=P)
                             ).then_inc(raw_in[j], 16)

            for j in range(4):
                load(trunk, None, 0, j)
            with sp.Fori(1, N_U // 4) as i:
                for j in range(4):
                    load(trunk, i, 0, j)
            with sp.Fori(0, (N_D - N_U) // 4) as i:
                for j in range(4):
                    load(up, i, N_U, j)
            with sp.Fori(0, (N_END - N_D) // 4) as i:
                for j in range(4):
                    load(down, i, N_D, j)
            for k in range(KT):
                sp.wait_ge(y_done, k + 1)
                sp.dma_start(yT[:, k, :], yraw[:, k, :]).then_inc(y_out, 16)
            sp.wait_ge(y_out, 16 * KT)

        @b.gpsimd
        def _(pool):
            def split(j, n, free=True):
                pool.wait_ge(raw_in[j], (n - j) * 4 + 16)
                if free:
                    pool.wait_ge(tile_done, n - 1)
                pool.sem_inc(passed, 1)
                nc.gpsimd.tensor_scalar(w_hi[j % 2][:, :, :], w_raw[j][:, :, :], 1.0, 1.0, ALU.mult, ALU.mult
                                        ).then_inc(w_hi_done, 1)
                pool.wait_ge(w_hi_done, n + 1)
                nc.gpsimd.tensor_tensor(w_lo[j % 2][:, :, :], w_raw[j][:, :, :], f(w_hi[j % 2][:, :, :]),
                                        ALU.subtract).then_inc(w_split, 1)

            for j in range(4):
                split(j, j, free=j >= 2)
            with pool.Fori(1, (N_U + LOOP1) // 4) as i:
                for j in range(4):
                    split(j, i * 4 + j)

            def gated(bb, blkno):
                pool.wait_ge(oh_done, blkno + 1)
                tok = blkno * GB
                nc.gpsimd.tensor_tensor(
                    oh1[bb][:, :, :], oh1[bb][:, :, :],
                    chT[:, 2, ds(tok, GB)].unsqueeze(2).to_broadcast([P, GB, NK]), ALU.mult).then_inc(ohg_done, 1)

            with pool.Fori(0, LOOP2) as i:
                for j in range(4):
                    split(j, i * 4 + (N_U + LOOP1 + j))
                    if j % 2:
                        gated(j // 2, i * 2 + j // 2)
            for j in range(4):
                split(j, N_D - 4 + j)
            gated(0, NGB - 1)
            with pool.Fori(N_D // 4, N_END // 4) as i:
                for j in range(4):
                    split(j, i * 4 + j)

        @b.tensor
        def _(pe):
            def product(j, n, hi, lo, p):
                pe.wait_ge(w_split, n + 1)
                s = j % 2
                for k in range(KT):
                    for part, (wt, act) in enumerate(((w_hi[s], hi), (w_hi[s], lo), (w_lo[s], hi))):
                        for a in range(2):
                            last = nc.tensor.matmul(
                                ps[:, 2 * p + a, 0:H2], wt[:, k, :], act[:, k, a * H2:(a + 1) * H2],
                                start=k == 0 and part == 0, stop=k == KT - 1 and part == 2)
                last.then_inc(tile_done, 1)

            def stage(first, count, operand):
                with pe.Fori(0, count // 4) as i:
                    for j in range(4):
                        pe.wait_ge(pair_free[j % 2], i * 2 + (first // 2 + j // 2 + 1))
                        product(j, i * 4 + (first + j), *operand(j), j % 2)

            def norm(r):
                for k in range(KT):
                    pe.wait_ge(sq_done, 8 * r + k + 1)
                    for a in range(2):
                        last = nc.tensor.matmul(ps[:, 4 + a, 0:H2], ones[:, :], SQ[r][:, k % 2, a * H2:(a + 1) * H2],
                                                start=k == 0, stop=k == KT - 1)
                    last.then_inc(sq_used, 1)

            hn = lambda j: (h_hi, h_lo)
            pe.wait_ge(ones_set, 1)
            norm(0)
            pe.wait_ge(nrm_done, KT)
            pe.wait_ge(const_in, CONSTS)
            pe.wait_ge(rms_done, 1)
            for a in range(2):
                for k in range(KT):
                    last = nc.tensor.matmul(ps[0:RANK, 4 + a, 0:H2], wgl_sb[:, k, :],
                                            hn_raw[:, k, a * H2:(a + 1) * H2], start=k == 0, stop=k == KT - 1)
            last.then_inc(gl_done, 1)
            pe.wait_ge(gl_copied, 1)
            for h in range(HEADS):
                if h >= 2:
                    pe.wait_ge(z_read, 2 * (h - 1))
                for a in range(2):
                    last = nc.tensor.matmul(ps[:, 4 + 2 * (h % 2) + a, 0:H2], wg_sb[:, h * DK:(h + 1) * DK],
                                            glT[:, a * H2:(a + 1) * H2], start=True, stop=True)
                last.then_inc(z_done, 1)
            pe.wait_ge(lo_done, KT)
            stage(N_Q, 16, hn)
            for p in range(2):
                pe.wait_ge(pair_free[p], N_XA // 2 + 1)
            pe.wait_ge(z_read, 2 * HEADS)
            for c in range(CT):
                w = P if c < CT - 1 else LAST
                if c >= 2:
                    pe.wait_ge(vt_copied, c - 1)
                for m in range(KT):
                    last = nc.tensor.transpose(ps[0:w, 4 + 2 * (c % 2) + m // 4, (m % 4) * P:(m % 4 + 1) * P],
                                               vT[:, m, c * P:c * P + w], idt[:, :])
                last.then_inc(vt_done, 1)
            stage(N_XA, 8, hn)
            pe.wait_ge(vt_copied, CT)
            turn = 0
            for lv in range(8):
                if lv:
                    pe.wait_ge(zed_done, lv)
                for c, w in level_tiles(lv):
                    if turn >= 4:
                        pe.wait_ge(a_copied, turn - 3)
                    for h in range(HEADS):
                        z, zk = (qk, HEADS + h) if lv == 0 else (zed[lv % 2], h)
                        last = nc.tensor.matmul(ps[0:w, 4 + turn % 4, h * P:h * P + w], z[:, zk, c * P:c * P + w],
                                                z[:, h, c * P:c * P + w], start=True, stop=True)
                    last.then_inc(a_done, 1)
                    turn += 1
            pe.wait_ge(a_copied, turn)
            pe.wait_ge(qe_done, 2)
            for c in range(CT):
                w, np_ = (P, P) if c < CT - 1 else (LAST, PREST)
                if c:
                    pe.wait_ge(s_done, 2 * c)
                for h in range(HEADS):
                    last = nc.tensor.transpose(ps[0:w, 6, h * P:(h + 1) * P], qk[:, HEADS + h, c * P:c * P + w],
                                               idt[:, :])
                last.then_inc(kT_done, 1)
                if c:
                    pe.wait_ge(o_copied, c)
                for g in range(2 * HEADS):
                    h, d = g // 2, g % 2
                    b0 = 4 + g // 4
                    c0 = (g % 4) * P
                    last = nc.tensor.matmul(ps[:, b0, c0:c0 + w], v_nat[0:w, c, g * P:(g + 1) * P],
                                            attn[0:w, c, h, 0:w], start=True, stop=c == 0)
                    if c:
                        last = nc.tensor.matmul(ps[:, b0, c0:c0 + np_], st_p[:, h, d * P:(d + 1) * P],
                                                qk[:, h, c * P:c * P + np_], start=False, stop=True)
                last.then_inc(o_done, 1)
                pe.wait_ge(k_nat_done, c + 1)
                for hp in range(2):
                    for h in (2 * hp, 2 * hp + 1):
                        last = nc.tensor.matmul(ps[:, 7 - hp, (h % 2) * DV:(h % 2 + 1) * DV],
                                                k_nat[0:np_, h * DK:(h + 1) * DK],
                                                v_nat[0:np_, c, h * DV:(h + 1) * DV], start=True, stop=True)
                    last.then_inc(u_done, 1)
            for p in range(2):
                pe.wait_ge(pair_free[p], N_GA // 2 + 1)
            for s in range(NSEQ):
                pe.wait_ge(gla_in[s % 2], 16 * (s // 2 + 1))
                for g in range(2 * HEADS):
                    h, d = g // 2, g % 2
                    t0 = TP + s * DEC
                    last = nc.tensor.matmul(ps[:, 3, g * 64 + s * DEC:g * 64 + (s + 1) * DEC],
                                            st_s[s % 2][:, h, d * P:(d + 1) * P], qk[:, h, t0:t0 + DEC],
                                            start=True, stop=True)
                last.then_inc(si_done, 1)
                pe.wait_ge(kseg_done, s + 1)
                pe.wait_ge(s_done, 2 * (CT + s))
                for hp in range(2):
                    for h in (2 * hp, 2 * hp + 1):
                        last = nc.tensor.matmul(ps[:, 7 - hp, (h % 2) * DV:(h % 2 + 1) * DV],
                                                k_seg[0:LAST, h * DK:(h + 1) * DK],
                                                v_nat[0:LAST, CT - 1, h * DV:(h + 1) * DV], start=True, stop=True)
                    last.then_inc(u_done, 1)
            pe.wait_ge(s_done, 2 * (CT + NSEQ))
            pe.wait_ge(o_copied, CT)
            for h in range(HEADS):
                if h >= 2:
                    pe.wait_ge(orms_done, h - 1)
                for d in range(2):
                    pe.wait_ge(osq_done, 2 * h + d + 1)
                    for a in range(2):
                        last = nc.tensor.matmul(ps[:, 4 + 2 * (h % 2) + a, 0:H2], ones[:, :],
                                                sq_o[:, d, a * H2:(a + 1) * H2], start=d == 0, stop=d == 1)
                    last.then_inc(osq_used, 1)
            pe.wait_ge(orms_done, HEADS)
            pe.wait_ge(rgw_in, 16 * 3)
            for k in range(KT):
                pe.wait_ge(conv_done, 2 * (k + 1))
                if k:
                    pe.wait_ge(ri_done, 2 * k)
                for g in range(2):
                    for a in range(2):
                        last = nc.tensor.matmul(ps[:, 4 + 2 * g + a, 0:H2], gate_w[:, g, k, :],
                                                xc[:, a * H2:(a + 1) * H2], start=True, stop=True)
                last.then_inc(gates_done, 1)
                n = N_GA + k
                pe.wait_ge(pair_free[n % 2], n // 2 + 1)
                product(n, n, h_hi, h_lo, n % 2)
            pe.wait_ge(ylo_done, KT)
            stage(N_ZA, 16, lambda j: (h_hi, h_lo) if j % 2 == 0 else (y_hi, y_lo))
            stage(N_R, 8, hn)
            pe.wait_ge(ylo_done, 2 * KT)
            stage(N_ZB, 16, lambda j: (h_hi, h_lo) if j % 2 == 0 else (y_hi, y_lo))
            pe.wait_ge(ylo_done, 3 * KT)
            stage(N_OUT, 8, lambda j: (y_hi, y_lo))
            norm(1)
            pe.wait_ge(lo_done, 2 * KT)
            pe.wait_ge(keys_in, 16)
            pe.wait_ge(rms_done, 2)
            with pe.Fori(0, PH // 2) as i:
                for j in range(4):
                    pe.wait_ge(pair_free[j % 2], i * 2 + (N_WQ // 2 + j // 2 + 1))
                    product(j, i * 4 + (N_WQ + j), h_hi, h_lo, j % 2)
                    if j % 2 == 0:
                        continue
                    hb = j // 2
                    for p in range(2):
                        pe.wait_ge(pair_free[p], i * 2 + (N_WQ // 2 + hb + 2))
                    pe.wait_ge(sc_copied, i * 6 + (3 * hb + 1))
                    for c in range(CT):
                        w = P if c < CT - 1 else LAST
                        for side in range(2):
                            last = nc.tensor.matmul(
                                ps[0:w, 4 + c // 2, ((c % 2) * 2 + side) * P:((c % 2) * 2 + side + 1) * P],
                                qh[hb][:, side, c * P:c * P + w],
                                keys_sb[:, ds(i * 2 + hb, 1), side, :].rearrange("p o k -> p (o k)"),
                                start=True, stop=True)
                    last.then_inc(sc_done, 1)
            stage(N_U, LOOP1, hn)
            pe.wait_ge(sc_copied, 3 * PH + 1)
            pe.wait_ge(chosen_done, 1)
            for c in range(CT):
                w = P if c < CT - 1 else LAST
                if c == 4:
                    pe.wait_ge(bank_read, 1)
                for q in range(3):
                    last = nc.tensor.transpose(ps[:, 4 + c % 4, q * P:q * P + w], chosen[0:w, c, q, :],
                                               idt[0:w, 0:w])
                last.then_inc(ct_done, 1)

            def gate_block(bb, blkno):
                pe.wait_ge(ohg_done, blkno + 1)
                for q in range(4):
                    pe.wait_ge(bank_read, blkno * 4 + (CT + q - 3))
                    for t in range(4):
                        last = nc.tensor.matmul(ps[:, 4 + q, t * P:(t + 1) * P], oh2[bb][:, 4 * q + t, :],
                                                oh1[bb][:, 4 * q + t, :], start=True, stop=True)
                    last.then_inc(g_mm, 1)

            pe.wait_ge(bank_read, CT)
            first = N_U + LOOP1
            with pe.Fori(0, LOOP2) as i:
                for j in range(4):
                    pe.wait_ge(pair_free[j % 2], i * 2 + (first // 2 + j // 2 + 1))
                    product(j, i * 4 + (first + j), h_hi, h_lo, j % 2)
                    if j % 2:
                        gate_block(j // 2, i * 2 + j // 2)
            for j in range(4):
                n = N_D - 4 + j
                pe.wait_ge(pair_free[j % 2], n // 2 + 1)
                product(j, n, h_hi, h_lo, j % 2)
            gate_block(0, NGB - 1)
            with pe.Fori(0, NGRP // 2) as i:
                for gg in range(2):
                    pe.wait_ge(c_lo_done, i * 2 + (gg + 1))
                    for d in range(KT):
                        pe.wait_ge(d_free[d % 4], i * 4 + (2 * gg + d // 4 + 1))
                        product(d, i * 16 + (N_D + 8 * gg + d), c_hi[gg], c_lo[gg], d % 4)
            norm(2)

        @b.scalar
        def _(act):
            A = nc.scalar.activation

            def step(ins, n):
                ins.then_inc(act_step, 1)
                act.wait_ge(act_step, n)

            loads = ((col[:, :], cols), (idt[:, :], ident), (iot[:, :], iota), (lmask_in[:, :, :], masks),
                     (rst[:, :], reset), (segm[:, :], segmask), (wgl_sb[:, :, :], wgl), (wg_sb[:, :], wg))
            assert CONSTS == 16 * len(loads)
            for dst, src in loads:
                act.dma_start(dst, src).then_inc(const_in, 16)
            for p in range(2):
                act.sem_inc(pair_free[p], 1)
            for j in range(4):
                act.sem_inc(a_stored[j], 16)
            for j in range(2):
                act.sem_inc(g_stored[j], 16)

            epsc = small[:, 40:41]

            def norm(r, raw, split=True):
                for k in range(KT):
                    if r == 1:
                        act.wait_ge(pair_free[k % 2], (N_OUT + k) // 2 + 2)
                    if k >= 2:
                        act.wait_ge(sq_used, 8 * r + k - 1)
                    A(SQ[r][:, k % 2, :], x[:, k, :], ACT.Square).then_inc(sq_done, 1)
                act.wait_ge(sq_used, 8 * (r + 1))
                A(halves(rstd[:, :]), pair(2), ACT.Sqrt, bias=epsc, scale=1.0 / D).then_inc(rms_done, 1)
                if split:
                    for k in range(KT):
                        act.wait_ge(nrm_done, 8 * r + k + 1)
                        A(h_hi[:, k, :], raw[:, k, :], ACT.Copy).then_inc(hi_done, 1)

            act.wait_ge(ones_set, 1)
            act.wait_ge(x_in, 32)
            norm(0, hn_raw)
            act.wait_ge(lam_abs, 1)
            A(small[:, 16:24], small[:, 16:24], ACT.Exp, scale=-1.0).then_inc(lam_exp, 1)
            act.wait_ge(const_in, CONSTS)
            for h in range(HEADS):
                act.wait_ge(z_done, h + 1)
                A(halves(cum[:, h, :]), pair(2 + h % 2), ACT.Identity, bias=c_("bg", h)).then_inc(z_read, 1)
                A(halves(gtmp[:, h, :]), pair(2 + h % 2), ACT.Abs, bias=c_("bg", h)).then_inc(z_read, 1)
            act.wait_ge(z_read, 2 * HEADS)
            step(A(gtmp[:, :, :], gtmp[:, :, :], ACT.Exp, scale=-1.0), 1)
            A(gtmp[:, :, :], gtmp[:, :, :], ACT.Ln, bias=1.0).then_inc(lsig, 1)
            for n in range(8):
                act.wait_ge(tile_done, n + 1)
                if n == 0:
                    act.wait_ge(lo_done, KT)
                A(halves(qk[:, n, :]), pair(n % 2), ACT.Copy, scale=DK ** -0.5 if n < 4 else 1.0
                  ).then_inc(pair_free[n % 2], 1)
            act.wait_ge(masks_in, 1)
            with act.Fori(0, 4) as i:
                for j in range(2):
                    act.wait_ge(tile_done, i * 2 + (N_V + j + 1))
                    A(block(vT, i * 2 + j), pair(j), ACT.Copy).then_inc(pair_free[j], 1)
            def xa_tile(m):
                p = m % 2
                act.wait_ge(tile_done, N_XA + m + 1)
                A(xpad[:, m, 3:3 + H2], ps[:, 2 * p, 0:H2], ACT.Copy)
                A(xpad[:, m, 3 + H2:3 + TP], ps[:, 2 * p + 1, 0:TP - H2], ACT.Copy)
                A(xpad[:, m, 3 + TP:].rearrange("p (s c) -> p s c", s=NSEQ)[:, :, 3:],
                  ps[:, 2 * p + 1, TP - H2:H2].rearrange("p (s c) -> p s c", s=NSEQ), ACT.Copy
                  ).then_inc(pair_free[p], 1)

            def level_exp(lv):
                act.wait_ge(diff_done, lv)
                z = zed[lv % 2]
                span = level_span(lv)
                A(z[:, :, 0:span], z[:, :, 0:span], ACT.Exp).then_inc(exp_done, 1)

            for m in range(2):
                xa_tile(m)
                level_exp(m + 1)
            for m in range(2, KT):
                xa_tile(m)
            for lv in range(3, 8):
                level_exp(lv)
            act.wait_ge(a_done, TURNS)
            act.wait_ge(zed_done, 8)
            A(zed[0][:, :, :], cum[:, :, :], ACT.Exp).then_inc(qe_exp, 1)
            A(zed[1][:, :, :], zed[1][:, :, :], ACT.Exp).then_inc(qe_exp, 1)
            A(end_cum[:, :, 0:CT + NSEQ], end_cum[:, :, 0:CT + NSEQ], ACT.Exp).then_inc(end_done, 1)
            for s in range(2):
                act.dma_start(st_s[s][:, :, :], gla0[s].rearrange("h k v -> k h v")).then_inc(gla_in[s], 16)
            for c in range(CT):
                w = P if c < CT - 1 else LAST
                act.wait_ge(kT_done, c + 1)
                if c:
                    act.wait_ge(u_done, 2 * c)
                A(k_nat[0:w, :], ps[0:w, 6, :], ACT.Copy).then_inc(k_nat_done, 1)
                act.wait_ge(o_done, c + 1)
                if c == 0:
                    act.wait_ge(qe_done, 2)
                A(o[:, :, c * P:c * P + w],
                  ps[:, 4:6, :].rearrange("p a (g t) -> p (a g) t", g=4)[:, :, 0:w], ACT.Copy).then_inc(o_copied, 1)
            for s in range(NSEQ):
                act.wait_ge(s_done, 2 * (CT + s + 1))
                act.dma_start(gla_s[s].rearrange("h k v -> k h v"), st_s[s % 2][:, :, :]
                              ).then_inc(gla_out[s % 2], 16)
                if s + 2 < NSEQ:
                    act.wait_ge(gla_out[s % 2], 16 * (s // 2 + 1))
                    act.dma_start(st_s[s % 2][:, :, :], gla0[s + 2].rearrange("h k v -> k h v")
                                  ).then_inc(gla_in[s % 2], 16)
            act.dma_start(gla_p.rearrange("h k v -> k h v"), st_p[:, :, :]).then_inc(glap_out, 16)
            act.wait_ge(glap_out, 16)
            for i in range(2):
                act.wait_ge(gla_out[i], 16 * (NSEQ // 2))
            act.dma_start(gate_w[:, :, :, :], gates).then_inc(rgw_in, 16)
            act.dma_start(c0sb[:, :, :, :], conv0).then_inc(rgw_in, 16)
            act.dma_start(h0sb[:, :, :], h0).then_inc(rgw_in, 16)
            act.wait_ge(o_norm, 1)
            for h in range(HEADS):
                for d in range(2):
                    if h:
                        act.wait_ge(osq_used, 2 * (h - 1) + d + 1)
                    A(sq_o[:, d, :], o[:, 2 * h + d, :], ACT.Square).then_inc(osq_done, 1)
                act.wait_ge(osq_used, 2 * h + 2)
                if h:
                    act.wait_ge(o_norm, 1 + 2 * h)
                A(halves(rstd[:, :]), pair(2 + h % 2), ACT.Sqrt, bias=epsc, scale=1.0 / DV).then_inc(orms_done, 1)
            act.wait_ge(rgw_in, 16 * 3)
            act.wait_ge(osq_used, 2 * HEADS)
            act.wait_ge(w2_done, 1)
            for k in range(KT):
                if k:
                    act.wait_ge(gates_done, k)
                    act.wait_ge(w2_done, 1 + 3 * k)
                A(xc[:, 0:TP], xpad[:, k, 3:3 + TP], ACT.Identity, bias=c_("cb", k), scale=c_("cw3", k)
                  ).then_inc(tap0, 1)
                A(xc[:, TP:].rearrange("p (s c) -> p s c", s=NSEQ),
                  xpad[:, k, 3 + TP:].rearrange("p (s c) -> p s c", s=NSEQ)[:, :, 3:],
                  ACT.Identity, bias=c_("cb", k), scale=c_("cw3", k)).then_inc(tap0, 1)
                act.wait_ge(gates_done, k + 1)
                A(halves(rr[:, :]), pair(2), ACT.Sigmoid, bias=c_("ba", k)).then_inc(ri_done, 1)
                A(halves(ii[:, :]), pair(3), ACT.Sigmoid, bias=c_("bx", k)).then_inc(ri_done, 1)
                act.wait_ge(ri_done, 2 * k + 2)
                if k:
                    act.wait_ge(w2_done, 1 + 3 * k)
                A(aa[:, :], rr[:, :], ACT.Exp, scale=small[:, k:k + 1]).then_inc(ae_done, 1)
                A(rr[:, :], rr[:, :], ACT.Tanh, scale=small[:, 8 + k:9 + k]).then_inc(ae_done, 1)
                act.wait_ge(w2_done, 1 + 3 * k + 1)
                A(rr[:, :], rr[:, :], ACT.Sqrt).then_inc(sq2_done, 1)
                n = N_GA + k
                act.wait_ge(tile_done, n + 1)
                A(halves(ga[:, k, :]), pair(n % 2), ACT.Gelu).then_inc(pair_free[n % 2], 1)
                act.wait_ge(ya_done, k + 1)
                A(y_hi[:, k, :], ga[:, k, :], ACT.Copy).then_inc(yhi_done, 1)
            act.wait_ge(states_done, 1)
            act.dma_start(conv_out, cfin[:, :, :, :]).then_inc(small_out, 16)
            act.dma_start(h_out, hfin[:, :, :]).then_inc(small_out, 16)
            act.wait_ge(small_out, 32)

            def sigmoid_tiles(first):
                with act.Fori(0, 4) as i:
                    for j in range(2):
                        act.wait_ge(tile_done, i * 4 + (first + 2 * j + 1))
                        act.wait_ge(pair_free[1], i * 2 + (first // 2 + j))
                        A(halves(sgate[j][:, :]), pair(0), ACT.Sigmoid).then_inc(pair_free[0], 1)

            sigmoid_tiles(N_ZA)
            act.wait_ge(pair_free[1], N_R // 2 + 1)
            act.wait_ge(tile_done, N_R)
            for m in range(KT):
                n = N_R + m
                act.wait_ge(tile_done, n + 1)
                if m >= 2:
                    act.wait_ge(ya_done, KT + m - 1)
                A(halves(sgate[m % 2][:, :]), pair(m % 2), ACT.Silu).then_inc(pair_free[m % 2], 1)
                act.wait_ge(ya_done, KT + m + 1)
                A(y_hi[:, m, :], o[:, m, :], ACT.Copy).then_inc(yhi_done, 1)
            sigmoid_tiles(N_ZB)
            act.wait_ge(tile_done, N_OUT)
            for m in range(KT):
                act.wait_ge(mix_done, m + 1)
                A(y_hi[:, m, :], mix[:, m, :], ACT.Copy).then_inc(yhi_done, 1)
            norm(1, hn2_raw)
            act.wait_ge(lo_done, 2 * KT)
            act.dma_start(keys_sb[:, :, :, :], keys).then_inc(keys_in, 16)
            with act.Fori(0, PH // 2) as i:
                for j in range(4):
                    act.wait_ge(tile_done, i * 4 + (N_WQ + j + 1))
                    act.wait_ge(sc_copied, i * 6 + 1)
                    A(halves(qh[j // 2][:, j % 2, :]), pair(j % 2), ACT.Copy).then_inc(pair_free[j % 2], 1)
            act.wait_ge(sc_copied, 3 * PH + 1)

            def up_tiles(i0, i1, extra=None):
                with act.Fori(i0, i1) as i:
                    for j in range(4):
                        act.wait_ge(tile_done, i * 4 + (N_U + j + 1))
                        act.wait_ge(a_stored[j], i * 16 + 16)
                        A(halves(ast[j][:, :]), pair(j % 2), ACT.Gelu).then_inc(pair_free[j % 2], 1)
                        act.wait_ge(pair_free[j % 2], i * 2 + (N_U // 2 + j // 2 + 2))
                        act.dma_start(a_dram[ds(i * 4 + j, 1), :, :].rearrange("o p t -> p (o t)"), ast[j][:, :]
                                      ).then_inc(a_stored[j], 16)
                        if extra and j % 2:
                            extra(j // 2, i * 2 + (j // 2 - 2 * i0))

            up_tiles(0, LOOP1 // 4)
            act.wait_ge(picked, 1)
            A(chosen[:, :, 2, :], chosen[:, :, 2, :], ACT.Exp).then_inc(gate_exp, 1)
            for c in range(CT):
                act.wait_ge(ct_done, c + 1)
                w = P if c < CT - 1 else LAST
                A(chT[:, :, c * P:c * P + w], ps[:, 4 + c % 4, 0:3 * P].rearrange("p (q t) -> p q t", q=3)[:, :, 0:w],
                  ACT.Copy).then_inc(bank_read, 1)

            def gate_copies(bb, blkno):
                act.wait_ge(g_stored[bb], (blkno - bb) * 8 + 16)
                for q in range(4):
                    act.wait_ge(g_mm, blkno * 4 + (q + 1))
                    A(gst[bb][:, :, 4 * q:4 * q + 4].rearrange("p e t -> p t e"),
                      ps[:, 4 + q, :].rearrange("p (t e) -> p t e", t=4), ACT.Copy).then_inc(bank_read, 1)
                act.wait_ge(bank_read, blkno * 4 + (CT + 4))
                act.dma_start(g_dram[ds(blkno, 1), :, :].rearrange("o p e -> p (o e)"),
                              gst[bb][:, :, :].rearrange("p e t -> p (e t)")).then_inc(g_stored[bb], 16)

            i0 = LOOP1 // 4
            up_tiles(i0, i0 + LOOP2, gate_copies)
            up_tiles(i0 + LOOP2, NK // 4)
            gate_copies(0, NGB - 1)
            for j in range(4):
                act.wait_ge(a_stored[j], 16 * (NK // 4 + 1))
            act.wait_ge(g_stored[0], 16 * (NGB // 2 + 2))
            act.wait_ge(g_stored[1], 16 * (NGB // 2 + 1))
            act.wait_ge(tile_done, N_D)

            def c_load(gg, g):
                act.dma_start(c_act[gg][:, :, :], a_dram[ds(g * E1G, E1G), :, :].rearrange("e p t -> p e t")
                              ).then_inc(c_in[gg], 16)
                act.dma_start(c_gate[gg][:, :, :, :].rearrange("p b e t -> p b (e t)"),
                              g_dram[:, :, ds(g * (E1G * GB), E1G * GB)].rearrange("b p e -> p b e")
                              ).then_inc(c_in[gg], 16)

            def c_split(gg, g):
                act.wait_ge(c_raw, g + 1)
                A(c_hi[gg][:, :, :], c_act[gg][:, :, :], ACT.Copy).then_inc(c_hi_done, 1)

            c_load(0, 0)
            c_load(1, 1)
            c_split(0, 0)
            with act.Fori(0, NGRP // 2 - 1) as i:
                for gg in range(2):
                    g = i * 2 + gg
                    act.wait_ge(c_lo_done, g + 1)
                    c_load(gg, g + 2)
                    c_split(1 - gg, g + 1)
            c_split(1, NGRP - 1)
            for p in range(4):
                act.wait_ge(d_free[p], 2 * NGRP + 1)
            norm(2, yraw, split=False)

        @b.vector
        def _(dve):
            V = nc.vector
            n_step = [0]

            def link(ins):
                n_step[0] += 1
                ins.then_inc(dve_step, 1)
                dve.wait_ge(dve_step, n_step[0])

            V.memset(small[:, 40:41], EPS)
            V.memset(ones[:, :], 1.0).then_inc(ones_set, 1)

            def norm(r, raw, g, split=True):
                dve.wait_ge(rms_done, r + 1)
                link(V.reciprocal(rstd[:, :], rstd[:, :]))
                for k in range(KT):
                    V.scalar_tensor_tensor(raw[:, k, :], x[:, k, :], c_(g, k), rstd[:, :], ALU.mult, ALU.mult
                                           ).then_inc(nrm_done if split else y_done, 1)
                    if split and k:
                        lo(r, raw, k - 1)
                if split:
                    lo(r, raw, KT - 1)

            def lo(r, raw, k):
                dve.wait_ge(hi_done, 8 * r + k + 1)
                V.tensor_tensor(h_lo[:, k, :], raw[:, k, :], f(h_hi[:, k, :]), ALU.subtract).then_inc(lo_done, 1)

            dve.wait_ge(x_in, 32)
            dve.wait_ge(const_in, CONSTS)
            V.tensor_copy(lmask[:, :, :], lmask_in[:, :, :]).then_inc(masks_in, 1)
            lam = col[:, COLS["lam"]:COLS["lam"] + KT]
            V.scalar_tensor_tensor(small[:, 16:24], lam, -1.0, lam, ALU.mult, ALU.max).then_inc(lam_abs, 1)
            norm(0, hn_raw, "norm1")
            dve.wait_ge(gl_done, 1)
            V.tensor_copy(halves(glT[:, :]), ps[0:RANK, 4:6, 0:H2]).then_inc(gl_copied, 1)
            dve.wait_ge(lsig, 1)
            link(V.scalar_tensor_tensor(gtmp[:, :, :].rearrange("p h t -> p (h t)"),
                                        cum[:, :, :].rearrange("p h t -> p (h t)"), 0.0,
                                        gtmp[:, :, :].rearrange("p h t -> p (h t)"), ALU.min, ALU.subtract))
            link(V.tensor_scalar(gtmp[:, :, :], gtmp[:, :, :], 1.0 / 16.0, None, ALU.mult))
            for h in range(HEADS):
                last = V.tensor_tensor_scan(cum[:, h, :], rst[:, :], gtmp[:, h, :], 0.0, ALU.mult, ALU.add)
            link(last)
            link(V.memset(attn[:, :, :, :], 0.0))
            V.memset(st_p[:, :, :], 0.0)
            for c in range(CT):
                w = P if c < CT - 1 else LAST
                dve.wait_ge(vt_done, c + 1)
                V.tensor_copy(v_nat[0:w, c, :].rearrange("p (a n) -> p a n", a=2),
                              ps[0:w, 4 + 2 * (c % 2):6 + 2 * (c % 2), :]).then_inc(vt_copied, 1)

            def level_views(buf, heads, lv):
                hs = HALF[lv - 1]
                span = level_span(lv)
                out = []
                if span == T:
                    v = buf[:, heads, :].rearrange("p h (n b) -> p (h n) b", b=2 * hs)
                    return [(v[:, :, 0:hs], v[:, :, hs:], v[:, :, hs - 1:hs])]
                for h in range(heads.start, heads.stop):
                    v = buf[:, h, 0:span].rearrange("p (n b) -> p n b", b=2 * hs)
                    out.append((v[:, :, 0:hs], v[:, :, hs:], v[:, :, hs - 1:hs]))
                return out

            all_h = slice(0, HEADS)

            def diffs(lv):
                hs = HALF[lv - 1]
                z = zed[lv % 2]
                for (z0, z1, _), (c0, c1, cm) in zip(level_views(z, all_h, lv), level_views(cum, all_h, lv)):
                    n = c0.shape[1]
                    V.tensor_tensor(z0, cm.to_broadcast([P, n, hs]), c0, ALU.subtract)
                    last = V.tensor_tensor(z1, c1, cm.to_broadcast([P, n, hs]), ALU.subtract)
                last.then_inc(diff_done, 1)

            def mults(lv):
                dve.wait_ge(exp_done, lv)
                z = zed[lv % 2]
                for (z0, z1, _), (_, q1, _), (k0, _, _) in zip(
                        level_views(z, all_h, lv), level_views(qk, all_h, lv),
                        level_views(qk, slice(HEADS, 2 * HEADS), lv)):
                    V.tensor_tensor(z0, z0, k0, ALU.mult)
                    last = V.tensor_tensor(z1, z1, q1, ALU.mult)
                last.then_inc(zed_done, 1)

            turn = [0]

            def keep(lv):
                for c, w in level_tiles(lv):
                    dve.wait_ge(a_done, turn[0] + 1)
                    bank = ps[0:w, 4 + turn[0] % 4, :].rearrange("p (h t) -> p h t", h=HEADS)[:, :, 0:w]
                    V.copy_predicated(attn[0:w, c, :, 0:w],
                                      lmask[0:w, lv, 0:w].unsqueeze(1).to_broadcast([w, HEADS, w]), bank
                                      ).then_inc(a_copied, 1)
                    turn[0] += 1

            for p in range(2):
                dve.wait_ge(pair_free[p], 5)
            dve.wait_ge(vt_done, CT)
            diffs(1)
            diffs(2)
            mults(1)
            mults(2)
            keep(0)
            for lv in range(3, 8):
                keep(lv - 2)
                dve.wait_ge(a_done, turns_to(lv - 2))
                diffs(lv)
                mults(lv)
            keep(6)
            for h in range(HEADS):
                V.tensor_copy(end_cum[:, h, 0:CT - 1], cum[:, h, 0:(CT - 1) * P].rearrange("p (c t) -> p c t", t=P)[:, :, P - 1])
                V.tensor_copy(end_cum[:, h, CT - 1:CT], cum[:, h, TP - 1:TP])
                last = V.tensor_copy(end_cum[:, h, CT:CT + NSEQ], cum[:, h, TP:].rearrange("p (s t) -> p s t", t=DEC)[:, :, DEC - 1])
            link(last)
            keep(7)
            for h in range(HEADS):
                for lo_, n, w, e in ((0, CT - 1, P, 0), ((CT - 1) * P, 1, PREST, CT - 1), (TP, NSEQ, DEC, CT)):
                    last = V.tensor_tensor(
                        zed[1][:, h, lo_:lo_ + n * w].rearrange("p (n t) -> p n t", t=w),
                        end_cum[:, h, e:e + n].unsqueeze(2).to_broadcast([P, n, w]),
                        cum[:, h, lo_:lo_ + n * w].rearrange("p (n t) -> p n t", t=w), ALU.subtract)
            last.then_inc(zed_done, 1)
            dve.wait_ge(qe_exp, 1)
            V.tensor_tensor(qk[:, 0:HEADS, :], qk[:, 0:HEADS, :], zed[0][:, :, :], ALU.mult).then_inc(qe_done, 1)
            dve.wait_ge(qe_exp, 2)
            V.tensor_tensor(qk[:, HEADS:, :], qk[:, HEADS:, :], zed[1][:, :, :], ALU.mult).then_inc(qe_done, 1)
            dve.wait_ge(end_done, 1)
            for c in range(CT):
                for hp in range(2):
                    dve.wait_ge(u_done, 2 * c + hp + 1)
                    if c:
                        dve.wait_ge(o_done, c + 1)
                        dve.wait_ge(s_done, 2 * c + hp)
                    for h in (2 * hp, 2 * hp + 1):
                        last = V.scalar_tensor_tensor(st_p[:, h, :], st_p[:, h, :], end_cum[:, h, c:c + 1],
                                                      ps[:, 7 - hp, (h % 2) * DV:(h % 2 + 1) * DV], ALU.mult, ALU.add)
                    last.then_inc(s_done, 1)
            for s in range(NSEQ):
                if s:
                    dve.wait_ge(u_done, 2 * (CT + s))
                else:
                    dve.wait_ge(k_nat_done, CT)
                V.tensor_scalar(k_seg[0:LAST, :], k_nat[0:LAST, :], segm[0:LAST, s:s + 1], None, ALU.mult
                                ).then_inc(kseg_done, 1)
                dve.wait_ge(si_done, s + 1)
                for hp in range(2):
                    dve.wait_ge(u_done, 2 * (CT + s) + hp + 1)
                    for h in (2 * hp, 2 * hp + 1):
                        last = V.scalar_tensor_tensor(st_s[s % 2][:, h, :], st_s[s % 2][:, h, :],
                                                      end_cum[:, h, CT + s:CT + s + 1],
                                                      ps[:, 7 - hp, (h % 2) * DV:(h % 2 + 1) * DV], ALU.mult, ALU.add)
                    last.then_inc(s_done, 1)
            dve.wait_ge(o_copied, CT)
            V.tensor_tensor(o[:, :, TP:], o[:, :, TP:], ps[:, 3, :].rearrange("p (g t) -> p g t", t=NSEQ * DEC),
                            ALU.add).then_inc(o_norm, 1)
            for h in range(HEADS):
                dve.wait_ge(orms_done, h + 1)
                link(V.reciprocal(rstd[:, :], rstd[:, :]))
                dve.wait_ge(osq_done, 2 * h + 2)
                for d in range(2):
                    V.scalar_tensor_tensor(o[:, 2 * h + d, :], o[:, 2 * h + d, :], c_("gng", d), rstd[:, :],
                                           ALU.mult, ALU.mult).then_inc(o_norm, 1)
            dve.wait_ge(o_norm, 1 + 2 * HEADS)
            dve.wait_ge(rgw_in, 16 * 3)
            dve.wait_ge(lam_exp, 1)
            e_, zz, z2, acc, rate = (small[:, 8 * q:8 * q + 8] for q in (2, 3, 4, 6, 0))
            link(V.tensor_scalar(zz, e_, 2.0, None, ALU.add))
            link(V.reciprocal(zz, zz))
            link(V.tensor_tensor(zz, zz, e_, ALU.mult))
            link(V.tensor_tensor(z2, zz, zz, ALU.mult))
            link(V.memset(acc, 1.0 / 17))
            for q in (15, 13, 11, 9, 7, 5, 3, 1):
                link(V.tensor_tensor(acc, acc, z2, ALU.mult))
                link(V.tensor_scalar(acc, acc, 1.0 / q, None, ALU.add))
            link(V.tensor_tensor(acc, acc, zz, ALU.mult))
            link(V.tensor_scalar(zz, lam, -1.0, 0.0, ALU.mult, ALU.max))
            link(V.scalar_tensor_tensor(acc, acc, 2.0, zz, ALU.mult, ALU.add))
            link(V.tensor_scalar(rate, acc, -8.0, None, ALU.mult))
            V.tensor_scalar(small[:, 8:16], acc, 8.0, None, ALU.mult).then_inc(w2_done, 1)
            V.memset(xpad[:, :, 0:3], 0.0)
            link(V.tensor_copy(xpad[:, :, 3 + TP:].rearrange("p k (s c) -> p k s c", s=NSEQ)[:, :, :, 0:3],
                               c0sb[:, :, :, :]))
            V.tensor_copy(cfin[:, :, 0, :], xpad[:, :, TP:TP + 3])
            link(V.tensor_copy(cfin[:, :, 1:, :],
                               xpad[:, :, 3 + TP:].rearrange("p k (s c) -> p k s c", s=NSEQ)[:, :, :, DEC:]))
            for k in range(KT):
                xs = xpad[:, k, 3 + TP:].rearrange("p (s c) -> p s c", s=NSEQ)
                cs = xc[:, TP:].rearrange("p (s c) -> p s c", s=NSEQ)
                dve.wait_ge(tap0, 2 * k + 2)
                for tap in (2, 1, 0):
                    w = c_(f"cw{tap}", k)
                    a_ = V.scalar_tensor_tensor(xc[:, 0:TP], xpad[:, k, tap:tap + TP], w, xc[:, 0:TP],
                                                ALU.mult, ALU.add)
                    if tap == 0:
                        a_.then_inc(conv_done, 1)
                    b_ = V.scalar_tensor_tensor(cs, xs[:, :, tap:tap + DEC], w, cs, ALU.mult, ALU.add)
                    if tap:
                        link(b_)
                b_.then_inc(conv_done, 1)
                dve.wait_ge(ri_done, 2 * k + 2)
                dve.wait_ge(conv_done, 2 * k + 2)
                link(V.tensor_tensor(ii[:, :], ii[:, :], xc[:, :], ALU.mult))
                dve.wait_ge(ae_done, 2 * k + 2)
                if k:
                    dve.wait_ge(ya_done, k)
                link(V.tensor_tensor(hh[:, :], aa[:, :], aa[:, :], ALU.mult))
                link(V.scalar_tensor_tensor(rr[:, :], hh[:, :], 1.0, rr[:, :], ALU.add, ALU.mult))
                V.tensor_scalar(rr[:, :], rr[:, :], 2.0 ** -100, None, ALU.max).then_inc(w2_done, 1)
                dve.wait_ge(sq2_done, k + 1)
                link(V.tensor_tensor(ii[:, :], ii[:, :], rr[:, :], ALU.mult))
                as_ = aa[:, TP:].rearrange("p (s c) -> p s c", s=NSEQ)[:, :, 0]
                us_ = ii[:, TP:].rearrange("p (s c) -> p s c", s=NSEQ)[:, :, 0]
                link(V.tensor_tensor(h0sb[:, k, :], h0sb[:, k, :], as_, ALU.mult))
                link(V.tensor_tensor(us_, us_, h0sb[:, k, :], ALU.add))
                link(V.memset(as_, 0.0))
                V.tensor_tensor_scan(hh[:, :], aa[:, :], ii[:, :], 0.0, ALU.mult, ALU.add).then_inc(w2_done, 1)
                dve.wait_ge(w2_done, 1 + 3 * k + 2)
                V.tensor_copy(hfin[:, k, 0:1], hh[:, TP - 1:TP])
                V.tensor_copy(hfin[:, k, 1:], hh[:, TP:].rearrange("p (s c) -> p s c", s=NSEQ)[:, :, DEC - 1]
                              ).then_inc(w2_done, 1)
                n = N_GA + k
                dve.wait_ge(pair_free[n % 2], n // 2 + 2)
                V.tensor_tensor(ga[:, k, :], ga[:, k, :], hh[:, :], ALU.mult).then_inc(ya_done, 1)
                dve.wait_ge(yhi_done, k + 1)
                V.tensor_tensor(y_lo[:, k, :], ga[:, k, :], f(y_hi[:, k, :]), ALU.subtract).then_inc(ylo_done, 1)
            dve.sem_inc(states_done, 1)
            dve.wait_ge(ylo_done, KT)
            with dve.Fori(0, 4) as i:
                for j in range(2):
                    dve.wait_ge(tile_done, i * 4 + (N_ZA + 2 * j + 2))
                    dve.wait_ge(pair_free[0], i * 2 + (N_ZA // 2 + j + 2))
                    V.tensor_tensor(block(mix, i * 2 + j), pair(1), halves(sgate[j][:, :]), ALU.mult
                                    ).then_inc(pair_free[1], 1)
            for m in range(KT):
                n = N_R + m
                dve.wait_ge(pair_free[n % 2], n // 2 + 2)
                V.tensor_tensor(o[:, m, :], o[:, m, :], sgate[m % 2][:, :], ALU.mult).then_inc(ya_done, 1)
                dve.wait_ge(yhi_done, KT + m + 1)
                V.tensor_tensor(y_lo[:, m, :], o[:, m, :], f(y_hi[:, m, :]), ALU.subtract).then_inc(ylo_done, 1)
            with dve.Fori(0, 4) as i:
                for j in range(2):
                    dve.wait_ge(tile_done, i * 4 + (N_ZB + 2 * j + 2))
                    dve.wait_ge(pair_free[0], i * 2 + (N_ZB // 2 + j + 2))
                    V.tensor_tensor(halves(prod[:, :]), pair(1), halves(sgate[j][:, :]), ALU.mult
                                    ).then_inc(pair_free[1], 1)
                    dve.wait_ge(pair_free[1], i * 2 + (N_ZB // 2 + j + 2))
                    V.tensor_tensor(block(mix, i * 2 + j), block(mix, i * 2 + j), halves(prod[:, :]), ALU.add
                                    ).then_inc(mix_done, 1)
                    dve.wait_ge(mix_done, i * 2 + (j + 1))
            for m in range(KT):
                dve.wait_ge(yhi_done, 2 * KT + m + 1)
                V.tensor_tensor(y_lo[:, m, :], mix[:, m, :], f(y_hi[:, m, :]), ALU.subtract).then_inc(ylo_done, 1)
            for m in range(KT):
                n = N_OUT + m
                dve.wait_ge(tile_done, n + 1)
                V.tensor_tensor(halves(x[:, m, :]), halves(x[:, m, :]), pair(m % 2), ALU.add
                                ).then_inc(pair_free[m % 2], 1)
            norm(1, hn2_raw, "norm2")
            dve.wait_ge(lo_done, 2 * KT)
            V.memset(scores[:, CT - 1, :, :], 0.0).then_inc(sc_copied, 1)
            dve.wait_ge(sc_copied, 1)
            with dve.Fori(0, PH) as i:
                dve.wait_ge(sc_done, i + 1)
                for part in range(3):
                    nt = 2 if part < 2 else 1
                    w = P if part < 2 else LAST
                    V.tensor_copy(
                        scores[0:w, 2 * part:2 * part + nt, ds(i * 2, 2), :],
                        ps[0:w, 4 + part, 0:nt * 2 * P].rearrange("p (c s k) -> p c s k", c=nt, s=2)
                    ).then_inc(sc_copied, 1)
            dve.wait_ge(sc_copied, 3 * PH + 1)
            LOWEST = -3.4028235e38
            STEPS = 21

            with dve.Fori(0, CT) as i:
                n_top = [0]

                def then(ins):
                    n_top[0] += 1
                    ins.then_inc(top_step, 1)
                    dve.wait_ge(top_step, i * STEPS + n_top[0])
                    dve.sem_inc(passed, 1)

                def best(n, vals, best_v, best_i):
                    for q in range(n):
                        last = V.max(best_v(q, 0), vals(q))
                    then(last)
                    for q in range(n):
                        last = V.max_index(best_i(q, 0), best_v(q, 0), vals(q))
                    then(last)
                    for q in range(n):
                        last = V.match_replace(vals(q), best_v(q, 0), vals(q), LOWEST)
                    then(last)
                    for q in range(n):
                        last = V.max(best_v(q, 8), vals(q))
                    then(last)
                    for q in range(n):
                        last = V.max_index(best_i(q, 8), best_v(q, 8), vals(q))
                    then(last)

                then(V.tensor_copy(work[:, :, :], scores[:, ds(i, 1), :, :].rearrange("p o q k -> p (o q) k")))
                best(2 * PH, lambda q: work[:, q, :], lambda q, s: tv[:, q, s:s + 8], lambda q, s: ti[:, q, s:s + 8])
                V.tensor_copy(tif[:, :, :], ti[:, :, :])
                tvs = tv[:, :, :].rearrange("p (h s) k -> p h s k", s=2)
                then(V.tensor_tensor(cand[:, :, :, :],
                                     tvs[:, :, 0, :].unsqueeze(3).to_broadcast([P, PH, TOPK, TOPK]),
                                     tvs[:, :, 1, :].unsqueeze(2).to_broadcast([P, PH, TOPK, TOPK]), ALU.add))
                best(PH, lambda q: cand[:, q, :, :].rearrange("p a b -> p (a b)"),
                     lambda q, s: cv[:, q, s:s + 8], lambda q, s: ci[:, q, s:s + 8])
                V.tensor_scalar(ca[:, 0, :, :], ci[:, :, :], 4, None, ALU.logical_shift_right)
                then(V.tensor_scalar(ca[:, 1, :, :], ci[:, :, :], 15, None, ALU.bitwise_and))
                then(V.tensor_copy(caf[:, :, :, :], ca[:, :, :, :]))
                tifs = tif[:, :, :].rearrange("p (h s) k -> p h s k", s=2)
                for side in range(2):
                    then(V.tensor_tensor(pick[:, :, :, :],
                                         iot[:, 0:TOPK].unsqueeze(1).unsqueeze(1).to_broadcast([P, PH, TOPK, TOPK]),
                                         caf[:, side, :, :].unsqueeze(3).to_broadcast([P, PH, TOPK, TOPK]),
                                         ALU.is_equal))
                    then(V.tensor_tensor(pick[:, :, :, :], pick[:, :, :, :],
                                         tifs[:, :, side, :].unsqueeze(2).to_broadcast([P, PH, TOPK, TOPK]),
                                         ALU.mult))
                    then(V.tensor_reduce(chosen[:, ds(i, 1), side, :].rearrange("p o j -> p (o j)"),
                                         pick[:, :, :, :].rearrange("p h k a -> p (h k) a"), AX, ALU.add))
                then(V.tensor_tensor(chosen[:, ds(i, 1), 2, :].rearrange("p o (h k) -> p (o h) k", h=PH),
                                     cv[:, :, :], cv[:, :, 0:1].to_broadcast([P, PH, TOPK]), ALU.subtract))
            assert n_top[0] == STEPS, n_top
            dve.sem_inc(picked, 1)
            dve.wait_ge(gate_exp, 1)
            for c in range(CT):
                last = V.tensor_reduce(sm[:, c, :], chosen[:, c, 2, :].rearrange("p (h k) -> p h k", h=PH), AX, ALU.add)
            link(last)
            link(V.reciprocal(sm[:, :, :], sm[:, :, :]))
            for c in range(CT):
                cg = chosen[:, c, 2, :].rearrange("p (h k) -> p h k", h=PH)
                last = V.tensor_tensor(cg, cg, sm[:, c, :].unsqueeze(2).to_broadcast([P, PH, TOPK]), ALU.mult)
            last.then_inc(chosen_done, 1)

            def one_hots(bb, blkno, wait=True):
                if wait:
                    dve.wait_ge(g_mm, blkno * 4 - 4)
                for buf, q in ((oh2[bb], 1), (oh1[bb], 0)):
                    last = V.tensor_tensor(buf[:, :, :], iot[:, :].unsqueeze(1).to_broadcast([P, GB, NK]),
                                           chT[:, q, ds(blkno * GB, GB)].unsqueeze(2).to_broadcast([P, GB, NK]),
                                           ALU.is_equal)
                last.then_inc(oh_done, 1)

            dve.wait_ge(bank_read, CT)
            one_hots(0, 0, wait=False)
            one_hots(1, 1, wait=False)
            with dve.Fori(1, LOOP2) as i:
                one_hots(0, i * 2)
                one_hots(1, i * 2 + 1)
            one_hots(0, NGB - 1)

            for p in range(2):
                dve.wait_ge(pair_free[p], N_D // 2 + 1)
                dve.sem_inc(d_free[p], 1)
            dve.wait_ge(bank_read, CT + 4 * NGB)
            for p in range(2, 4):
                dve.sem_inc(d_free[p], 1)

            def prepare(gg, g):
                dve.wait_ge(c_in[gg], (g - gg) * 16 + 32)
                a4 = c_act[gg][:, :, :].rearrange("p e (b t) -> p e b t", t=GB)
                V.tensor_tensor(a4, a4, c_gate[gg][:, :, :, :].rearrange("p b e t -> p e b t"), ALU.mult
                                ).then_inc(c_raw, 1)
                dve.wait_ge(c_hi_done, g + 1)
                V.tensor_tensor(c_lo[gg][:, :, :], c_act[gg][:, :, :], f(c_hi[gg][:, :, :]), ALU.subtract
                                ).then_inc(c_lo_done, 1)

            def gather(g):
                for d in range(KT):
                    dve.wait_ge(tile_done, g * 8 + (N_D + d + 1))
                    V.tensor_tensor(halves(x[:, d, :]), halves(x[:, d, :]), pair(d % 4), ALU.add
                                    ).then_inc(d_free[d % 4], 1)

            prepare(0, 0)
            with dve.Fori(0, NGRP // 2 - 1) as i:
                for gg in range(2):
                    prepare(1 - gg, i * 2 + (gg + 1))
                    gather(i * 2 + gg)
            prepare(1, NGRP - 1)
            gather(NGRP - 2)
            gather(NGRP - 1)
            norm(2, yraw, "normf", split=False)


def _tiles(w):
    n = w.shape[1] // P
    return w.reshape(KT, P, n, P).transpose(2, 1, 0, 3).reshape(n, P, D)


def _blocks(v):
    return v.reshape(-1, P).T


def kernel(**inputs):
    import concourse.bacc as _bacc
    from concourse.bass_utils import run_bass_kernel_spmd as _run

    a = {k: np.asarray(v) for k, v in inputs.items()}
    f4 = np.float32
    tokens = np.concatenate([a["meta"], a["x_prompt"][0], a["x_sample"].reshape(NSEQ * DEC, D)], axis=0)
    feat = lambda t: t.T.reshape(KT, P, -1).transpose(1, 0, 2)
    win = a["w_in"][0]
    offs = np.cumsum([0, D, D, HEADS * DK, HEADS * DK, HEADS * DV, HEADS * DV, RANK, D, D])
    xa, ga, q, k, v, r, gl, za, zb = (win[:, offs[i]:offs[i + 1]] for i in range(9))
    inter = lambda p, q_: np.stack([_tiles(p), _tiles(q_)], axis=1).reshape(2 * KT, P, D)
    trunk = np.concatenate([_tiles(q), _tiles(k), _tiles(v), _tiles(xa), _tiles(ga), inter(za, a["w_pa"][0]),
                            _tiles(r), inter(zb, a["w_pb"][0]), _tiles(a["w_out"][0]), _tiles(a["peer_wq"][0])])
    up = a["peer_u"][0].reshape(NK, NK, KT, P).transpose(0, 3, 2, 1).reshape(NK, P, D)
    down = a["peer_v"][0].reshape(NGRP, E1G, NK, KT, P).transpose(0, 3, 2, 1, 4).reshape(NGRP * KT, P, D)
    vec = {"norm1": a["norm1_g"][0], "cw0": a["conv_w"][0, 0], "cw1": a["conv_w"][0, 1], "cw2": a["conv_w"][0, 2],
           "cw3": a["conv_w"][0, 3], "cb": a["conv_b"][0], "ba": a["rg_ba"][0], "bx": a["rg_bx"][0],
           "lam": a["rg_lam"][0], "norm2": a["norm2_g"][0], "normf": a["normf_g"], "bg": a["gla_bg"][0],
           "gng": a["gla_norm_g"][0]}
    cols = np.concatenate([_blocks(vec[n]) for n in COLS], axis=1)
    s_, t_ = np.arange(P)[:, None], np.arange(P)[None, :]
    masks = np.stack([s_ == t_] + [(s_ // (2 * h) == t_ // (2 * h)) & (s_ % (2 * h) < h) & (t_ % (2 * h) >= h)
                                   for h in HALF], axis=1).astype(f4)
    reset = np.ones((P, T), f4)
    reset[:, list(range(0, CT * P, P)) + list(range(TP, T, DEC))] = 0.0
    rows = np.arange(P)[:, None] - PREST
    segmask = ((rows // DEC == np.arange(NSEQ)[None, :]) & (rows >= 0)).astype(f4)
    iota = np.broadcast_to(np.arange(P, dtype=f4)[None, :], (P, P))
    gates = np.zeros((P, 2, KT, P), f4)
    for g, w in enumerate((a["rg_wa"][0], a["rg_wx"][0])):
        for n in range(16):
            e = 64 * (n % 2)
            gates[e:e + 64, g, n // 2, e:e + 64] = w[n]
    keys = np.stack([a["peer_k1"][0], a["peer_k2"][0]], axis=1).transpose(3, 0, 1, 2)
    arrays = {
        "xT": feat(tokens), "trunk": trunk, "up": up, "down": down, "cols": cols, "masks": masks,
        "ident": np.eye(P, dtype=f4), "reset": reset, "segmask": segmask, "iota": iota,
        "wgl": gl.reshape(KT, P, RANK).transpose(1, 0, 2), "wg": a["gla_wg"][0], "gates": gates, "keys": keys,
        "conv0": a["state_conv"][0].transpose(2, 0, 1).reshape(KT, P, NSEQ, 3).transpose(1, 0, 2, 3),
        "h0": a["state_rglru"][0].T.reshape(KT, P, NSEQ).transpose(1, 0, 2),
        "gla0": a["state_gla"][0],
    }
    outs = {"yT": (P, KT, T), "conv_out": (P, KT, 1 + NSEQ, 3), "h_out": (P, KT, 1 + NSEQ),
            "gla_p": (HEADS, DK, DV), "gla_s": (NSEQ, HEADS, DK, DV)}
    nc = _bacc.Bacc("TRN2", target_bir_lowering=False, num_devices=1)
    feed, args = {}, {}
    for name, arr in arrays.items():
        arr = np.ascontiguousarray(arr)
        feed["in_" + name] = arr
        args[name] = nc.dram_tensor("in_" + name, arr.shape, mybir.dt.from_np(arr.dtype), kind="ExternalInput").ap()
    args["a_dram"] = nc.dram_tensor("act_scratch", (NK, P, T), F32).ap()
    args["g_dram"] = nc.dram_tensor("gate_scratch", (NGB, P, NK * GB), F32).ap()
    for name, shape in outs.items():
        args[name] = nc.dram_tensor("out_" + name, shape, F32, kind="ExternalOutput").ap()
    build(nc, **args)
    res = _run(nc, [feed], core_ids=[0]).results[0]
    y = res["out_yT"].transpose(1, 0, 2).reshape(D, T).T
    hs = res["out_h_out"].transpose(2, 1, 0).reshape(1 + NSEQ, D)
    cs = res["out_conv_out"].transpose(2, 3, 1, 0).reshape(1 + NSEQ, 3, D)
    return (np.ascontiguousarray(y[META:TP])[None], np.ascontiguousarray(y[TP:]).reshape(NSEQ, DEC, D),
            cs[None, 0:1], hs[None, 0:1], res["out_gla_p"][None, None], cs[None, 1:], hs[None, 1:],
            res["out_gla_s"][None])
```

```python
import numpy as np

import concourse.bass as bass
from concourse import mybir
from concourse.bass import ds

F32 = mybir.dt.float32
F32R = mybir.dt.float32r
U8 = mybir.dt.uint8
U32 = mybir.dt.uint32
ALU = mybir.AluOpType
ACT = mybir.ActivationFunctionType
AX = mybir.AxisListType.X

P = 128
D = 1024
KT = D // P
META, SEQ = 16, 512
NSEQ, DEC = 8, 8
TP = META + SEQ
T = TP + NSEQ * DEC
H2 = T // 2
TO = T - META
HO = TO // 2
OLAST = TO % P
EPS = 1e-6
HEADS, DK, DV, RANK = 4, 128, 256, 16
CT = (T + P - 1) // P
LAST = T - (CT - 1) * P
PREST = TP - (CT - 1) * P
HALF = [64, 32, 16, 8, 4, 2, 1]
PH, NK, TOPK = 8, 128, 16
GB = 16
NGB = TO // GB
QT = 4
BQ = GB // QT
RING = 4
AHEAD = 3
E1G = 8
NGRP = NK // E1G

N_Q, N_K, N_V, N_XA, N_ZA, N_R, N_GZ, N_PA, N_PB, N_OUT, N_WQ, N_U, N_D, N_END = (
    0, 4, 8, 16, 24, 32, 40, 56, 64, 72, 80, 96, 224, 352)

LOOP1 = 52
LOOP2 = NGB // 2
TAIL = NK - LOOP1 - 4 * LOOP2
assert NGB == 2 * LOOP2 and TAIL >= 0 and LOOP1 % 4 == 0
CONSTS = 16 * 8


def level_span(lv):
    hs = HALF[lv - 1]
    return (CT - 1) * P if hs > DEC else TP if hs == DEC else T


def level_tiles(lv):
    last = LAST if lv == 0 else level_span(lv) - (CT - 1) * P
    return [(c, P) for c in range(CT - 1)] + ([(CT - 1, last)] if last else [])


def turns_to(lv):
    return sum(len(level_tiles(v)) for v in range(lv + 1))


TURNS = turns_to(len(HALF))


COLS = {}
_n = 0
for _name, _w in (("norm1", 8), ("cw0", 8), ("cw1", 8), ("cw2", 8), ("cw3", 8), ("cb", 8), ("ba", 8), ("bx", 8),
                  ("lam", 8), ("norm2", 8), ("normf", 8), ("bg", 4), ("gng", 2)):
    COLS[_name] = _n
    _n += _w
NCOL = _n


def build(nc, xT, trunk, up, down, cols, masks, ident, reset, segmask, iota, wgl, wg, gates, keys, conv0, h0,
          gla0, a_dram, g_dram, s_dram, yT, conv_out, h_out, gla_p, gla_s):
    def sem(name):
        return nc.semaphore(name).__enter__()

    base = 16512
    TB = KT * T * 4

    def at(name, shape, dt, off):
        return nc.alloc_sbuf_tensor_at(name, shape, dt, offset=base + off)

    o_ring = 0
    w_raw = [at(f"w_raw{i}", [P, KT, P], F32, o_ring + 4096 * i) for i in range(4)]
    w_hi = [at(f"w_hi{i}", [P, KT, P], F32R, o_ring + 16384 + 4096 * i) for i in range(2)]
    w_lo = [at(f"w_lo{i}", [P, KT, P], F32R, o_ring + 24576 + 4096 * i) for i in range(2)]
    o_const = 32768
    col = at("col", [P, NCOL], F32, o_const)
    small = at("small", [P, 64], F32, o_const + 512)
    idt = at("idt", [P, P], F32, o_const + 1024)
    ones = at("ones", [P, P], F32, o_const + 1536)
    iot = at("iot", [P, P], F32, o_const + 2048)
    rstd = at("rstd", [P, T], F32, o_const + 2560)
    o_x = o_const + 2560 + 2368
    x = at("x", [P, KT, T], F32, o_x)
    o_h = o_x + TB
    h_hi = at("h_hi", [P, KT, T], F32R, o_h)
    h_lo = at("h_lo", [P, KT, T], F32R, o_h + TB)
    r3 = o_h + 2 * TB
    r4 = r3 + TB
    r5 = r4 + CT * D * 4
    r6 = r5 + TB
    XPW = 3 + TP + NSEQ * (3 + DEC)
    r7 = r6 + KT * XPW * 4 + 32
    hn_raw = at("hn_raw", [P, KT, T], F32, r3)
    qk = at("qk", [P, KT, T], F32, r3)
    y_hi = at("y_hi", [P, KT, TO], F32R, r3)
    v_nat = at("v_nat", [P, CT, D], F32, r4)
    y_lo = at("y_lo", [P, KT, TO], F32R, r4)
    vT = at("vT", [P, KT, T], F32, r5)
    zed = [at(f"zed{i}", [P, HEADS, T], F32, r5 + i * TB // 2) for i in range(2)]
    o = at("o", [P, KT, T], F32, r5)
    hn2_raw = at("hn2_raw", [P, KT, T], F32, r6)
    xpad = at("xpad", [P, KT, XPW], F32, r6)
    g7 = r7
    attn = at("attn", [P, CT, HEADS, P], F32, g7)
    gtmp = at("gtmp", [P, HEADS, T], F32, g7)
    cum = at("cum", [P, HEADS, T], F32, g7 + 10240)
    st_p = at("st_p", [P, HEADS, DV], F32, g7 + 19712)
    st_s = [at(f"st_s{i}", [P, HEADS, DV], F32, g7 + 23808 + 4096 * i) for i in range(2)]
    lmask_in = at("lmask_in", [P, 8, P], F32, r5)
    lmask = at("lmask", [P, 8, P], U8, g7 + 32000)
    k_nat = at("k_nat", [P, HEADS * DK], F32, g7 + 33024)
    k_seg = at("k_seg", [P, HEADS * DK], F32, g7 + 35072)
    end_cum = at("end_cum", [P, HEADS, 16], F32, g7 + 37120)
    segm = at("segm", [P, NSEQ], F32, o_const + 768)
    assert base + g7 + 37408 < 229368, g7
    wgl_sb = at("wgl_sb", [P, KT, RANK], F32, g7 + 19712)
    wg_sb = at("wg_sb", [RANK, HEADS * DK], F32, g7 + 20224)
    glT = at("glT", [RANK, T], F32, g7 + 22272)
    rst = at("rst", [P, T], F32, g7 + 24640)
    sq = at("sq", [P, T], F32, o_h + 8 * TB)
    stg = at("stg", [P, TO], F32, g7 + 37408)
    assert base + g7 + 37408 + 2368 < 229368
    ga = at("ga", [P, KT, TO], F32, r7)
    sr = at("sr", [P, KT, TO], F32, r7)
    zsb = at("zsb", [P, KT, TO], F32, r7)
    mix = at("mix", [P, KT, TO], F32, o_h)
    zsa = at("zsa", [P, KT, TO], F32, o_h + TB)
    y2_hi = at("y2_hi", [P, KT, TO], F32R, r6)
    t7 = r7 + TB
    xc = at("xc", [P, T], F32, t7)
    rr = at("rr", [P, T], F32, t7 + 2368)
    ii = at("ii", [P, T], F32, t7 + 2 * 2368)
    aa = at("aa", [P, T], F32, t7 + 3 * 2368)
    y2_lo = at("y2_lo", [P, KT, TO], F32R, t7)
    sq_o = at("sq_o", [P, 2, TO], F32, r6)
    c0sb = at("c0sb", [P, KT, NSEQ, 3], F32, t7 + 9472)
    gate_w = at("gate_w", [P, 2, KT, P], F32, t7 + 10240)
    h0sb = at("h0sb", [P, KT, NSEQ], F32, r4 + TB)
    hfin = at("hfin", [P, KT, 1 + NSEQ], F32, r4 + TB + 256)
    cfin = at("cfin", [P, KT, 1 + NSEQ, 3], F32, r4 + TB + 544)
    assert t7 + 18432 <= g7 + 37408 and TB + 544 + 864 <= CT * D * 4
    hh = rstd
    prod = rstd[:, META:]
    s3 = r3
    scores = at("scores", [P, CT, 16, NK], F32, s3)
    oh2 = [at(f"oh2{i}", [P, QT, NK], F32R, s3 + 2048 * i) for i in range(RING)]
    oh1 = [at(f"oh1{i}", [P, QT, 2, NK], F32R, s3 + 8192 + 4096 * i) for i in range(RING)]
    row1 = [at(f"row1{i}", [P, QT, NK], F32, s3 + 45568 + 2048 * i) for i in range(RING)]
    gst = [at(f"gst{i}", [P, NK, GB], F32, s3 + 24576 + 8192 * i) for i in range(2)]
    g_hi = at("g_hi", [P, TO], F32R, s3 + 40960)
    g_lo = at("g_lo", [P, TO], F32, s3 + 40960 + 2304)
    s4 = s3 + 49152
    keys_sb = at("keys_sb", [P, PH, 2, NK], F32, s4)
    qh = [at(f"qh{i}", [P, 2, TO], F32, s4 + 8192 + 4736 * i) for i in range(2)]
    work = at("work", [P, 16, NK], F32, s4)
    cand = at("cand", [P, PH, TOPK, TOPK], F32, s4 + 8192)
    pick = at("pick", [P, PH, TOPK, TOPK], F32, s4 + 16384)
    ast = [at(f"ast{i}", [P, TO], F32, s4 + 24576 + 2368 * i) for i in range(4)]
    s5 = s4 + 24576 + 4 * 2368
    chosen = at("chosen", [P, CT, 3, P], F32, s5)
    chT = at("chT", [P, 3, TO], F32, s5 + 7680)
    s6 = s5 + 7680 + 7104
    tv = at("tv", [P, 16, TOPK], F32, s6)
    ti = at("ti", [P, 16, TOPK], U32, s6 + 1024)
    tif = at("tif", [P, 16, TOPK], F32, s6 + 2048)
    cv = at("cv", [P, PH, TOPK], F32, s6 + 3072)
    ci = at("ci", [P, PH, TOPK], U32, s6 + 3584)
    ca = at("ca", [P, 2, PH, TOPK], U32, s6 + 4096)
    caf = at("caf", [P, 2, PH, TOPK], F32, s6 + 5120)
    sm = at("sm", [P, CT, PH], F32, s6 + 6144)
    assert base + s6 + 6304 < 229368
    place = ((2, 0), (3, 1), (4, 5), (7, 6))
    c_act, c_gate, c_hi, c_lo = (
        [at(f"{name}{i}", shape, dt, o_h + where[i] * TB) for i in range(2)] for name, shape, dt, where in (
            ("c_act", [P, E1G, TO], F32, place[0]), ("c_gate", [P, NGB, E1G, GB], F32, place[1]),
            ("c_hi", [P, E1G, TO], F32R, place[2]), ("c_lo", [P, E1G, TO], F32R, place[3])))
    assert base + o_h + 8 * TB + 2368 < 229368
    yraw = at("yraw", [P, KT, TO], F32, o_h)

    ps = nc.alloc_psum_tensor("ps", [P, 8, 512], F32)

    def pair(p):
        return ps[:, 2 * p:2 * p + 2, 0:H2]

    def opair(p):
        return ps[:, 2 * p:2 * p + 2, 0:HO]

    def halves(ap):
        return ap.rearrange("p (a b) -> p a b", a=2)

    def block(buf, m):
        return buf[:, ds(m, 1), :].rearrange("p o (a b) -> p (o a) b", a=2)

    def f(ap):
        return ap.bitcast(F32)

    def quad_views(q):
        place_ = gst[q // BQ][:, :, QT * (q % BQ):QT * (q % BQ + 1)].rearrange("p e t -> p t e")
        return place_, ps[:, 4 + 2 * (q % 2):6 + 2 * (q % 2), :].rearrange("p a (t s e) -> p (a t) s e", s=2, e=NK)

    def c_(name, k=0):
        j = COLS[name] + k
        return col[:, j:j + 1]

    x_in = [sem(f"x_in{i}") for i in range(4)]
    sig_stored, zsa_in, sr_in, zsb_in = (sem(n) for n in ("sig_stored", "zsa_in", "sr_in", "zsb_in"))
    const_in = sem("const_in")
    rgw_in = sem("rgw_in")
    keys_in = sem("keys_in")
    raw_in = [sem(f"raw_in{i}") for i in range(4)]
    w_hi_done = sem("w_hi_done")
    w_split = sem("w_split")
    tile_done = sem("tile_done")
    pair_free = [sem(f"pair_free{i}") for i in range(2)]
    ones_set = sem("ones_set")
    masks_in = sem("masks_in")
    passed = sem("passed")
    sq_done, sq_used, ms_done, rms_done, nrm_done, hi_done, lo_done = (
        sem(n) for n in ("sq_done", "sq_used", "ms_done", "rms_done", "nrm_done", "hi_done", "lo_done"))
    dve_step, act_step = sem("dve_step"), sem("act_step")
    gl_done, gl_copied, z_done, z_read, lsig, cum_done = (
        sem(n) for n in ("gl_done", "gl_copied", "z_done", "z_read", "lsig", "cum_done"))
    vt_done, vt_copied = sem("vt_done"), sem("vt_copied")
    diff_done, exp_done, zed_done, zed_used, a_done, a_copied = (
        sem(n) for n in ("diff_done", "exp_done", "zed_done", "zed_used", "a_done", "a_copied"))
    end_done, qe_exp, qe_done, kT_done, k_nat_done, o_done, o_copied, u_done, s_done, kseg_done, si_done = (
        sem(n) for n in ("end_done", "qe_exp", "qe_done", "kT_done", "k_nat_done", "o_done", "o_copied", "u_done",
                         "s_done", "kseg_done", "si_done"))
    gla_in = [sem(f"gla_in{i}") for i in range(2)]
    gla_out = [sem(f"gla_out{i}") for i in range(2)]
    glap_out = sem("glap_out")
    osq_done, osq_used, orms_done, o_norm = (sem(n) for n in ("osq_done", "osq_used", "orms_done", "o_norm"))
    tap0, conv_done, gates_done, ri_done, ae_done, w2_done, sq2_done, ya_done, yhi_done, ylo_done = (
        sem(n) for n in ("tap0", "conv_done", "gates_done", "ri_done", "ae_done", "w2_done", "sq2_done", "ya_done",
                         "yhi_done", "ylo_done"))
    states_done, mix_done, small_out = sem("states_done"), sem("mix_done"), sem("small_out")
    lam_abs, lam_exp = sem("lam_abs"), sem("lam_exp")
    sc_done, sc_copied = sem("sc_done"), sem("sc_copied")
    top_step, picked, gate_exp, chosen_done, ct_done, bank_read = (
        sem(n) for n in ("top_step", "picked", "gate_exp", "chosen_done", "ct_done", "bank_read"))
    a_stored = [sem(f"a_stored{i}") for i in range(4)]
    gparts_done, oh_done, ohg_done, g_mm, g_part = (
        sem(n) for n in ("gparts_done", "oh_done", "ohg_done", "g_mm", "g_part"))
    g_stored = [sem(f"g_stored{i}") for i in range(2)]
    c_in = [sem(f"c_in{i}") for i in range(2)]
    c_raw, c_hi_done, c_lo_done = sem("c_raw"), sem("c_hi_done"), sem("c_lo_done")
    d_free = [sem(f"d_free{i}") for i in range(4)]
    y_done, y_out = sem("y_done"), sem("y_out")

    blk = nc.Block()
    with blk as b:

        @b.sync
        def _(sp):
            for i in range(4):
                sp.dma_start(x[:, 2 * i:2 * i + 2, :], xT[:, 2 * i:2 * i + 2, :]).then_inc(x_in[i], 16)

            def load(src, i, first, j):
                n = first + j if i is None else i * 4 + (first + j)
                if i is not None:
                    sp.wait_ge(w_split, n - 3)
                k = j if i is None else i * 4 + j
                sp.dma_start(w_raw[j][:, :, :], src[ds(k, 1), :, :].rearrange("o p (k m) -> p (o k) m", m=P)
                             ).then_inc(raw_in[j], 16)

            for j in range(4):
                load(trunk, None, 0, j)
            with sp.Fori(1, N_U // 4) as i:
                for j in range(4):
                    load(trunk, i, 0, j)
            with sp.Fori(0, (N_D - N_U) // 4) as i:
                for j in range(4):
                    load(up, i, N_U, j)
            with sp.Fori(0, (N_END - N_D) // 4) as i:
                for j in range(4):
                    load(down, i, N_D, j)
            for k in range(KT):
                sp.wait_ge(y_done, k + 1)
                sp.dma_start(yT[:, k, :], yraw[:, k, :]).then_inc(y_out, 16)
            sp.wait_ge(y_out, 16 * KT)

        @b.gpsimd
        def _(pool):
            def split(j, n, free=True):
                pool.wait_ge(raw_in[j], (n - j) * 4 + 16)
                if free:
                    pool.wait_ge(tile_done, n - 1)
                pool.sem_inc(passed, 1)
                nc.gpsimd.tensor_scalar(w_hi[j % 2][:, :, :], w_raw[j][:, :, :], 1.0, 1.0, ALU.mult, ALU.mult
                                        ).then_inc(w_hi_done, 1)
                pool.wait_ge(w_hi_done, n + 1)
                nc.gpsimd.tensor_tensor(w_lo[j % 2][:, :, :], w_raw[j][:, :, :], f(w_hi[j % 2][:, :, :]),
                                        ALU.subtract).then_inc(w_split, 1)

            for j in range(4):
                split(j, j, free=j >= 2)
            with pool.Fori(1, N_END // 4) as i:
                for j in range(4):
                    split(j, i * 4 + j)

        @b.tensor
        def _(pe):
            def product(j, n, hi, lo, p, ready=None, every=False):
                pe.wait_ge(w_split, n + 1)
                s = j % 2
                w = H2 if every else HO
                t0 = hi.shape[2] - 2 * w
                for k in range(KT):
                    if ready:
                        ready(k)
                    for part, (wt, act) in enumerate(((w_hi[s], hi), (w_hi[s], lo), (w_lo[s], hi))):
                        for a in range(2):
                            last = nc.tensor.matmul(
                                ps[:, 2 * p + a, 0:w], wt[:, k, :], act[:, k, t0 + a * w:t0 + (a + 1) * w],
                                start=k == 0 and part == 0, stop=k == KT - 1 and part == 2)
                last.then_inc(tile_done, 1)

            def stage(first, count, operand, ready=None, every=False):
                with pe.Fori(0, count // 4) as i:
                    for j in range(4):
                        pe.wait_ge(pair_free[j % 2], i * 2 + (first // 2 + j // 2 + 1))
                        product(j, i * 4 + (first + j), *operand(j), j % 2, ready if j == 0 else None, every)

            def norm(r):
                pe.wait_ge(sq_used, KT * (r + 1))
                w = H2 if r == 0 else HO
                for a in range(2):
                    last = nc.tensor.matmul(ps[:, 4 + a, 0:w], ones[:, :], rstd[:, T - (2 - a) * w:T - (1 - a) * w],
                                            start=True, stop=True)
                last.then_inc(ms_done, 1)

            def split_input(r):
                return lambda k: pe.wait_ge(lo_done, KT * r + k + 1)

            def tile(n, act=(h_hi, h_lo)):
                pe.wait_ge(pair_free[n % 2], n // 2 + 1)
                product(n, n, *act, n % 2)

            hn = lambda j: (h_hi, h_lo)
            pe.wait_ge(ones_set, 1)
            norm(0)
            pe.wait_ge(nrm_done, KT)
            pe.wait_ge(const_in, CONSTS)
            pe.wait_ge(rms_done, 1)
            for a in range(2):
                for k in range(KT):
                    last = nc.tensor.matmul(ps[0:RANK, 4 + a, 0:H2], wgl_sb[:, k, :],
                                            hn_raw[:, k, a * H2:(a + 1) * H2], start=k == 0, stop=k == KT - 1)
            last.then_inc(gl_done, 1)
            pe.wait_ge(gl_copied, 1)
            for h in range(HEADS):
                if h >= 2:
                    pe.wait_ge(z_read, 2 * (h - 1))
                for a in range(2):
                    last = nc.tensor.matmul(ps[:, 4 + 2 * (h % 2) + a, 0:H2], wg_sb[:, h * DK:(h + 1) * DK],
                                            glT[:, a * H2:(a + 1) * H2], start=True, stop=True)
                last.then_inc(z_done, 1)
            stage(N_Q, 16, hn, split_input(0), every=True)
            for p in range(2):
                pe.wait_ge(pair_free[p], N_XA // 2 + 1)
            pe.wait_ge(z_read, 2 * HEADS)
            for c in range(CT):
                w = P if c < CT - 1 else LAST
                if c >= 2:
                    pe.wait_ge(vt_copied, c - 1)
                for m in range(KT):
                    last = nc.tensor.transpose(ps[0:w, 4 + 2 * (c % 2) + m // 4, (m % 4) * P:(m % 4 + 1) * P],
                                               vT[:, m, c * P:c * P + w], idt[:, :])
                last.then_inc(vt_done, 1)
            stage(N_XA, 8, hn, every=True)
            pe.wait_ge(vt_copied, CT)
            turn = 0
            for lv in range(8):
                tile(N_ZA + lv)
                if lv:
                    pe.wait_ge(zed_done, lv)
                for c, w in level_tiles(lv):
                    if turn >= 4:
                        pe.wait_ge(a_copied, turn - 3)
                    for h in range(HEADS):
                        z, zk = (qk, HEADS + h) if lv == 0 else (zed[lv % 2], h)
                        last = nc.tensor.matmul(ps[0:w, 4 + turn % 4, h * P:h * P + w], z[:, zk, c * P:c * P + w],
                                                z[:, h, c * P:c * P + w], start=True, stop=True)
                    last.then_inc(a_done, 1)
                    turn += 1
            pe.wait_ge(a_copied, turn)
            pe.wait_ge(qe_done, 2)
            for c in range(CT):
                w, np_ = (P, P) if c < CT - 1 else (LAST, PREST)
                if c:
                    pe.wait_ge(s_done, 2 * c)
                for h in range(HEADS):
                    last = nc.tensor.transpose(ps[0:w, 6, h * P:(h + 1) * P], qk[:, HEADS + h, c * P:c * P + w],
                                               idt[:, :])
                last.then_inc(kT_done, 1)
                tile(N_R + c)
                if c:
                    pe.wait_ge(o_copied, c)
                for g in range(2 * HEADS):
                    h, d = g // 2, g % 2
                    b0 = 4 + g // 4
                    c0 = (g % 4) * P
                    last = nc.tensor.matmul(ps[:, b0, c0:c0 + w], v_nat[0:w, c, g * P:(g + 1) * P],
                                            attn[0:w, c, h, 0:w], start=True, stop=c == 0)
                    if c:
                        last = nc.tensor.matmul(ps[:, b0, c0:c0 + np_], st_p[:, h, d * P:(d + 1) * P],
                                                qk[:, h, c * P:c * P + np_], start=False, stop=True)
                last.then_inc(o_done, 1)
                pe.wait_ge(k_nat_done, c + 1)
                for hp in range(2):
                    for h in (2 * hp, 2 * hp + 1):
                        last = nc.tensor.matmul(ps[:, 7 - hp, (h % 2) * DV:(h % 2 + 1) * DV],
                                                k_nat[0:np_, h * DK:(h + 1) * DK],
                                                v_nat[0:np_, c, h * DV:(h + 1) * DV], start=True, stop=True)
                    last.then_inc(u_done, 1)
            pe.wait_ge(o_copied, CT)
            for s in range(NSEQ):
                if s % 2 == 0 and CT + s // 2 < KT:
                    tile(N_R + CT + s // 2)
                pe.wait_ge(gla_in[s % 2], 16 * (s // 2 + 1))
                for g in range(2 * HEADS):
                    h, d = g // 2, g % 2
                    t0 = TP + s * DEC
                    last = nc.tensor.matmul(ps[:, 4, g * 64 + s * DEC:g * 64 + (s + 1) * DEC],
                                            st_s[s % 2][:, h, d * P:(d + 1) * P], qk[:, h, t0:t0 + DEC],
                                            start=True, stop=True)
                last.then_inc(si_done, 1)
                pe.wait_ge(kseg_done, s + 1)
                pe.wait_ge(s_done, 2 * (CT + s))
                for hp in range(2):
                    for h in (2 * hp, 2 * hp + 1):
                        last = nc.tensor.matmul(ps[:, 7 - hp, (h % 2) * DV:(h % 2 + 1) * DV],
                                                k_seg[0:LAST, h * DK:(h + 1) * DK],
                                                v_nat[0:LAST, CT - 1, h * DV:(h + 1) * DV], start=True, stop=True)
                    last.then_inc(u_done, 1)
            pe.wait_ge(s_done, 2 * (CT + NSEQ))
            pe.wait_ge(o_norm, 1)
            pe.wait_ge(rgw_in, 16 * 3)
            for k in range(KT):
                pe.wait_ge(conv_done, 2 * (k + 1))
                if k:
                    pe.wait_ge(ri_done, 2 * k)
                for g in range(2):
                    for a in range(2):
                        last = nc.tensor.matmul(ps[:, 4 + 2 * g + a, 0:H2], gate_w[:, g, k, :],
                                                xc[:, a * H2:(a + 1) * H2], start=True, stop=True)
                last.then_inc(gates_done, 1)
                tile(N_GZ + 2 * k)
                tile(N_GZ + 2 * k + 1)
            pe.wait_ge(ri_done, 2 * KT)
            for m in range(KT):
                n = N_PA + m
                pe.wait_ge(pair_free[n % 2], n // 2 + 1)
                product(n, n, y_hi, y_lo, n % 2, (lambda k: pe.wait_ge(ylo_done, k + 1)) if m == 0 else None)
                if m < HEADS:
                    h = m
                    if h >= 2:
                        pe.wait_ge(orms_done, h - 1)
                    for d in range(2):
                        pe.wait_ge(osq_done, 2 * h + d + 1)
                        for a in range(2):
                            last = nc.tensor.matmul(ps[:, 4 + 2 * (h % 2) + a, 0:HO], ones[:, :],
                                                    sq_o[:, d, a * HO:(a + 1) * HO], start=d == 0, stop=d == 1)
                        last.then_inc(osq_used, 1)
            stage(N_PB, 8, lambda j: (y2_hi, y2_lo), lambda k: pe.wait_ge(ylo_done, KT + k + 1))
            stage(N_OUT, 8, lambda j: (y_hi, y_lo), lambda k: pe.wait_ge(ylo_done, 2 * KT + k + 1))
            norm(1)
            pe.wait_ge(keys_in, 16)
            pe.wait_ge(rms_done, 2)
            with pe.Fori(0, PH // 2) as i:
                for j in range(4):
                    pe.wait_ge(pair_free[j % 2], i * 2 + (N_WQ // 2 + j // 2 + 1))
                    product(j, i * 4 + (N_WQ + j), h_hi, h_lo, j % 2, split_input(1) if j == 0 else None)
                    if j % 2 == 0:
                        continue
                    hb = j // 2
                    for p in range(2):
                        pe.wait_ge(pair_free[p], i * 2 + (N_WQ // 2 + hb + 2))
                    pe.wait_ge(sc_copied, i * 6 + (3 * hb + 1))
                    for c in range(CT):
                        w = P if c < CT - 1 else OLAST
                        for side in range(2):
                            last = nc.tensor.matmul(
                                ps[0:w, 4 + c // 2, ((c % 2) * 2 + side) * P:((c % 2) * 2 + side + 1) * P],
                                qh[hb][:, side, c * P:c * P + w],
                                keys_sb[:, ds(i * 2 + hb, 1), side, :].rearrange("p o k -> p (o k)"),
                                start=True, stop=True)
                    last.then_inc(sc_done, 1)
            stage(N_U, LOOP1, hn)
            pe.wait_ge(sc_copied, 3 * PH + 1)
            pe.wait_ge(chosen_done, 1)
            for c in range(CT):
                w = P if c < CT - 1 else OLAST
                if c == 4:
                    pe.wait_ge(bank_read, 1)
                for q in range(3):
                    last = nc.tensor.transpose(ps[:, 4 + c % 4, q * P:q * P + w], chosen[0:w, c, q, :],
                                               idt[0:w, 0:w])
                last.then_inc(ct_done, 1)

            def gate_quad(q, n):
                pe.wait_ge(oh_done, 2 * n + 2)
                pe.wait_ge(ohg_done, n + 1)
                pe.wait_ge(bank_read, n + (CT - 1))
                for t in range(QT):
                    last = nc.tensor.matmul(ps[:, 4 + 2 * (q % 2) + t // 2, (t % 2) * 2 * P:(t % 2 + 1) * 2 * P],
                                            oh2[q][:, t, :], oh1[q][:, t, :, :].rearrange("p s e -> p (s e)"),
                                            start=True, stop=True)
                last.then_inc(g_mm, 1)

            pe.wait_ge(bank_read, CT)
            first = N_U + LOOP1
            with pe.Fori(0, LOOP2) as i:
                for j in range(4):
                    pe.wait_ge(pair_free[j % 2], i * 2 + (first // 2 + j // 2 + 1))

                    def quads(k):
                        if k in (2, 6):
                            q = 2 * j + k // 4
                            gate_quad(q % RING, i * 2 * BQ + q)

                    product(j, i * 4 + (first + j), h_hi, h_lo, j % 2, quads)
            stage(N_D - TAIL, TAIL, hn)
            with pe.Fori(0, NGRP // 2) as i:
                for gg in range(2):
                    pe.wait_ge(c_lo_done, i * 2 + (gg + 1))
                    for d in range(KT):
                        pe.wait_ge(d_free[d % 4], i * 4 + (2 * gg + d // 4 + 1))
                        product(d, i * 16 + (N_D + 8 * gg + d), c_hi[gg], c_lo[gg], d % 4)
            norm(2)

        @b.scalar
        def _(act):
            A = nc.scalar.activation

            def step(ins, n):
                ins.then_inc(act_step, 1)
                act.wait_ge(act_step, n)

            loads = ((col[:, :], cols), (idt[:, :], ident), (iot[:, :], iota), (lmask_in[:, :, :], masks),
                     (rst[:, :], reset), (segm[:, :], segmask), (wgl_sb[:, :, :], wgl), (wg_sb[:, :], wg))
            assert CONSTS == 16 * len(loads)
            for dst, src in loads:
                act.dma_start(dst, src).then_inc(const_in, 16)
            for p in range(2):
                act.sem_inc(pair_free[p], 1)
            for j in range(4):
                act.sem_inc(a_stored[j], 16)
            for j in range(2):
                act.sem_inc(g_stored[j], 16)

            epsc = small[:, 40:41]

            def norm(r, raw, split=True):
                t0 = META if r else 0
                for k in range(KT):
                    if r == 0:
                        act.wait_ge(x_in[k // 2], 16)
                    elif r == 1:
                        act.wait_ge(pair_free[k % 2], (N_OUT + k) // 2 + 2)
                    else:
                        act.wait_ge(d_free[k % 4], 2 * NGRP + k // 4)
                    if r or k:
                        act.wait_ge(sq_used, KT * r + k)
                    A(sq[:, t0:], x[:, k, t0:], ACT.Square).then_inc(sq_done, 1)
                act.wait_ge(ms_done, r + 1)
                A(halves(rstd[:, t0:]), opair(2) if r else pair(2), ACT.Sqrt, bias=epsc, scale=1.0 / D
                  ).then_inc(rms_done, 1)
                if split:
                    for k in range(KT):
                        act.wait_ge(nrm_done, 8 * r + k + 1)
                        A(h_hi[:, k, t0:], raw[:, k, t0:], ACT.Copy).then_inc(hi_done, 1)

            act.wait_ge(ones_set, 1)
            norm(0, hn_raw)
            act.wait_ge(lam_abs, 1)
            A(small[:, 16:24], small[:, 16:24], ACT.Exp, scale=-1.0).then_inc(lam_exp, 1)
            act.wait_ge(const_in, CONSTS)
            for h in range(HEADS):
                act.wait_ge(z_done, h + 1)
                A(halves(cum[:, h, :]), pair(2 + h % 2), ACT.Identity, bias=c_("bg", h)).then_inc(z_read, 1)
                A(halves(gtmp[:, h, :]), pair(2 + h % 2), ACT.Abs, bias=c_("bg", h)).then_inc(z_read, 1)
            act.wait_ge(z_read, 2 * HEADS)
            step(A(gtmp[:, :, :], gtmp[:, :, :], ACT.Exp, scale=-1.0), 1)
            A(gtmp[:, :, :], gtmp[:, :, :], ACT.Ln, bias=1.0).then_inc(lsig, 1)
            for n in range(8):
                act.wait_ge(tile_done, n + 1)
                if n == 0:
                    act.wait_ge(lo_done, KT)
                A(halves(qk[:, n, :]), pair(n % 2), ACT.Copy, scale=DK ** -0.5 if n < 4 else 1.0
                  ).then_inc(pair_free[n % 2], 1)
            act.wait_ge(masks_in, 1)
            with act.Fori(0, 4) as i:
                for j in range(2):
                    act.wait_ge(tile_done, i * 2 + (N_V + j + 1))
                    A(block(vT, i * 2 + j), pair(j), ACT.Copy).then_inc(pair_free[j], 1)
            def xa_tile(m):
                p = m % 2
                act.wait_ge(tile_done, N_XA + m + 1)
                A(xpad[:, m, 3:3 + H2], ps[:, 2 * p, 0:H2], ACT.Copy)
                A(xpad[:, m, 3 + H2:3 + TP], ps[:, 2 * p + 1, 0:TP - H2], ACT.Copy)
                A(xpad[:, m, 3 + TP:].rearrange("p (s c) -> p s c", s=NSEQ)[:, :, 3:],
                  ps[:, 2 * p + 1, TP - H2:H2].rearrange("p (s c) -> p s c", s=NSEQ), ACT.Copy
                  ).then_inc(pair_free[p], 1)

            def level_exp(lv):
                act.wait_ge(diff_done, lv)
                z = zed[lv % 2]
                span = level_span(lv)
                A(z[:, :, 0:span], z[:, :, 0:span], ACT.Exp).then_inc(exp_done, 1)

            for m in range(2):
                xa_tile(m)
                level_exp(m + 1)
            for m in range(2, KT):
                xa_tile(m)

            def to_dram(n, slot, func):
                act.wait_ge(tile_done, n + 1)
                if slot:
                    act.wait_ge(sig_stored, 16 * slot)
                A(halves(stg[:, :]), opair(n % 2), func).then_inc(pair_free[n % 2], 1)
                act.wait_ge(pair_free[n % 2], n // 2 + 2)
                act.dma_start(s_dram[slot, :, :], stg[:, :]).then_inc(sig_stored, 16)

            for m in range(KT):
                to_dram(N_ZA + m, m, ACT.Sigmoid)
                if 3 <= m + 2 <= 7:
                    level_exp(m + 2)
            act.wait_ge(a_done, TURNS)
            act.wait_ge(zed_done, 8)
            A(zed[0][:, :, :], cum[:, :, :], ACT.Exp).then_inc(qe_exp, 1)
            A(zed[1][:, :, :], zed[1][:, :, :], ACT.Exp).then_inc(qe_exp, 1)
            A(end_cum[:, :, 0:CT + NSEQ], end_cum[:, :, 0:CT + NSEQ], ACT.Exp).then_inc(end_done, 1)
            for s in range(2):
                act.dma_start(st_s[s][:, :, :], gla0[s].rearrange("h k v -> k h v")).then_inc(gla_in[s], 16)
            for c in range(CT):
                w = P if c < CT - 1 else LAST
                act.wait_ge(kT_done, c + 1)
                if c:
                    act.wait_ge(u_done, 2 * c)
                A(k_nat[0:w, :], ps[0:w, 6, :], ACT.Copy).then_inc(k_nat_done, 1)
                to_dram(N_R + c, KT + c, ACT.Silu)
                act.wait_ge(o_done, c + 1)
                if c == 0:
                    act.wait_ge(qe_done, 2)
                A(o[:, :, c * P:c * P + w],
                  ps[:, 4:6, :].rearrange("p a (g t) -> p (a g) t", g=4)[:, :, 0:w], ACT.Copy).then_inc(o_copied, 1)
            for s in range(NSEQ):
                if s % 2 == 0 and CT + s // 2 < KT:
                    to_dram(N_R + CT + s // 2, KT + CT + s // 2, ACT.Silu)
                act.wait_ge(s_done, 2 * (CT + s + 1))
                act.dma_start(gla_s[s].rearrange("h k v -> k h v"), st_s[s % 2][:, :, :]
                              ).then_inc(gla_out[s % 2], 16)
                if s + 2 < NSEQ:
                    act.wait_ge(gla_out[s % 2], 16 * (s // 2 + 1))
                    act.dma_start(st_s[s % 2][:, :, :], gla0[s + 2].rearrange("h k v -> k h v")
                                  ).then_inc(gla_in[s % 2], 16)
            act.dma_start(gla_p.rearrange("h k v -> k h v"), st_p[:, :, :]).then_inc(glap_out, 16)
            act.wait_ge(glap_out, 16)
            for i in range(2):
                act.wait_ge(gla_out[i], 16 * (NSEQ // 2))
            act.dma_start(gate_w[:, :, :, :], gates).then_inc(rgw_in, 16)
            act.dma_start(c0sb[:, :, :, :], conv0).then_inc(rgw_in, 16)
            act.dma_start(h0sb[:, :, :], h0).then_inc(rgw_in, 16)
            act.wait_ge(rgw_in, 16 * 3)
            act.wait_ge(w2_done, 1)

            def first_tap(k):
                A(xc[:, 0:TP], xpad[:, k, 3:3 + TP], ACT.Identity, bias=c_("cb", k), scale=c_("cw3", k)
                  ).then_inc(tap0, 1)
                A(xc[:, TP:].rearrange("p (s c) -> p s c", s=NSEQ),
                  xpad[:, k, 3 + TP:].rearrange("p (s c) -> p s c", s=NSEQ)[:, :, 3:],
                  ACT.Identity, bias=c_("cb", k), scale=c_("cw3", k)).then_inc(tap0, 1)

            first_tap(0)
            for k in range(KT):
                act.wait_ge(gates_done, k + 1)
                if k:
                    act.wait_ge(w2_done, 1 + 3 * k)
                A(halves(rr[:, :]), pair(2), ACT.Sigmoid, bias=c_("ba", k)).then_inc(ri_done, 1)
                A(halves(ii[:, :]), pair(3), ACT.Sigmoid, bias=c_("bx", k)).then_inc(ri_done, 1)
                act.wait_ge(ri_done, 2 * k + 2)
                A(aa[:, :], rr[:, :], ACT.Exp, scale=small[:, k:k + 1]).then_inc(ae_done, 1)
                A(rr[:, :], rr[:, :], ACT.Tanh, scale=small[:, 8 + k:9 + k]).then_inc(ae_done, 1)
                act.wait_ge(w2_done, 1 + 3 * k + 1)
                A(rr[:, :], rr[:, :], ACT.Sqrt).then_inc(sq2_done, 1)
                if k < KT - 1:
                    first_tap(k + 1)
                n = N_GZ + 2 * k
                act.wait_ge(tile_done, n + 1)
                A(halves(ga[:, k, :]), opair(0), ACT.Gelu).then_inc(pair_free[0], 1)
                act.wait_ge(ya_done, k + 1)
                A(y_hi[:, k, :], ga[:, k, :], ACT.Copy).then_inc(yhi_done, 1)
                to_dram(n + 1, 2 * KT + k, ACT.Sigmoid)
            act.wait_ge(sig_stored, 16 * 3 * KT)

            def from_dram(dst, first, done):
                act.dma_start(dst[:, :, :], s_dram[first:first + KT, :, :].rearrange("k p t -> p k t")
                              ).then_inc(done, 16)

            act.wait_ge(tile_done, N_PA)
            from_dram(zsa, 0, zsa_in)
            act.wait_ge(ylo_done, KT)
            from_dram(sr, KT, sr_in)
            act.wait_ge(states_done, 1)
            act.dma_start(conv_out, cfin[:, :, :, :]).then_inc(small_out, 16)
            act.dma_start(h_out, hfin[:, :, :]).then_inc(small_out, 16)
            for h in range(HEADS):
                for d in range(2):
                    if h:
                        act.wait_ge(osq_used, 2 * (h - 1) + d + 1)
                    A(sq_o[:, d, :], o[:, 2 * h + d, META:], ACT.Square).then_inc(osq_done, 1)
                act.wait_ge(osq_used, 2 * h + 2)
                if h:
                    act.wait_ge(o_norm, 1 + 2 * h)
                A(halves(rstd[:, META:]), opair(2 + h % 2), ACT.Sqrt, bias=epsc, scale=1.0 / DV).then_inc(orms_done, 1)
            for k in range(KT):
                act.wait_ge(ya_done, KT + k + 1)
                A(y2_hi[:, k, :], o[:, k, META:], ACT.Copy).then_inc(yhi_done, 1)
            act.wait_ge(small_out, 32)
            act.wait_ge(ya_done, 2 * KT)
            from_dram(zsb, 2 * KT, zsb_in)
            act.wait_ge(tile_done, N_PB)
            for m in range(KT):
                act.wait_ge(mix_done, m + 1)
                A(y_hi[:, m, :], mix[:, m, :], ACT.Copy).then_inc(yhi_done, 1)
            norm(1, hn2_raw)
            act.wait_ge(lo_done, 2 * KT)
            act.dma_start(keys_sb[:, :, :, :], keys).then_inc(keys_in, 16)
            with act.Fori(0, PH // 2) as i:
                for j in range(4):
                    act.wait_ge(tile_done, i * 4 + (N_WQ + j + 1))
                    act.wait_ge(sc_copied, i * 6 + 1)
                    A(halves(qh[j // 2][:, j % 2, :]), opair(j % 2), ACT.Copy).then_inc(pair_free[j % 2], 1)
            act.wait_ge(sc_copied, 3 * PH + 1)

            def up_tiles(i0, i1, before=None, after=None):
                with act.Fori(i0, i1) as i:
                    for j in range(4):
                        if before:
                            before(j, i - i0)
                        act.wait_ge(tile_done, i * 4 + (N_U + j + 1))
                        act.wait_ge(a_stored[j], i * 16 + 16)
                        A(halves(ast[j][:, :]), opair(j % 2), ACT.Gelu).then_inc(pair_free[j % 2], 1)
                        act.wait_ge(pair_free[j % 2], i * 2 + (N_U // 2 + j // 2 + 2))
                        act.dma_start(a_dram[ds(i * 4 + j, 1), :, :].rearrange("o p t -> p (o t)"), ast[j][:, :]
                                      ).then_inc(a_stored[j], 16)
                        if after:
                            after(j, i - i0)

            up_tiles(0, LOOP1 // 4)
            act.wait_ge(picked, 1)
            A(chosen[:, :, 2, :], chosen[:, :, 2, :], ACT.Exp).then_inc(gate_exp, 1)
            for c in range(CT):
                act.wait_ge(ct_done, c + 1)
                w = P if c < CT - 1 else OLAST
                A(chT[:, :, c * P:c * P + w], ps[:, 4 + c % 4, 0:3 * P].rearrange("p (q t) -> p q t", q=3)[:, :, 0:w],
                  ACT.Copy).then_inc(bank_read, 1)

            act.wait_ge(bank_read, CT)
            A(g_hi[:, :], chT[:, 2, :], ACT.Copy).then_inc(gparts_done, 1)

            def gated(q, n):
                act.wait_ge(oh_done, 2 * n + 1)
                for t in range(QT):
                    last = A(oh1[q][:, t, 1, :], row1[q][:, t, :], ACT.Copy, scale=g_lo[:, ds(n * QT + t, 1)])
                last.then_inc(ohg_done, 1)

            def gates_out(j, i, more=True):
                for q in (2 * j, 2 * j + 1):
                    if q % BQ == 0:
                        act.wait_ge(g_stored[q // BQ], i * 16 + 16)
                    act.wait_ge(g_mm, i * 2 * BQ + (q + 1))
                    gates_, parts = quad_views(q)
                    A(gates_, parts[:, :, 1, :], ACT.Copy).then_inc(g_part, 1)
                    if more or q + AHEAD - 1 < 2 * BQ:
                        gated((q + AHEAD - 1) % RING, i * 2 * BQ + (q + AHEAD - 1))

            def store_gates(j, i):
                if j % 2 == 0:
                    return
                bb = j // 2
                act.wait_ge(bank_read, i * 2 * BQ + (CT + BQ * (bb + 1)))
                act.dma_start(g_dram[ds(i * 2 + bb, 1), :, :].rearrange("o p e -> p (o e)"),
                              gst[bb][:, :, :].rearrange("p e t -> p (e t)")).then_inc(g_stored[bb], 16)

            i0 = LOOP1 // 4
            act.wait_ge(gparts_done, 2)
            for q in range(AHEAD - 1):
                gated(q, q)
            up_tiles(i0, i0 + LOOP2 - 1, gates_out, store_gates)
            up_tiles(i0 + LOOP2 - 1, i0 + LOOP2, lambda j, i: gates_out(j, i + (LOOP2 - 1), False),
                     lambda j, i: store_gates(j, i + (LOOP2 - 1)))

            def c_load(gg, g):
                act.dma_start(c_act[gg][:, :, :], a_dram[ds(g * E1G, E1G), :, :].rearrange("e p t -> p e t")
                              ).then_inc(c_in[gg], 16)
                act.dma_start(c_gate[gg][:, :, :, :].rearrange("p b e t -> p b (e t)"),
                              g_dram[:, :, ds(g * (E1G * GB), E1G * GB)].rearrange("b p e -> p b e")
                              ).then_inc(c_in[gg], 16)

            def c_split(gg, g):
                act.wait_ge(c_raw, g + 1)
                A(c_hi[gg][:, :, :], c_act[gg][:, :, :], ACT.Copy).then_inc(c_hi_done, 1)

            act.wait_ge(g_stored[0], 16 * (NGB // 2 + 1))
            act.wait_ge(g_stored[1], 16 * (NGB // 2 + 1))
            for j in range(4):
                act.wait_ge(a_stored[j], 16 * ((NK - TAIL) // 4 + 1))
            c_load(0, 0)
            up_tiles(i0 + LOOP2, NK // 4)
            c_split(0, 0)
            for j in range(4):
                act.wait_ge(a_stored[j], 16 * (NK // 4 + 1))
            act.wait_ge(tile_done, N_D)
            c_load(1, 1)
            with act.Fori(0, NGRP // 2 - 1) as i:
                for gg in range(2):
                    g = i * 2 + gg
                    act.wait_ge(c_lo_done, g + 1)
                    c_load(gg, g + 2)
                    c_split(1 - gg, g + 1)
            c_split(1, NGRP - 1)
            norm(2, yraw, split=False)

        @b.vector
        def _(dve):
            V = nc.vector
            n_step = [0]

            def link(ins):
                n_step[0] += 1
                ins.then_inc(dve_step, 1)
                dve.wait_ge(dve_step, n_step[0])

            V.memset(small[:, 40:41], EPS)
            V.memset(ones[:, :], 1.0).then_inc(ones_set, 1)

            def squares(r, k):
                t0 = META if r else 0
                dve.wait_ge(sq_done, KT * r + k + 1)
                if k == 0:
                    V.tensor_copy(rstd[:, t0:], sq[:, t0:]).then_inc(sq_used, 1)
                    return
                dve.wait_ge(sq_used, KT * r + k)
                V.tensor_tensor(rstd[:, t0:], rstd[:, t0:], sq[:, t0:], ALU.add).then_inc(sq_used, 1)

            def norm(r, raw, g, split=True):
                dve.wait_ge(rms_done, r + 1)
                t0 = META if r else 0
                link(V.reciprocal(rstd[:, t0:], rstd[:, t0:]))
                for k in range(KT):
                    V.scalar_tensor_tensor(raw[:, k, t0 if split else 0:], x[:, k, t0:], c_(g, k), rstd[:, t0:],
                                           ALU.mult, ALU.mult
                                           ).then_inc(nrm_done if split else y_done, 1)
                    if split and k:
                        lo(r, raw, k - 1)
                if split:
                    lo(r, raw, KT - 1)

            def lo(r, raw, k):
                dve.wait_ge(hi_done, 8 * r + k + 1)
                t0 = META if r else 0
                V.tensor_tensor(h_lo[:, k, t0:], raw[:, k, t0:], f(h_hi[:, k, t0:]), ALU.subtract
                                ).then_inc(lo_done, 1)

            for k in range(KT):
                squares(0, k)
            dve.wait_ge(const_in, CONSTS)
            V.tensor_copy(lmask[:, :, :], lmask_in[:, :, :]).then_inc(masks_in, 1)
            lam = col[:, COLS["lam"]:COLS["lam"] + KT]
            V.scalar_tensor_tensor(small[:, 16:24], lam, -1.0, lam, ALU.mult, ALU.max).then_inc(lam_abs, 1)
            norm(0, hn_raw, "norm1")
            dve.wait_ge(gl_done, 1)
            V.tensor_copy(halves(glT[:, :]), ps[0:RANK, 4:6, 0:H2]).then_inc(gl_copied, 1)
            dve.wait_ge(lsig, 1)
            link(V.scalar_tensor_tensor(gtmp[:, :, :].rearrange("p h t -> p (h t)"),
                                        cum[:, :, :].rearrange("p h t -> p (h t)"), 0.0,
                                        gtmp[:, :, :].rearrange("p h t -> p (h t)"), ALU.min, ALU.subtract))
            link(V.tensor_scalar(gtmp[:, :, :], gtmp[:, :, :], 1.0 / 16.0, None, ALU.mult))
            for h in range(HEADS):
                last = V.tensor_tensor_scan(cum[:, h, :], rst[:, :], gtmp[:, h, :], 0.0, ALU.mult, ALU.add)
            link(last)
            link(V.memset(attn[:, :, :, :], 0.0))
            V.memset(st_p[:, :, :], 0.0)
            for c in range(CT):
                w = P if c < CT - 1 else LAST
                dve.wait_ge(vt_done, c + 1)
                V.tensor_copy(v_nat[0:w, c, :].rearrange("p (a n) -> p a n", a=2),
                              ps[0:w, 4 + 2 * (c % 2):6 + 2 * (c % 2), :]).then_inc(vt_copied, 1)

            def level_views(buf, heads, lv):
                hs = HALF[lv - 1]
                span = level_span(lv)
                out = []
                if span == T:
                    v = buf[:, heads, :].rearrange("p h (n b) -> p (h n) b", b=2 * hs)
                    return [(v[:, :, 0:hs], v[:, :, hs:], v[:, :, hs - 1:hs])]
                for h in range(heads.start, heads.stop):
                    v = buf[:, h, 0:span].rearrange("p (n b) -> p n b", b=2 * hs)
                    out.append((v[:, :, 0:hs], v[:, :, hs:], v[:, :, hs - 1:hs]))
                return out

            all_h = slice(0, HEADS)

            def diffs(lv):
                hs = HALF[lv - 1]
                z = zed[lv % 2]
                for (z0, z1, _), (c0, c1, cm) in zip(level_views(z, all_h, lv), level_views(cum, all_h, lv)):
                    n = c0.shape[1]
                    V.tensor_tensor(z0, cm.to_broadcast([P, n, hs]), c0, ALU.subtract)
                    last = V.tensor_tensor(z1, c1, cm.to_broadcast([P, n, hs]), ALU.subtract)
                last.then_inc(diff_done, 1)

            def mults(lv):
                dve.wait_ge(exp_done, lv)
                z = zed[lv % 2]
                for (z0, z1, _), (_, q1, _), (k0, _, _) in zip(
                        level_views(z, all_h, lv), level_views(qk, all_h, lv),
                        level_views(qk, slice(HEADS, 2 * HEADS), lv)):
                    V.tensor_tensor(z0, z0, k0, ALU.mult)
                    last = V.tensor_tensor(z1, z1, q1, ALU.mult)
                last.then_inc(zed_done, 1)

            turn = [0]

            def keep(lv):
                for c, w in level_tiles(lv):
                    dve.wait_ge(a_done, turn[0] + 1)
                    bank = ps[0:w, 4 + turn[0] % 4, :].rearrange("p (h t) -> p h t", h=HEADS)[:, :, 0:w]
                    V.copy_predicated(attn[0:w, c, :, 0:w],
                                      lmask[0:w, lv, 0:w].unsqueeze(1).to_broadcast([w, HEADS, w]), bank
                                      ).then_inc(a_copied, 1)
                    turn[0] += 1

            for p in range(2):
                dve.wait_ge(pair_free[p], 5)
            dve.wait_ge(vt_done, CT)
            diffs(1)
            diffs(2)
            mults(1)
            mults(2)
            keep(0)
            for lv in range(3, 8):
                keep(lv - 2)
                dve.wait_ge(a_done, turns_to(lv - 2))
                diffs(lv)
                mults(lv)
            keep(6)
            for h in range(HEADS):
                V.tensor_copy(end_cum[:, h, 0:CT - 1], cum[:, h, 0:(CT - 1) * P].rearrange("p (c t) -> p c t", t=P)[:, :, P - 1])
                V.tensor_copy(end_cum[:, h, CT - 1:CT], cum[:, h, TP - 1:TP])
                last = V.tensor_copy(end_cum[:, h, CT:CT + NSEQ], cum[:, h, TP:].rearrange("p (s t) -> p s t", t=DEC)[:, :, DEC - 1])
            link(last)
            keep(7)
            for h in range(HEADS):
                for lo_, n, w, e in ((0, CT - 1, P, 0), ((CT - 1) * P, 1, PREST, CT - 1), (TP, NSEQ, DEC, CT)):
                    last = V.tensor_tensor(
                        zed[1][:, h, lo_:lo_ + n * w].rearrange("p (n t) -> p n t", t=w),
                        end_cum[:, h, e:e + n].unsqueeze(2).to_broadcast([P, n, w]),
                        cum[:, h, lo_:lo_ + n * w].rearrange("p (n t) -> p n t", t=w), ALU.subtract)
            last.then_inc(zed_done, 1)
            dve.wait_ge(qe_exp, 1)
            V.tensor_tensor(qk[:, 0:HEADS, :], qk[:, 0:HEADS, :], zed[0][:, :, :], ALU.mult).then_inc(qe_done, 1)
            dve.wait_ge(qe_exp, 2)
            V.tensor_tensor(qk[:, HEADS:, :], qk[:, HEADS:, :], zed[1][:, :, :], ALU.mult).then_inc(qe_done, 1)
            dve.wait_ge(end_done, 1)
            for c in range(CT):
                for hp in range(2):
                    dve.wait_ge(u_done, 2 * c + hp + 1)
                    if c:
                        dve.wait_ge(o_done, c + 1)
                        dve.wait_ge(s_done, 2 * c + hp)
                    for h in (2 * hp, 2 * hp + 1):
                        last = V.scalar_tensor_tensor(st_p[:, h, :], st_p[:, h, :], end_cum[:, h, c:c + 1],
                                                      ps[:, 7 - hp, (h % 2) * DV:(h % 2 + 1) * DV], ALU.mult, ALU.add)
                    last.then_inc(s_done, 1)
            for s in range(NSEQ):
                if s:
                    dve.wait_ge(u_done, 2 * (CT + s))
                else:
                    dve.wait_ge(k_nat_done, CT)
                V.tensor_scalar(k_seg[0:LAST, :], k_nat[0:LAST, :], segm[0:LAST, s:s + 1], None, ALU.mult
                                ).then_inc(kseg_done, 1)
                dve.wait_ge(si_done, s + 1)
                for hp in range(2):
                    dve.wait_ge(u_done, 2 * (CT + s) + hp + 1)
                    for h in (2 * hp, 2 * hp + 1):
                        last = V.scalar_tensor_tensor(st_s[s % 2][:, h, :], st_s[s % 2][:, h, :],
                                                      end_cum[:, h, CT + s:CT + s + 1],
                                                      ps[:, 7 - hp, (h % 2) * DV:(h % 2 + 1) * DV], ALU.mult, ALU.add)
                    last.then_inc(s_done, 1)
            dve.wait_ge(o_copied, CT)
            V.tensor_tensor(o[:, :, TP:], o[:, :, TP:], ps[:, 4, :].rearrange("p (g t) -> p g t", t=NSEQ * DEC),
                            ALU.add).then_inc(o_norm, 1)
            dve.wait_ge(rgw_in, 16 * 3)
            dve.wait_ge(lam_exp, 1)
            e_, zz, z2, acc, rate = (small[:, 8 * q:8 * q + 8] for q in (2, 3, 4, 6, 0))
            link(V.tensor_scalar(zz, e_, 2.0, None, ALU.add))
            link(V.reciprocal(zz, zz))
            link(V.tensor_tensor(zz, zz, e_, ALU.mult))
            link(V.tensor_tensor(z2, zz, zz, ALU.mult))
            link(V.memset(acc, 1.0 / 17))
            for q in (15, 13, 11, 9, 7, 5, 3, 1):
                link(V.tensor_tensor(acc, acc, z2, ALU.mult))
                link(V.tensor_scalar(acc, acc, 1.0 / q, None, ALU.add))
            link(V.tensor_tensor(acc, acc, zz, ALU.mult))
            link(V.tensor_scalar(zz, lam, -1.0, 0.0, ALU.mult, ALU.max))
            link(V.scalar_tensor_tensor(acc, acc, 2.0, zz, ALU.mult, ALU.add))
            link(V.tensor_scalar(rate, acc, -8.0, None, ALU.mult))
            V.tensor_scalar(small[:, 8:16], acc, 8.0, None, ALU.mult).then_inc(w2_done, 1)
            V.memset(xpad[:, :, 0:3], 0.0)
            link(V.tensor_copy(xpad[:, :, 3 + TP:].rearrange("p k (s c) -> p k s c", s=NSEQ)[:, :, :, 0:3],
                               c0sb[:, :, :, :]))
            V.tensor_copy(cfin[:, :, 0, :], xpad[:, :, TP:TP + 3])
            link(V.tensor_copy(cfin[:, :, 1:, :],
                               xpad[:, :, 3 + TP:].rearrange("p k (s c) -> p k s c", s=NSEQ)[:, :, :, DEC:]))
            def taps(k):
                xs = xpad[:, k, 3 + TP:].rearrange("p (s c) -> p s c", s=NSEQ)
                cs = xc[:, TP:].rearrange("p (s c) -> p s c", s=NSEQ)
                dve.wait_ge(tap0, 2 * k + 2)
                for tap in (2, 1, 0):
                    w = c_(f"cw{tap}", k)
                    a_ = V.scalar_tensor_tensor(xc[:, 0:TP], xpad[:, k, tap:tap + TP], w, xc[:, 0:TP],
                                                ALU.mult, ALU.add)
                    if tap == 0:
                        a_.then_inc(conv_done, 1)
                    b_ = V.scalar_tensor_tensor(cs, xs[:, :, tap:tap + DEC], w, cs, ALU.mult, ALU.add)
                    if tap:
                        link(b_)
                b_.then_inc(conv_done, 1)

            taps(0)
            for k in range(KT):
                dve.wait_ge(ri_done, 2 * k + 2)
                dve.wait_ge(conv_done, 2 * k + 2)
                link(V.tensor_tensor(ii[:, :], ii[:, :], xc[:, :], ALU.mult))
                dve.wait_ge(ae_done, 2 * k + 2)
                if k:
                    dve.wait_ge(ya_done, k)
                link(V.tensor_tensor(hh[:, :], aa[:, :], aa[:, :], ALU.mult))
                link(V.scalar_tensor_tensor(rr[:, :], hh[:, :], 1.0, rr[:, :], ALU.add, ALU.mult))
                V.tensor_scalar(rr[:, :], rr[:, :], 2.0 ** -100, None, ALU.max).then_inc(w2_done, 1)
                as_ = aa[:, TP:].rearrange("p (s c) -> p s c", s=NSEQ)[:, :, 0]
                us_ = ii[:, TP:].rearrange("p (s c) -> p s c", s=NSEQ)[:, :, 0]
                link(V.tensor_tensor(h0sb[:, k, :], h0sb[:, k, :], as_, ALU.mult))
                dve.wait_ge(sq2_done, k + 1)
                link(V.tensor_tensor(ii[:, :], ii[:, :], rr[:, :], ALU.mult))
                link(V.tensor_tensor(us_, us_, h0sb[:, k, :], ALU.add))
                link(V.memset(as_, 0.0))
                V.tensor_tensor_scan(hh[:, :], aa[:, :], ii[:, :], 0.0, ALU.mult, ALU.add).then_inc(w2_done, 1)
                if k < KT - 1:
                    taps(k + 1)
                dve.wait_ge(w2_done, 1 + 3 * k + 2)
                V.tensor_copy(hfin[:, k, 0:1], hh[:, TP - 1:TP])
                V.tensor_copy(hfin[:, k, 1:], hh[:, TP:].rearrange("p (s c) -> p s c", s=NSEQ)[:, :, DEC - 1]
                              ).then_inc(w2_done, 1)
                dve.wait_ge(pair_free[0], (N_GZ + 2 * k) // 2 + 2)
                V.tensor_tensor(ga[:, k, :], ga[:, k, :], hh[:, META:], ALU.mult).then_inc(ya_done, 1)
                dve.wait_ge(yhi_done, k + 1)
                V.tensor_tensor(y_lo[:, k, :], ga[:, k, :], f(y_hi[:, k, :]), ALU.subtract).then_inc(ylo_done, 1)
            dve.wait_ge(w2_done, 1 + 3 * KT)
            dve.sem_inc(states_done, 1)
            dve.wait_ge(zsa_in, 16)
            for m in range(KT):
                n = N_PA + m
                dve.wait_ge(tile_done, n + 1)
                V.tensor_tensor(halves(mix[:, m, :]), opair(n % 2), halves(zsa[:, m, :]), ALU.mult
                                ).then_inc(pair_free[n % 2], 1)
                if not m:
                    continue
                if m <= HEADS:
                    h = m - 1
                    dve.wait_ge(orms_done, h + 1)
                    link(V.reciprocal(rstd[:, META:], rstd[:, META:]))
                    for d in range(2):
                        oh = o[:, 2 * h + d, META:]
                        V.scalar_tensor_tensor(oh, oh, c_("gng", d), rstd[:, META:],
                                               ALU.mult, ALU.mult).then_inc(o_norm, 1)
                    dve.wait_ge(o_norm, 1 + 2 * (h + 1))
                    dve.wait_ge(sr_in, 16)
                    for k in (2 * h, 2 * h + 1):
                        V.tensor_tensor(o[:, k, META:], o[:, k, META:], sr[:, k, :], ALU.mult).then_inc(ya_done, 1)
                if m >= HEADS:
                    for k in (2 * (m - HEADS), 2 * (m - HEADS) + 1):
                        dve.wait_ge(yhi_done, KT + k + 1)
                        V.tensor_tensor(y2_lo[:, k, :], o[:, k, META:], f(y2_hi[:, k, :]), ALU.subtract
                                        ).then_inc(ylo_done, 1)
            dve.wait_ge(zsb_in, 16)
            for m in range(KT):
                n = N_PB + m
                dve.wait_ge(tile_done, n + 1)
                V.tensor_tensor(halves(prod), opair(n % 2), halves(zsb[:, m, :]), ALU.mult
                                ).then_inc(pair_free[n % 2], 1)
                dve.wait_ge(pair_free[n % 2], n // 2 + 2)
                V.tensor_tensor(mix[:, m, :], mix[:, m, :], prod, ALU.add).then_inc(mix_done, 1)
                dve.wait_ge(yhi_done, 2 * KT + m + 1)
                V.tensor_tensor(y_lo[:, m, :], mix[:, m, :], f(y_hi[:, m, :]), ALU.subtract).then_inc(ylo_done, 1)
            for m in range(KT):
                n = N_OUT + m
                dve.wait_ge(tile_done, n + 1)
                V.tensor_tensor(halves(x[:, m, META:]), halves(x[:, m, META:]), opair(m % 2), ALU.add
                                ).then_inc(pair_free[m % 2], 1)
                if m:
                    squares(1, m - 1)
            squares(1, KT - 1)
            norm(1, hn2_raw, "norm2")
            dve.wait_ge(lo_done, 2 * KT)
            V.memset(scores[:, CT - 1, :, :], 0.0).then_inc(sc_copied, 1)
            dve.wait_ge(sc_copied, 1)
            with dve.Fori(0, PH) as i:
                dve.wait_ge(sc_done, i + 1)
                for part in range(3):
                    nt = 2 if part < 2 else 1
                    w = P if part < 2 else OLAST
                    V.tensor_copy(
                        scores[0:w, 2 * part:2 * part + nt, ds(i * 2, 2), :],
                        ps[0:w, 4 + part, 0:nt * 2 * P].rearrange("p (c s k) -> p c s k", c=nt, s=2)
                    ).then_inc(sc_copied, 1)
            dve.wait_ge(sc_copied, 3 * PH + 1)
            LOWEST = -3.4028235e38
            STEPS = 21

            with dve.Fori(0, CT) as i:
                n_top = [0]

                def then(ins):
                    n_top[0] += 1
                    ins.then_inc(top_step, 1)
                    dve.wait_ge(top_step, i * STEPS + n_top[0])
                    dve.sem_inc(passed, 1)

                def best(n, vals, best_v, best_i):
                    for q in range(n):
                        last = V.max(best_v(q, 0), vals(q))
                    then(last)
                    for q in range(n):
                        last = V.max_index(best_i(q, 0), best_v(q, 0), vals(q))
                    then(last)
                    for q in range(n):
                        last = V.match_replace(vals(q), best_v(q, 0), vals(q), LOWEST)
                    then(last)
                    for q in range(n):
                        last = V.max(best_v(q, 8), vals(q))
                    then(last)
                    for q in range(n):
                        last = V.max_index(best_i(q, 8), best_v(q, 8), vals(q))
                    then(last)

                then(V.tensor_copy(work[:, :, :], scores[:, ds(i, 1), :, :].rearrange("p o q k -> p (o q) k")))
                best(2 * PH, lambda q: work[:, q, :], lambda q, s: tv[:, q, s:s + 8], lambda q, s: ti[:, q, s:s + 8])
                V.tensor_copy(tif[:, :, :], ti[:, :, :])
                tvs = tv[:, :, :].rearrange("p (h s) k -> p h s k", s=2)
                then(V.tensor_tensor(cand[:, :, :, :],
                                     tvs[:, :, 0, :].unsqueeze(3).to_broadcast([P, PH, TOPK, TOPK]),
                                     tvs[:, :, 1, :].unsqueeze(2).to_broadcast([P, PH, TOPK, TOPK]), ALU.add))
                best(PH, lambda q: cand[:, q, :, :].rearrange("p a b -> p (a b)"),
                     lambda q, s: cv[:, q, s:s + 8], lambda q, s: ci[:, q, s:s + 8])
                V.tensor_scalar(ca[:, 0, :, :], ci[:, :, :], 4, None, ALU.logical_shift_right)
                then(V.tensor_scalar(ca[:, 1, :, :], ci[:, :, :], 15, None, ALU.bitwise_and))
                then(V.tensor_copy(caf[:, :, :, :], ca[:, :, :, :]))
                tifs = tif[:, :, :].rearrange("p (h s) k -> p h s k", s=2)
                for side in range(2):
                    then(V.tensor_tensor(pick[:, :, :, :],
                                         iot[:, 0:TOPK].unsqueeze(1).unsqueeze(1).to_broadcast([P, PH, TOPK, TOPK]),
                                         caf[:, side, :, :].unsqueeze(3).to_broadcast([P, PH, TOPK, TOPK]),
                                         ALU.is_equal))
                    then(V.tensor_tensor(pick[:, :, :, :], pick[:, :, :, :],
                                         tifs[:, :, side, :].unsqueeze(2).to_broadcast([P, PH, TOPK, TOPK]),
                                         ALU.mult))
                    then(V.tensor_reduce(chosen[:, ds(i, 1), side, :].rearrange("p o j -> p (o j)"),
                                         pick[:, :, :, :].rearrange("p h k a -> p (h k) a"), AX, ALU.add))
                then(V.tensor_tensor(chosen[:, ds(i, 1), 2, :].rearrange("p o (h k) -> p (o h) k", h=PH),
                                     cv[:, :, :], cv[:, :, 0:1].to_broadcast([P, PH, TOPK]), ALU.subtract))
            assert n_top[0] == STEPS, n_top
            dve.sem_inc(picked, 1)
            dve.wait_ge(gate_exp, 1)
            for c in range(CT):
                last = V.tensor_reduce(sm[:, c, :], chosen[:, c, 2, :].rearrange("p (h k) -> p h k", h=PH), AX, ALU.add)
            link(last)
            link(V.reciprocal(sm[:, :, :], sm[:, :, :]))
            for c in range(CT):
                cg = chosen[:, c, 2, :].rearrange("p (h k) -> p h k", h=PH)
                last = V.tensor_tensor(cg, cg, sm[:, c, :].unsqueeze(2).to_broadcast([P, PH, TOPK]), ALU.mult)
            last.then_inc(chosen_done, 1)

            dve.wait_ge(gparts_done, 1)
            V.tensor_tensor(g_lo[:, :], chT[:, 2, :], f(g_hi[:, :]), ALU.subtract).then_inc(gparts_done, 1)

            def one_hots(q, n, wait=True):
                if wait:
                    dve.wait_ge(g_mm, n - (RING - 1))
                for buf, side in ((oh2[q], 1), (row1[q], 0)):
                    last = V.tensor_tensor(buf[:, :, :], iot[:, :].unsqueeze(1).to_broadcast([P, QT, NK]),
                                           chT[:, side, ds(n * QT, QT)].unsqueeze(2).to_broadcast([P, QT, NK]),
                                           ALU.is_equal)
                last.then_inc(oh_done, 1)
                dve.wait_ge(oh_done, 2 * n + 1)
                V.tensor_tensor(oh1[q][:, :, 0, :], row1[q][:, :, :],
                                f(g_hi[:, ds(n * QT, QT)]).unsqueeze(2).to_broadcast([P, QT, NK]), ALU.mult
                                ).then_inc(oh_done, 1)

            def gather_gates(q, n):
                dve.wait_ge(g_part, n + 1)
                gates_, parts = quad_views(q)
                V.tensor_tensor(gates_, gates_, parts[:, :, 0, :], ALU.add).then_inc(bank_read, 1)

            def gate_pass(i, more):
                for q in range(2 * BQ):
                    gather_gates(q, i * 2 * BQ + q)
                    if more or q + AHEAD < 2 * BQ:
                        one_hots((q + AHEAD) % RING, i * 2 * BQ + (q + AHEAD))

            for q in range(AHEAD):
                one_hots(q, q, wait=False)
            with dve.Fori(0, LOOP2 - 1) as i:
                gate_pass(i, True)
            gate_pass(LOOP2 - 1, False)

            def prepare(gg, g):
                dve.wait_ge(c_in[gg], (g - gg) * 16 + 32)
                a4 = c_act[gg][:, :, :].rearrange("p e (b t) -> p e b t", t=GB)
                V.tensor_tensor(a4, a4, c_gate[gg][:, :, :, :].rearrange("p b e t -> p e b t"), ALU.mult
                                ).then_inc(c_raw, 1)
                dve.wait_ge(c_hi_done, g + 1)
                V.tensor_tensor(c_lo[gg][:, :, :], c_act[gg][:, :, :], f(c_hi[gg][:, :, :]), ALU.subtract
                                ).then_inc(c_lo_done, 1)

            def gather(g):
                for d in range(KT):
                    dve.wait_ge(tile_done, g * 8 + (N_D + d + 1))
                    V.tensor_tensor(halves(x[:, d, META:]), halves(x[:, d, META:]), opair(d % 4), ALU.add
                                    ).then_inc(d_free[d % 4], 1)

            prepare(0, 0)
            for p in range(2):
                dve.wait_ge(pair_free[p], N_D // 2 + 1)
                dve.sem_inc(d_free[p], 1)
            dve.wait_ge(bank_read, CT + BQ * NGB)
            for p in range(2, 4):
                dve.sem_inc(d_free[p], 1)
            with dve.Fori(0, NGRP // 2 - 1) as i:
                for gg in range(2):
                    prepare(1 - gg, i * 2 + (gg + 1))
                    gather(i * 2 + gg)
            prepare(1, NGRP - 1)
            gather(NGRP - 2)
            gather(NGRP - 1)
            for k in range(KT):
                squares(2, k)
            norm(2, yraw, "normf", split=False)


def _tiles(w):
    n = w.shape[1] // P
    return w.reshape(KT, P, n, P).transpose(2, 1, 0, 3).reshape(n, P, D)


def _blocks(v):
    return v.reshape(-1, P).T


def kernel(**inputs):
    import concourse.bacc as _bacc
    from concourse.bass_utils import run_bass_kernel_spmd as _run

    a = {k: np.asarray(v) for k, v in inputs.items()}
    f4 = np.float32
    tokens = np.concatenate([a["meta"], a["x_prompt"][0], a["x_sample"].reshape(NSEQ * DEC, D)], axis=0)
    feat = lambda t: t.T.reshape(KT, P, -1).transpose(1, 0, 2)
    win = a["w_in"][0]
    offs = np.cumsum([0, D, D, HEADS * DK, HEADS * DK, HEADS * DV, HEADS * DV, RANK, D, D])
    xa, ga, q, k, v, r, gl, za, zb = (win[:, offs[i]:offs[i + 1]] for i in range(9))
    inter = lambda p, q_: np.stack([_tiles(p), _tiles(q_)], axis=1).reshape(2 * KT, P, D)
    trunk = np.concatenate([_tiles(w) for w in (q, k, v, xa, za, r)] + [inter(ga, zb)] + [
        _tiles(a[n][0]) for n in ("w_pa", "w_pb", "w_out", "peer_wq")])
    up = a["peer_u"][0].reshape(NK, NK, KT, P).transpose(0, 3, 2, 1).reshape(NK, P, D)
    down = a["peer_v"][0].reshape(NGRP, E1G, NK, KT, P).transpose(0, 3, 2, 1, 4).reshape(NGRP * KT, P, D)
    vec = {"norm1": a["norm1_g"][0], "cw0": a["conv_w"][0, 0], "cw1": a["conv_w"][0, 1], "cw2": a["conv_w"][0, 2],
           "cw3": a["conv_w"][0, 3], "cb": a["conv_b"][0], "ba": a["rg_ba"][0], "bx": a["rg_bx"][0],
           "lam": a["rg_lam"][0], "norm2": a["norm2_g"][0], "normf": a["normf_g"], "bg": a["gla_bg"][0],
           "gng": a["gla_norm_g"][0]}
    cols = np.concatenate([_blocks(vec[n]) for n in COLS], axis=1)
    s_, t_ = np.arange(P)[:, None], np.arange(P)[None, :]
    masks = np.stack([s_ == t_] + [(s_ // (2 * h) == t_ // (2 * h)) & (s_ % (2 * h) < h) & (t_ % (2 * h) >= h)
                                   for h in HALF], axis=1).astype(f4)
    reset = np.ones((P, T), f4)
    reset[:, list(range(0, CT * P, P)) + list(range(TP, T, DEC))] = 0.0
    rows = np.arange(P)[:, None] - PREST
    segmask = ((rows // DEC == np.arange(NSEQ)[None, :]) & (rows >= 0)).astype(f4)
    iota = np.broadcast_to(np.arange(P, dtype=f4)[None, :], (P, P))
    gates = np.zeros((P, 2, KT, P), f4)
    for g, w in enumerate((a["rg_wa"][0], a["rg_wx"][0])):
        for n in range(16):
            e = 64 * (n % 2)
            gates[e:e + 64, g, n // 2, e:e + 64] = w[n]
    keys = np.stack([a["peer_k1"][0], a["peer_k2"][0]], axis=1).transpose(3, 0, 1, 2)
    arrays = {
        "xT": feat(tokens), "trunk": trunk, "up": up, "down": down, "cols": cols, "masks": masks,
        "ident": np.eye(P, dtype=f4), "reset": reset, "segmask": segmask, "iota": iota,
        "wgl": gl.reshape(KT, P, RANK).transpose(1, 0, 2), "wg": a["gla_wg"][0], "gates": gates, "keys": keys,
        "conv0": a["state_conv"][0].transpose(2, 0, 1).reshape(KT, P, NSEQ, 3).transpose(1, 0, 2, 3),
        "h0": a["state_rglru"][0].T.reshape(KT, P, NSEQ).transpose(1, 0, 2),
        "gla0": a["state_gla"][0],
    }
    outs = {"yT": (P, KT, TO), "conv_out": (P, KT, 1 + NSEQ, 3), "h_out": (P, KT, 1 + NSEQ),
            "gla_p": (HEADS, DK, DV), "gla_s": (NSEQ, HEADS, DK, DV)}
    nc = _bacc.Bacc("TRN2", target_bir_lowering=False, num_devices=1)
    feed, args = {}, {}
    for name, arr in arrays.items():
        arr = np.ascontiguousarray(arr)
        feed["in_" + name] = arr
        args[name] = nc.dram_tensor("in_" + name, arr.shape, mybir.dt.from_np(arr.dtype), kind="ExternalInput").ap()
    args["a_dram"] = nc.dram_tensor("act_scratch", (NK, P, TO), F32).ap()
    args["s_dram"] = nc.dram_tensor("sig_scratch", (3 * KT, P, TO), F32).ap()
    args["g_dram"] = nc.dram_tensor("gate_scratch", (NGB, P, NK * GB), F32).ap()
    for name, shape in outs.items():
        args[name] = nc.dram_tensor("out_" + name, shape, F32, kind="ExternalOutput").ap()
    build(nc, **args)
    res = _run(nc, [feed], core_ids=[0]).results[0]
    y = res["out_yT"].transpose(1, 0, 2).reshape(D, TO).T
    hs = res["out_h_out"].transpose(2, 1, 0).reshape(1 + NSEQ, D)
    cs = res["out_conv_out"].transpose(2, 3, 1, 0).reshape(1 + NSEQ, 3, D)
    return (np.ascontiguousarray(y[:SEQ])[None], np.ascontiguousarray(y[SEQ:]).reshape(NSEQ, DEC, D),
            cs[None, 0:1], hs[None, 0:1], res["out_gla_p"][None, None], cs[None, 1:], hs[None, 1:],
            res["out_gla_s"][None])
```

```python
import numpy as np

import concourse.bass as bass
from concourse import mybir
from concourse.bass import ds

F32 = mybir.dt.float32
F32R = mybir.dt.float32r
U8 = mybir.dt.uint8
U32 = mybir.dt.uint32
ALU = mybir.AluOpType
ACT = mybir.ActivationFunctionType
AX = mybir.AxisListType.X

P = 128
D = 1024
KT = D // P
META, SEQ = 16, 512
NSEQ, DEC = 8, 8
TP = META + SEQ
T = TP + NSEQ * DEC
H2 = T // 2
TO = T - META
HO = TO // 2
OLAST = TO % P
EPS = 1e-6
HEADS, DK, DV, RANK = 4, 128, 256, 16
CT = (T + P - 1) // P
LAST = T - (CT - 1) * P
PREST = TP - (CT - 1) * P
HALF = [64, 32, 16, 8, 4, 2, 1]
PH, NK, TOPK = 8, 128, 16
GB = 16
NGB = TO // GB
QT = 4
BQ = GB // QT
RING = 4
AHEAD = 3
E1G = 8
NGRP = NK // E1G

N_Q, N_K, N_V, N_XA, N_ZA, N_R, N_GZ, N_PA, N_PB, N_OUT, N_WQ, N_U, N_D, N_END = (
    0, 4, 8, 16, 24, 32, 40, 56, 64, 72, 80, 96, 224, 352)

LOOP1 = 52
LOOP2 = NGB // 2
TAIL = NK - LOOP1 - 4 * LOOP2
assert NGB == 2 * LOOP2 and TAIL == 4 and LOOP1 % 4 == 0
CONSTS = 16 * 7


def level_span(lv):
    hs = HALF[lv - 1]
    return (CT - 1) * P if hs > DEC else TP if hs == DEC else T


def level_tiles(lv):
    last = LAST if lv == 0 else level_span(lv) - (CT - 1) * P
    return [(c, P) for c in range(CT - 1)] + ([(CT - 1, last)] if last else [])


def turns_to(lv):
    return sum(len(level_tiles(v)) for v in range(lv + 1))


TURNS = turns_to(len(HALF))


COLS = {}
_n = 0
for _name, _w in (("norm1", 8), ("cw0", 8), ("cw1", 8), ("cw2", 8), ("cw3", 8), ("cb", 8), ("ba", 8), ("bx", 8),
                  ("lam", 8), ("norm2", 8), ("normf", 8), ("bg", 4), ("gng", 2)):
    COLS[_name] = _n
    _n += _w
NCOL = _n


def build(nc, xT, trunk, up, down, cols, masks, ident, reset, segmask, iota, wgl, wg, gates, keys, conv0, h0,
          gla0, a_dram, g_dram, s_dram, yT, conv_out, h_out, gla_p, gla_s):
    def sem(name):
        return nc.semaphore(name).__enter__()

    base = 16512
    TB = KT * T * 4

    def at(name, shape, dt, off):
        return nc.alloc_sbuf_tensor_at(name, shape, dt, offset=base + off)

    o_ring = 0
    w_raw = [at(f"w_raw{i}", [P, KT, P], F32, o_ring + 4096 * i) for i in range(4)]
    w_hi = [at(f"w_hi{i}", [P, KT, P], F32R, o_ring + 16384 + 4096 * i) for i in range(2)]
    w_lo = [at(f"w_lo{i}", [P, KT, P], F32R, o_ring + 24576 + 4096 * i) for i in range(2)]
    o_const = 32768
    col = at("col", [P, NCOL], F32, o_const)
    small = at("small", [P, 64], F32, o_const + 512)
    idt = at("idt", [P, P], F32, o_const + 1024)
    ones = at("ones", [P, P], F32, o_const + 1536)
    iot = at("iot", [P, P], F32, o_const + 2048)
    rstd = at("rstd", [P, T], F32, o_const + 2560)
    o_x = o_const + 2560 + 2368
    x = at("x", [P, KT, T], F32, o_x)
    o_h = o_x + TB
    h_hi = at("h_hi", [P, KT, T], F32R, o_h)
    h_lo = at("h_lo", [P, KT, T], F32R, o_h + TB)
    r3 = o_h + 2 * TB
    r4 = r3 + TB
    r5 = r4 + CT * D * 4
    r6 = r5 + TB
    XPW = 3 + TP + NSEQ * (3 + DEC)
    r7 = r6 + KT * XPW * 4 + 32
    xg_hi = at("xg_hi", [P, KT, T], F32R, r4)
    xg_lo = at("xg_lo", [P, KT, T], F32R, r5)
    qk = at("qk", [P, KT, T], F32, r3)
    y_hi = at("y_hi", [P, KT, TO], F32R, r3)
    v_nat = at("v_nat", [P, CT, D], F32, r4)
    y_lo = at("y_lo", [P, KT, TO], F32R, r4)
    vT = at("vT", [P, KT, T], F32, r5)
    zed = [at(f"zed{i}", [P, HEADS, T], F32, r5 + i * TB // 2) for i in range(2)]
    o = at("o", [P, KT, T], F32, r5)
    hn_raw = at("hn_raw", [P, KT, T], F32, r6)
    xpad = at("xpad", [P, KT, XPW], F32, r6)
    g7 = r7
    attn = at("attn", [P, CT, HEADS, P], F32, g7)
    gtmp = at("gtmp", [P, HEADS, T], F32, g7)
    cum = at("cum", [P, HEADS, T], F32, g7 + 10240)
    st_p = at("st_p", [P, HEADS, DV], F32, g7 + 19712)
    SB = 4
    st_s = [at(f"st_s{i}", [P, HEADS, DV], F32, (g7 + 23808, g7 + 27904, r3 + TB // 2, r3 + TB // 2 + 4096)[i])
            for i in range(SB)]
    lmask_in = at("lmask_in", [P, 8, P], F32, g7 + 27008)
    lmask = at("lmask", [P, 8, P], U8, g7 + 32000)
    k_nat = at("k_nat", [P, HEADS * DK], F32, g7 + 33024)
    k_seg = at("k_seg", [P, HEADS * DK], F32, g7 + 35072)
    end_cum = at("end_cum", [P, HEADS, 16], F32, g7 + 37120)
    segm = at("segm", [P, NSEQ], F32, o_const + 768)
    assert base + g7 + 37408 < 229368, g7
    wgl_sb = at("wgl_sb", [P, KT, RANK], F32, g7 + 19712)
    wg_sb = at("wg_sb", [RANK, HEADS * DK], F32, g7 + 20224)
    glT = at("glT", [RANK, T], F32, g7 + 22272)
    rst = at("rst", [P, T], F32, g7 + 24640)
    sq = at("sq", [P, T], F32, o_h + 8 * TB)
    stg = at("stg", [P, TO], F32, g7 + 37408)
    assert base + g7 + 37408 + 2368 < 229368
    ga = at("ga", [P, KT, TO], F32, r7 + 18432)
    sr = at("sr", [P, KT, TO], F32, r7)
    zsb = at("zsb", [P, KT, TO], F32, r7)
    mix = at("mix", [P, KT, TO], F32, o_h)
    zsa = at("zsa", [P, KT, TO], F32, o_h + TB)
    y2_hi = at("y2_hi", [P, KT, TO], F32R, r6)
    t7 = r7 + TB
    xc0 = at("xc0", [P, T], F32, r7)
    rr = at("rr", [P, T], F32, r7 + 2368)
    ii = at("ii", [P, T], F32, r7 + 2 * 2368)
    aa = at("aa", [P, T], F32, r7 + 3 * 2368)
    y2_lo = at("y2_lo", [P, KT, TO], F32R, t7)
    sq_o = at("sq_o", [P, 2, TO], F32, r6)
    c0sb = at("c0sb", [P, KT, NSEQ, 3], F32, r7 + 9472)
    gate_w = at("gate_w", [P, 2, KT, P], F32, r7 + 10240)
    h0sb = at("h0sb", [P, KT, NSEQ], F32, g7 + 39776)
    assert base + g7 + 39776 + 256 < 229368
    hfin = at("hfin", [P, KT, 1 + NSEQ], F32, r4 + TB + 256)
    cfin = at("cfin", [P, KT, 1 + NSEQ, 3], F32, r4 + TB + 544)
    assert t7 + 18432 <= g7 + 37408 and TO * KT * 4 == 18432 and TB + 544 + 864 <= CT * D * 4
    hh = rstd
    prod = rstd[:, META:]
    s3 = r3
    scores = at("scores", [P, CT, 16, NK], F32, s3)
    oh2 = [at(f"oh2{i}", [P, QT, NK], F32R, s3 + 2048 * i) for i in range(RING)]
    oh1 = [at(f"oh1{i}", [P, QT, 2, NK], F32R, s3 + 8192 + 4096 * i) for i in range(RING)]
    row1 = [at(f"row1{i}", [P, QT, NK], F32, s3 + 45568 + 2048 * i) for i in range(RING)]
    gst = [at(f"gst{i}", [P, NK, GB], F32, s3 + 24576 + 8192 * i) for i in range(2)]
    g_hi = at("g_hi", [P, TO], F32R, s3 + 40960)
    g_lo = at("g_lo", [P, TO], F32, s3 + 40960 + 2304)
    s4 = s3 + CT * 16 * NK * 4
    xg2 = at("xg2", [P, KT, TO], F32, s4)
    keys_sb = at("keys_sb", [P, PH, 2, NK], F32, r6 + 1024)
    qh = [at(f"qh{i}", [P, 2, TO], F32, r6 + 9216 + 4608 * i) for i in range(2)]
    n_hi = at("n_hi", [P, KT, TO], F32R, s3 + 76800)
    n_lo = at("n_lo", [P, KT, TO], F32R, s3 + 95232)
    assert s4 + TO * KT * 4 <= r6 + 1024 and r6 + 18432 <= s3 + 76800 and s3 + 113664 == o_h + 8 * TB
    work = at("work", [P, 16, NK], F32, s4)
    cand = at("cand", [P, PH, TOPK, TOPK], F32, s4 + 8192)
    pick = at("pick", [P, PH, TOPK, TOPK], F32, s4 + 16384)
    ast = [at(f"ast{i}", [P, TO], F32, o_h + 2304 * i) for i in range(4)]
    s5 = o_h + 4 * 2304
    chT = at("chT", [P, 3, TO], F32, s5)
    chosen = at("chosen", [P, CT, 3, P], F32, s5 + 6912)
    s6 = s5 + 6912 + 7680
    tv = at("tv", [P, 16, TOPK], F32, s6)
    ti = at("ti", [P, 16, TOPK], U32, s6 + 1024)
    tif = at("tif", [P, 16, TOPK], F32, s6 + 2048)
    cv = at("cv", [P, PH, TOPK], F32, s6 + 3072)
    ci = at("ci", [P, PH, TOPK], U32, s6 + 3584)
    ca = at("ca", [P, 2, PH, TOPK], U32, s6 + 4096)
    caf = at("caf", [P, 2, PH, TOPK], F32, s6 + 5120)
    sm = at("sm", [P, CT, PH], F32, s6 + 6144)
    assert s6 + 6304 <= s3
    CB = E1G * TO * 4
    c_off = [s3 - CB, s3 + 3 * CB, s3 + CB, s3 + 2 * CB, s3 + 76800, s3 + 95232, s3, o_h]
    place = ((0, 4), (1, 5), (2, 6), (3, 7))
    c_act, c_gate, c_hi, c_lo = (
        [at(f"{name}{i}", shape, dt, c_off[where[i]]) for i in range(2)] for name, shape, dt, where in (
            ("c_act", [P, E1G, TO], F32, place[0]), ("c_gate", [P, NGB, E1G, GB], F32, place[1]),
            ("c_hi", [P, E1G, TO], F32R, place[2]), ("c_lo", [P, E1G, TO], F32R, place[3])))
    assert 3 * CB >= 53760 and s3 + 4 * CB <= s3 + 76800 and s5 + 6912 <= s3 - CB and o_h + CB <= s3 - CB
    assert base + o_h + 8 * TB + 2368 < 229368
    yraw = at("yraw", [P, KT, TO], F32, o_h)

    ps = nc.alloc_psum_tensor("ps", [P, 8, 512], F32)

    def pair(p):
        return ps[:, 2 * p:2 * p + 2, 0:H2]

    def opair(p):
        return ps[:, 2 * p:2 * p + 2, 0:HO]

    def halves(ap):
        return ap.rearrange("p (a b) -> p a b", a=2)

    def block(buf, m):
        return buf[:, ds(m, 1), :].rearrange("p o (a b) -> p (o a) b", a=2)

    def f(ap):
        return ap.bitcast(F32)

    def quad_views(q):
        place_ = gst[q // BQ][:, :, QT * (q % BQ):QT * (q % BQ + 1)].rearrange("p e t -> p t e")
        return place_, ps[:, 4 + 2 * (q % 2):6 + 2 * (q % 2), :].rearrange("p a (t s e) -> p (a t) s e", s=2, e=NK)

    R_FIRST, R_AT, R_BY = 2, (0, 1, 2, 3), (0, 3)
    assert R_FIRST + len(R_AT) + len(R_BY) == KT

    def xc(k):
        return xpad[:, k - 1, 0:T] if k else xc0[:, :]

    def c_(name, k=0):
        j = COLS[name] + k
        return col[:, j:j + 1]

    x_in = [sem(f"x_in{i}") for i in range(4)]
    sig_stored, zsa_in, sr_in, zsb_in = (sem(n) for n in ("sig_stored", "zsa_in", "sr_in", "zsb_in"))
    col_in, const_in = sem("col_in"), sem("const_in")
    rgw_in = sem("rgw_in")
    keys_in = sem("keys_in")
    raw_in = [sem(f"raw_in{i}") for i in range(4)]
    w_hi_done = sem("w_hi_done")
    w_split = sem("w_split")
    tile_done = sem("tile_done")
    pair_free = [sem(f"pair_free{i}") for i in range(2)]
    ones_set = sem("ones_set")
    masks_in = sem("masks_in")
    passed = sem("passed")
    xg_done, xg_hi_done, xg_lo_done = (sem(n) for n in ("xg_done", "xg_hi_done", "xg_lo_done"))
    sq_done, sq_used, ms_done, rms_done, nrm_done, hi_done, lo_done = (
        sem(n) for n in ("sq_done", "sq_used", "ms_done", "rms_done", "nrm_done", "hi_done", "lo_done"))
    dve_step, act_step = sem("dve_step"), sem("act_step")
    gl_done, gl_copied, z_done, z_read, lsig = (
        sem(n) for n in ("gl_done", "gl_copied", "z_done", "z_read", "lsig"))
    vt_done, vt_copied = sem("vt_done"), sem("vt_copied")
    diff_done, exp_done, zed_done, a_done, a_copied = (
        sem(n) for n in ("diff_done", "exp_done", "zed_done", "a_done", "a_copied"))
    end_done, qe_exp, qe_done, kT_done, k_nat_done, o_done, o_copied, u_done, s_done, kseg_done, si_done = (
        sem(n) for n in ("end_done", "qe_exp", "qe_done", "kT_done", "k_nat_done", "o_done", "o_copied", "u_done",
                         "s_done", "kseg_done", "si_done"))
    gla_in = [sem(f"gla_in{i}") for i in range(SB)]
    gla_out = [sem(f"gla_out{i}") for i in range(SB)]
    glap_out = sem("glap_out")
    osq_done, osq_used, orms_done, o_norm = (sem(n) for n in ("osq_done", "osq_used", "orms_done", "o_norm"))
    tap0, conv_done, gates_done, ri_done, ae_done, w2_done, sq2_done, ya_done, yhi_done, ylo_done = (
        sem(n) for n in ("tap0", "conv_done", "gates_done", "ri_done", "ae_done", "w2_done", "sq2_done", "ya_done",
                         "yhi_done", "ylo_done"))
    conv_kept, states_done, mix_done, small_out = sem("conv_kept"), sem("states_done"), sem("mix_done"), sem("small_out")
    lam_abs, lam_exp = sem("lam_abs"), sem("lam_exp")
    sc_done, sc_copied = sem("sc_done"), sem("sc_copied")
    top_step, picked, gate_exp, chosen_done, ct_done, bank_read = (
        sem(n) for n in ("top_step", "picked", "gate_exp", "chosen_done", "ct_done", "bank_read"))
    a_stored = [sem(f"a_stored{i}") for i in range(4)]
    gparts_done, oh_done, ohg_done, g_mm, g_part, g_first = (
        sem(n) for n in ("gparts_done", "oh_done", "ohg_done", "g_mm", "g_part", "g_first"))
    g_stored = [sem(f"g_stored{i}") for i in range(2)]
    c_in = [sem(f"c_in{i}") for i in range(2)]
    c_raw, c_hi_done, c_lo_done = sem("c_raw"), sem("c_hi_done"), sem("c_lo_done")
    d_free = [sem(f"d_free{i}") for i in range(4)]
    y_done, y_out = sem("y_done"), sem("y_out")

    blk = nc.Block()
    with blk as b:

        @b.sync
        def _(sp):
            for i in range(4):
                sp.dma_start(x[:, 2 * i:2 * i + 2, :], xT[:, 2 * i:2 * i + 2, :]).then_inc(x_in[i], 16)

            def load(src, i, first, j):
                n = first + j if i is None else i * 4 + (first + j)
                if i is not None:
                    sp.wait_ge(w_split, n - 3)
                k = j if i is None else i * 4 + j
                sp.dma_start(w_raw[j][:, :, :], src[ds(k, 1), :, :].rearrange("o p (k m) -> p (o k) m", m=P)
                             ).then_inc(raw_in[j], 16)

            for j in range(4):
                load(trunk, None, 0, j)
            with sp.Fori(1, N_U // 4) as i:
                for j in range(4):
                    load(trunk, i, 0, j)
            with sp.Fori(0, (N_D - N_U) // 4) as i:
                for j in range(4):
                    load(up, i, N_U, j)
            with sp.Fori(0, (N_END - N_D) // 4) as i:
                for j in range(4):
                    load(down, i, N_D, j)
            for k in range(KT):
                sp.wait_ge(y_done, k + 1)
                sp.dma_start(yT[:, k, :], yraw[:, k, :]).then_inc(y_out, 16)
            sp.wait_ge(y_out, 16 * KT)

        @b.gpsimd
        def _(pool):
            def split(j, n, free=True):
                pool.wait_ge(raw_in[j], (n - j) * 4 + 16)
                if free:
                    pool.wait_ge(tile_done, n - 1)
                pool.sem_inc(passed, 1)
                nc.gpsimd.tensor_scalar(w_hi[j % 2][:, :, :], w_raw[j][:, :, :], 1.0, 1.0, ALU.mult, ALU.mult
                                        ).then_inc(w_hi_done, 1)
                pool.wait_ge(w_hi_done, n + 1)
                nc.gpsimd.tensor_tensor(w_lo[j % 2][:, :, :], w_raw[j][:, :, :], f(w_hi[j % 2][:, :, :]),
                                        ALU.subtract).then_inc(w_split, 1)

            for j in range(4):
                split(j, j, free=j >= 2)
            with pool.Fori(1, N_END // 4) as i:
                for j in range(4):
                    split(j, i * 4 + j)

        @b.tensor
        def _(pe):
            def product(j, n, hi, lo, p, ready=None, every=False):
                pe.wait_ge(w_split, n + 1)
                s = j % 2
                w = H2 if every else HO
                t0 = hi.shape[2] - 2 * w
                for k in range(KT):
                    if ready:
                        ready(k)
                    for part, (wt, act) in enumerate(((w_hi[s], hi), (w_hi[s], lo), (w_lo[s], hi))):
                        for a in range(2):
                            last = nc.tensor.matmul(
                                ps[:, 2 * p + a, 0:w], wt[:, k, :], act[:, k, t0 + a * w:t0 + (a + 1) * w],
                                start=k == 0 and part == 0, stop=k == KT - 1 and part == 2)
                last.then_inc(tile_done, 1)

            def stage(first, count, operand, ready=None, every=False):
                with pe.Fori(0, count // 4) as i:
                    for j in range(4):
                        pe.wait_ge(pair_free[j % 2], i * 2 + (first // 2 + j // 2 + 1))
                        product(j, i * 4 + (first + j), *operand(j), j % 2, ready if j == 0 else None, every)

            def norm(r):
                pe.wait_ge(sq_used, KT * (r + 1))
                w = H2 if r == 0 else HO
                for a in range(2):
                    last = nc.tensor.matmul(ps[:, 4 + a, 0:w], ones[:, :], rstd[:, T - (2 - a) * w:T - (1 - a) * w],
                                            start=True, stop=True)
                last.then_inc(ms_done, 1)

            def tile(n, act=(h_hi, h_lo)):
                pe.wait_ge(pair_free[n % 2], n // 2 + 1)
                product(n, n, *act, n % 2)

            hn = lambda j: (h_hi, h_lo)
            pe.wait_ge(ones_set, 1)

            def queries_keys(n):
                pe.wait_ge(pair_free[n % 2], n // 2 + 1)
                product(n, n, xg_hi, xg_lo, n % 2, (lambda k: pe.wait_ge(xg_lo_done, k + 1)) if n == 0 else None,
                        every=True)

            queries_keys(0)
            norm(0)
            for n in range(1, 4):
                queries_keys(n)
            pe.wait_ge(nrm_done, KT)
            pe.wait_ge(const_in, CONSTS)
            pe.wait_ge(rms_done, 1)
            for a in range(2):
                for k in range(KT):
                    last = nc.tensor.matmul(ps[0:RANK, 4 + a, 0:H2], wgl_sb[:, k, :],
                                            hn_raw[:, k, a * H2:(a + 1) * H2], start=k == 0, stop=k == KT - 1)
            last.then_inc(gl_done, 1)
            pe.wait_ge(gl_copied, 1)
            for h in range(HEADS):
                if h >= 2:
                    pe.wait_ge(z_read, 2 * (h - 1))
                for a in range(2):
                    last = nc.tensor.matmul(ps[:, 4 + 2 * (h % 2) + a, 0:H2], wg_sb[:, h * DK:(h + 1) * DK],
                                            glT[:, a * H2:(a + 1) * H2], start=True, stop=True)
                last.then_inc(z_done, 1)
            for n in range(4, 8):
                queries_keys(n)
            stage(N_V, 8, hn, lambda k: pe.wait_ge(lo_done, k + 1), every=True)
            for p in range(2):
                pe.wait_ge(pair_free[p], N_XA // 2 + 1)
            pe.wait_ge(z_read, 2 * HEADS)
            for c in range(CT):
                w = P if c < CT - 1 else LAST
                if c >= 2:
                    pe.wait_ge(vt_copied, c - 1)
                for m in range(KT):
                    last = nc.tensor.transpose(ps[0:w, 4 + 2 * (c % 2) + m // 4, (m % 4) * P:(m % 4 + 1) * P],
                                               vT[:, m, c * P:c * P + w], idt[:, :])
                last.then_inc(vt_done, 1)
            stage(N_XA, 8, hn, every=True)
            pe.wait_ge(vt_copied, CT)
            turn = 0
            for lv in range(8):
                tile(N_ZA + lv)
                if lv:
                    pe.wait_ge(zed_done, lv)
                for c, w in level_tiles(lv):
                    if turn >= 4:
                        pe.wait_ge(a_copied, turn - 3)
                    for h in range(HEADS):
                        z, zk = (qk, HEADS + h) if lv == 0 else (zed[lv % 2], h)
                        last = nc.tensor.matmul(ps[0:w, 4 + turn % 4, h * P:h * P + w], z[:, zk, c * P:c * P + w],
                                                z[:, h, c * P:c * P + w], start=True, stop=True)
                    last.then_inc(a_done, 1)
                    turn += 1
            for n in range(R_FIRST):
                tile(N_R + n)
            pe.wait_ge(a_copied, turn)
            pe.wait_ge(qe_done, 2)
            for c in range(CT):
                w, np_ = (P, P) if c < CT - 1 else (LAST, PREST)
                if c:
                    pe.wait_ge(s_done, 2 * c)
                for h in range(HEADS):
                    last = nc.tensor.transpose(ps[0:w, 6, h * P:(h + 1) * P], qk[:, HEADS + h, c * P:c * P + w],
                                               idt[:, :])
                last.then_inc(kT_done, 1)
                if c in R_AT:
                    tile(N_R + R_FIRST + R_AT.index(c))
                if c:
                    pe.wait_ge(o_copied, c)
                for g in range(2 * HEADS):
                    h, d = g // 2, g % 2
                    b0 = 4 + g // 4
                    c0 = (g % 4) * P
                    last = nc.tensor.matmul(ps[:, b0, c0:c0 + w], v_nat[0:w, c, g * P:(g + 1) * P],
                                            attn[0:w, c, h, 0:w], start=True, stop=c == 0)
                    if c:
                        last = nc.tensor.matmul(ps[:, b0, c0:c0 + np_], st_p[:, h, d * P:(d + 1) * P],
                                                qk[:, h, c * P:c * P + np_], start=False, stop=True)
                last.then_inc(o_done, 1)
                pe.wait_ge(k_nat_done, c + 1)
                for hp in range(2):
                    for h in (2 * hp, 2 * hp + 1):
                        last = nc.tensor.matmul(ps[:, 7 - hp, (h % 2) * DV:(h % 2 + 1) * DV],
                                                k_nat[0:np_, h * DK:(h + 1) * DK],
                                                v_nat[0:np_, c, h * DV:(h + 1) * DV], start=True, stop=True)
                    last.then_inc(u_done, 1)
            pe.wait_ge(o_copied, CT)
            for s in range(NSEQ):
                if s in R_BY:
                    tile(N_R + KT - len(R_BY) + R_BY.index(s))
                pe.wait_ge(gla_in[s % SB], 16 * (s // SB + 1))
                for g in range(2 * HEADS):
                    h, d = g // 2, g % 2
                    t0 = TP + s * DEC
                    last = nc.tensor.matmul(ps[:, 4, g * 64 + s * DEC:g * 64 + (s + 1) * DEC],
                                            st_s[s % SB][:, h, d * P:(d + 1) * P], qk[:, h, t0:t0 + DEC],
                                            start=True, stop=True)
                last.then_inc(si_done, 1)
                pe.wait_ge(kseg_done, s + 1)
                pe.wait_ge(s_done, 2 * (CT + s))
                for hp in range(2):
                    for h in (2 * hp, 2 * hp + 1):
                        last = nc.tensor.matmul(ps[:, 7 - hp, (h % 2) * DV:(h % 2 + 1) * DV],
                                                k_seg[0:LAST, h * DK:(h + 1) * DK],
                                                v_nat[0:LAST, CT - 1, h * DV:(h + 1) * DV], start=True, stop=True)
                    last.then_inc(u_done, 1)
            pe.wait_ge(s_done, 2 * (CT + NSEQ))
            pe.wait_ge(o_norm, 1)
            pe.wait_ge(rgw_in, 16 * 3)
            for k in range(KT):
                pe.wait_ge(conv_done, 2 * (k + 1))
                if k:
                    pe.wait_ge(ri_done, 2 * k)
                for g in range(2):
                    for a in range(2):
                        last = nc.tensor.matmul(ps[:, 4 + 2 * g + a, 0:H2], gate_w[:, g, k, :],
                                                xc(k)[:, a * H2:(a + 1) * H2], start=True, stop=True)
                last.then_inc(gates_done, 1)
                tile(N_GZ + 2 * k)
                tile(N_GZ + 2 * k + 1)
            pe.wait_ge(ri_done, 2 * KT)
            for m in range(KT):
                n = N_PA + m
                pe.wait_ge(pair_free[n % 2], n // 2 + 1)
                product(n, n, y_hi, y_lo, n % 2, (lambda k: pe.wait_ge(ylo_done, k + 1)) if m == 0 else None)
                if m < HEADS:
                    h = m
                    if h >= 2:
                        pe.wait_ge(orms_done, h - 1)
                    for d in range(2):
                        pe.wait_ge(osq_done, 2 * h + d + 1)
                        for a in range(2):
                            last = nc.tensor.matmul(ps[:, 4 + 2 * (h % 2) + a, 0:HO], ones[:, :],
                                                    sq_o[:, d, a * HO:(a + 1) * HO], start=d == 0, stop=d == 1)
                        last.then_inc(osq_used, 1)
            stage(N_PB, 8, lambda j: (y2_hi, y2_lo), lambda k: pe.wait_ge(ylo_done, KT + k + 1))
            stage(N_OUT, 8, lambda j: (y_hi, y_lo), lambda k: pe.wait_ge(ylo_done, 2 * KT + k + 1))
            def queries(j, n, ready=None):
                pe.wait_ge(pair_free[j % 2], n // 2 + 1)
                product(j, n, h_hi, h_lo, j % 2, ready)

            def head_scores(hb, h):
                pe.wait_ge(pair_free[1], h + (N_WQ // 2 + 2))
                pe.wait_ge(sc_copied, h * 3 + 1)
                for c in range(CT):
                    w = P if c < CT - 1 else OLAST
                    for side in range(2):
                        last = nc.tensor.matmul(
                            ps[0:w, 4 + c // 2, ((c % 2) * 2 + side) * P:((c % 2) * 2 + side + 1) * P],
                            qh[hb][:, side, c * P:c * P + w],
                            keys_sb[:, ds(h, 1), side, :].rearrange("p o k -> p (o k)"), start=True, stop=True)
                last.then_inc(sc_done, 1)

            queries(0, N_WQ, lambda k: pe.wait_ge(xg_lo_done, KT + k + 1))
            norm(1)
            pe.wait_ge(keys_in, 16)
            pe.wait_ge(rms_done, 2)
            with pe.Fori(0, PH // 2 - 1) as i:
                for hb in range(2):
                    for t in (1, 2):
                        j = 2 * hb + t
                        pe.wait_ge(pair_free[j % 2], i * 2 + (N_WQ // 2 + j // 2 + 1))
                        product(j, i * 4 + (N_WQ + j), h_hi, h_lo, j % 2)
                    head_scores(hb, i * 2 + hb)
            queries(1, N_U - 3)
            queries(0, N_U - 2)
            head_scores(0, PH - 2)
            queries(1, N_U - 1)
            head_scores(1, PH - 1)
            pe.wait_ge(lo_done, 2 * KT)
            hn2 = lambda j: (n_hi, n_lo)
            stage(N_U, LOOP1, hn2)
            pe.wait_ge(sc_copied, 3 * PH + 1)
            pe.wait_ge(chosen_done, 1)
            for c in range(CT):
                w = P if c < CT - 1 else OLAST
                if c == 4:
                    pe.wait_ge(bank_read, 1)
                for q in range(3):
                    last = nc.tensor.transpose(ps[:, 4 + c % 4, q * P:q * P + w], chosen[0:w, c, q, :],
                                               idt[0:w, 0:w])
                last.then_inc(ct_done, 1)

            def gate_quad(q, n):
                pe.wait_ge(oh_done, 2 * n + 2)
                pe.wait_ge(ohg_done, n + 1)
                pe.wait_ge(bank_read, n + (CT - 1))
                for t in range(QT):
                    last = nc.tensor.matmul(ps[:, 4 + 2 * (q % 2) + t // 2, (t % 2) * 2 * P:(t % 2 + 1) * 2 * P],
                                            oh2[q][:, t, :], oh1[q][:, t, :, :].rearrange("p s e -> p (s e)"),
                                            start=True, stop=True)
                last.then_inc(g_mm, 1)

            pe.wait_ge(bank_read, CT)
            first = N_U + LOOP1
            with pe.Fori(0, LOOP2) as i:
                for j in range(4):
                    pe.wait_ge(pair_free[j % 2], i * 2 + (first // 2 + j // 2 + 1))

                    def quads(k):
                        if k in (2, 6):
                            q = 2 * j + k // 4
                            gate_quad(q % RING, i * 2 * BQ + q)

                    product(j, i * 4 + (first + j), n_hi, n_lo, j % 2, quads)
            stage(N_D - TAIL, TAIL, hn2)
            with pe.Fori(0, NGRP // 2) as i:
                for gg in range(2):
                    def expert_rows(k):
                        pe.wait_ge(c_lo_done, i * (2 * E1G) + (gg * E1G + k + 1))

                    for d in range(KT):
                        pe.wait_ge(d_free[d % 4], i * 4 + (2 * gg + d // 4 + 1))
                        product(d, i * 16 + (N_D + 8 * gg + d), c_hi[gg], c_lo[gg], d % 4,
                                expert_rows if d == 0 else None)
            norm(2)

        @b.scalar
        def _(act):
            A = nc.scalar.activation

            def step(ins, n):
                ins.then_inc(act_step, 1)
                act.wait_ge(act_step, n)

            loads = ((col[:, :], cols), (idt[:, :], ident), (iot[:, :], iota), (lmask_in[:, :, :], masks),
                     (rst[:, :], reset), (segm[:, :], segmask), (wgl_sb[:, :, :], wgl), (wg_sb[:, :], wg))
            assert CONSTS == 16 * (len(loads) - 1)
            for n, (dst, src) in enumerate(loads):
                act.dma_start(dst, src).then_inc(const_in if n else col_in, 16)
            for p in range(2):
                act.sem_inc(pair_free[p], 1)
            for j in range(4):
                act.sem_inc(a_stored[j], 16)
            for j in range(2):
                act.sem_inc(g_stored[j], 16)

            epsc = small[:, 40:41]

            def norm(r, raw, split=True):
                t0 = META if r else 0
                for k in range(KT):
                    if r == 0:
                        act.wait_ge(xg_done, k + 1)
                        A(xg_hi[:, k, :], hn_raw[:, k, :], ACT.Copy).then_inc(xg_hi_done, 1)
                    elif r == 1:
                        act.wait_ge(xg_done, KT + k + 1)
                        A(h_hi[:, k, META:], xg2[:, k, :], ACT.Copy).then_inc(xg_hi_done, 1)
                    else:
                        act.wait_ge(d_free[k % 4], 2 * NGRP + k // 4)
                    if r or k:
                        act.wait_ge(sq_used, KT * r + k)
                    A(sq[:, t0:], x[:, k, t0:], ACT.Square).then_inc(sq_done, 1)
                act.wait_ge(ms_done, r + 1)
                A(halves(rstd[:, t0:]), opair(2) if r else pair(2), ACT.Sqrt, bias=epsc, scale=1.0 / D
                  ).then_inc(rms_done, 1)
                if split:
                    for k in range(KT):
                        act.wait_ge(nrm_done, 8 * r + k + 1)
                        A((n_hi if r else h_hi)[:, k, :], raw[:, k, :], ACT.Copy).then_inc(hi_done, 1)

            act.wait_ge(ones_set, 1)
            norm(0, hn_raw)
            act.wait_ge(lam_abs, 1)
            A(small[:, 16:24], small[:, 16:24], ACT.Exp, scale=-1.0).then_inc(lam_exp, 1)
            act.wait_ge(const_in, CONSTS)
            for h in range(HEADS):
                act.wait_ge(z_done, h + 1)
                A(halves(cum[:, h, :]), pair(2 + h % 2), ACT.Identity, bias=c_("bg", h)).then_inc(z_read, 1)
                A(halves(gtmp[:, h, :]), pair(2 + h % 2), ACT.Abs, bias=c_("bg", h)).then_inc(z_read, 1)
            act.wait_ge(z_read, 2 * HEADS)
            step(A(gtmp[:, :, :], gtmp[:, :, :], ACT.Exp, scale=-1.0), 1)
            A(gtmp[:, :, :], gtmp[:, :, :], ACT.Ln, bias=1.0).then_inc(lsig, 1)
            act.wait_ge(masks_in, 1)
            with act.Fori(0, 4) as i:
                for j in range(2):
                    act.wait_ge(tile_done, i * 2 + (N_V + j + 1))
                    A(block(vT, i * 2 + j), pair(j), ACT.Copy).then_inc(pair_free[j], 1)
            def xa_tile(m):
                p = m % 2
                act.wait_ge(tile_done, N_XA + m + 1)
                A(xpad[:, m, 3:3 + H2], ps[:, 2 * p, 0:H2], ACT.Copy)
                A(xpad[:, m, 3 + H2:3 + TP], ps[:, 2 * p + 1, 0:TP - H2], ACT.Copy)
                A(xpad[:, m, 3 + TP:].rearrange("p (s c) -> p s c", s=NSEQ)[:, :, 3:],
                  ps[:, 2 * p + 1, TP - H2:H2].rearrange("p (s c) -> p s c", s=NSEQ), ACT.Copy
                  ).then_inc(pair_free[p], 1)

            def level_exp(lv):
                act.wait_ge(diff_done, lv)
                z = zed[lv % 2]
                span = level_span(lv)
                A(z[:, :, 0:span], z[:, :, 0:span], ACT.Exp).then_inc(exp_done, 1)

            for m in range(2):
                xa_tile(m)
                level_exp(m + 1)
            for m in range(2, KT):
                xa_tile(m)

            def to_dram(n, slot, func):
                act.wait_ge(tile_done, n + 1)
                if slot:
                    act.wait_ge(sig_stored, 16 * slot)
                A(halves(stg[:, :]), opair(n % 2), func).then_inc(pair_free[n % 2], 1)
                act.wait_ge(pair_free[n % 2], n // 2 + 2)
                act.dma_start(s_dram[slot, :, :], stg[:, :]).then_inc(sig_stored, 16)

            for m in range(KT):
                to_dram(N_ZA + m, m, ACT.Sigmoid)
                if 3 <= m + 2 <= 7:
                    level_exp(m + 2)
            act.wait_ge(a_done, TURNS)
            act.wait_ge(zed_done, 8)
            A(zed[0][:, :, :], cum[:, :, :], ACT.Exp).then_inc(qe_exp, 1)
            A(zed[1][:, :, :], zed[1][:, :, :], ACT.Exp).then_inc(qe_exp, 1)
            A(end_cum[:, :, 0:CT + NSEQ], end_cum[:, :, 0:CT + NSEQ], ACT.Exp).then_inc(end_done, 1)
            def state_in(s):
                act.dma_start(st_s[s % SB][:, :, :], gla0[s].rearrange("h k v -> k h v")
                              ).then_inc(gla_in[s % SB], 16)

            for s in range(2):
                state_in(s)
            for n in range(R_FIRST):
                to_dram(N_R + n, KT + n, ACT.Silu)
            for c in range(CT):
                w = P if c < CT - 1 else LAST
                act.wait_ge(kT_done, c + 1)
                if c:
                    act.wait_ge(u_done, 2 * c)
                A(k_nat[0:w, :], ps[0:w, 6, :], ACT.Copy).then_inc(k_nat_done, 1)
                if c == CT - 1:
                    for s in range(2, SB):
                        state_in(s)
                if c in R_AT:
                    n = R_FIRST + R_AT.index(c)
                    to_dram(N_R + n, KT + n, ACT.Silu)
                act.wait_ge(o_done, c + 1)
                if c == 0:
                    act.wait_ge(qe_done, 2)
                A(o[:, :, c * P:c * P + w],
                  ps[:, 4:6, :].rearrange("p a (g t) -> p (a g) t", g=4)[:, :, 0:w], ACT.Copy).then_inc(o_copied, 1)
            act.dma_start(c0sb[:, :, :, :], conv0).then_inc(rgw_in, 16)
            act.dma_start(h0sb[:, :, :], h0).then_inc(rgw_in, 16)
            act.dma_start(gate_w[:, :, :, :], gates).then_inc(rgw_in, 16)

            def first_tap(k):
                A(xc(k)[:, 0:TP], xpad[:, k, 3:3 + TP], ACT.Identity, bias=c_("cb", k), scale=c_("cw3", k)
                  ).then_inc(tap0, 1)
                A(xc(k)[:, TP:].rearrange("p (s c) -> p s c", s=NSEQ),
                  xpad[:, k, 3 + TP:].rearrange("p (s c) -> p s c", s=NSEQ)[:, :, 3:],
                  ACT.Identity, bias=c_("cb", k), scale=c_("cw3", k)).then_inc(tap0, 1)

            for s in range(NSEQ):
                if s in R_BY:
                    n = KT - len(R_BY) + R_BY.index(s)
                    to_dram(N_R + n, KT + n, ACT.Silu)
                act.wait_ge(s_done, 2 * (CT + s + 1))
                act.dma_start(gla_s[s].rearrange("h k v -> k h v"), st_s[s % SB][:, :, :]
                              ).then_inc(gla_out[s % SB], 16)
                if s == 0:
                    act.dma_start(gla_p.rearrange("h k v -> k h v"), st_p[:, :, :]).then_inc(glap_out, 16)
                elif s - 1 + SB < NSEQ:
                    act.wait_ge(gla_out[(s - 1) % SB], 16 * ((s - 1) // SB + 1))
                    state_in(s - 1 + SB)
                if s == NSEQ - 2:
                    act.wait_ge(w2_done, 1)
                    first_tap(0)
            for k in range(KT):
                if k < KT - 1:
                    act.wait_ge(conv_kept, 1)
                    act.wait_ge(conv_done, 2 * k + 2)
                    first_tap(k + 1)
                act.wait_ge(gates_done, k + 1)
                if k:
                    act.wait_ge(w2_done, 1 + 3 * k)
                A(halves(rr[:, :]), pair(2), ACT.Sigmoid, bias=c_("ba", k)).then_inc(ri_done, 1)
                A(halves(ii[:, :]), pair(3), ACT.Sigmoid, bias=c_("bx", k)).then_inc(ri_done, 1)
                act.wait_ge(ri_done, 2 * k + 2)
                A(aa[:, :], rr[:, :], ACT.Exp, scale=small[:, k:k + 1]).then_inc(ae_done, 1)
                A(rr[:, :], rr[:, :], ACT.Tanh, scale=small[:, 8 + k:9 + k]).then_inc(ae_done, 1)
                act.wait_ge(w2_done, 1 + 3 * k + 1)
                A(rr[:, :], rr[:, :], ACT.Sqrt).then_inc(sq2_done, 1)
                n = N_GZ + 2 * k
                act.wait_ge(tile_done, n + 1)
                if k == 0:
                    act.wait_ge(glap_out, 16)
                    for i in range(SB):
                        act.wait_ge(gla_out[i], 16 * (NSEQ // SB))
                A(halves(ga[:, k, :]), opair(0), ACT.Gelu).then_inc(pair_free[0], 1)
                act.wait_ge(ya_done, k + 1)
                A(y_hi[:, k, :], ga[:, k, :], ACT.Copy).then_inc(yhi_done, 1)
                to_dram(n + 1, 2 * KT + k, ACT.Sigmoid)
            act.wait_ge(sig_stored, 16 * 3 * KT)

            def from_dram(dst, first, done):
                act.dma_start(dst[:, :, :], s_dram[first:first + KT, :, :].rearrange("k p t -> p k t")
                              ).then_inc(done, 16)

            act.wait_ge(tile_done, N_PA)
            from_dram(zsa, 0, zsa_in)
            act.wait_ge(ylo_done, KT)
            from_dram(sr, KT, sr_in)
            act.wait_ge(states_done, 1)
            act.dma_start(conv_out, cfin[:, :, :, :]).then_inc(small_out, 16)
            act.dma_start(h_out, hfin[:, :, :]).then_inc(small_out, 16)
            for h in range(HEADS):
                for d in range(2):
                    if h:
                        act.wait_ge(osq_used, 2 * (h - 1) + d + 1)
                    A(sq_o[:, d, :], o[:, 2 * h + d, META:], ACT.Square).then_inc(osq_done, 1)
                act.wait_ge(osq_used, 2 * h + 2)
                if h:
                    act.wait_ge(o_norm, 1 + 2 * h)
                A(halves(rstd[:, META:]), opair(2 + h % 2), ACT.Sqrt, bias=epsc, scale=1.0 / DV).then_inc(orms_done, 1)
            for k in range(KT):
                act.wait_ge(ya_done, KT + k + 1)
                A(y2_hi[:, k, :], o[:, k, META:], ACT.Copy).then_inc(yhi_done, 1)
            act.wait_ge(small_out, 32)
            act.wait_ge(ya_done, 2 * KT)
            from_dram(zsb, 2 * KT, zsb_in)
            act.wait_ge(tile_done, N_PB)
            for m in range(KT):
                act.wait_ge(mix_done, m + 1)
                A(y_hi[:, m, :], mix[:, m, :], ACT.Copy).then_inc(yhi_done, 1)
            act.wait_ge(tile_done, N_OUT)
            act.dma_start(keys_sb[:, :, :, :], keys).then_inc(keys_in, 16)
            norm(1, xg2)
            act.wait_ge(sc_copied, 3 * PH + 1)

            def up_tiles(i0, i1, before=None, after=None):
                with act.Fori(i0, i1) as i:
                    for j in range(4):
                        if before:
                            before(j, i - i0)
                        act.wait_ge(tile_done, i * 4 + (N_U + j + 1))
                        act.wait_ge(a_stored[j], i * 16 + 16)
                        A(halves(ast[j][:, :]), opair(j % 2), ACT.Gelu).then_inc(pair_free[j % 2], 1)
                        act.wait_ge(pair_free[j % 2], i * 2 + (N_U // 2 + j // 2 + 2))
                        act.dma_start(a_dram[ds(i * 4 + j, 1), :, :].rearrange("o p t -> p (o t)"), ast[j][:, :]
                                      ).then_inc(a_stored[j], 16)
                        if after:
                            after(j, i - i0)

            up_tiles(0, LOOP1 // 4)
            act.wait_ge(picked, 1)
            A(chosen[:, :, 2, :], chosen[:, :, 2, :], ACT.Exp).then_inc(gate_exp, 1)
            for c in range(CT):
                act.wait_ge(ct_done, c + 1)
                w = P if c < CT - 1 else OLAST
                A(chT[:, :, c * P:c * P + w], ps[:, 4 + c % 4, 0:3 * P].rearrange("p (q t) -> p q t", q=3)[:, :, 0:w],
                  ACT.Copy).then_inc(bank_read, 1)

            act.wait_ge(bank_read, CT)
            A(g_hi[:, :], chT[:, 2, :], ACT.Copy).then_inc(gparts_done, 1)

            def gated(q, n):
                act.wait_ge(oh_done, 2 * n + 1)
                for t in range(QT):
                    last = A(oh1[q][:, t, 1, :], row1[q][:, t, :], ACT.Copy, scale=g_lo[:, ds(n * QT + t, 1)])
                last.then_inc(ohg_done, 1)

            def gates_out(j, i, more=True):
                for q in (2 * j, 2 * j + 1):
                    if q % BQ == 0:
                        act.wait_ge(g_stored[q // BQ], i * 16 + 16)
                    act.wait_ge(g_mm, i * 2 * BQ + (q + 1))
                    gates_, parts = quad_views(q)
                    A(gates_, parts[:, :, 1, :], ACT.Copy).then_inc(g_part, 1)
                    if more or q + AHEAD - 1 < 2 * BQ:
                        gated((q + AHEAD - 1) % RING, i * 2 * BQ + (q + AHEAD - 1))

            def store_gates(j, i):
                if j % 2 == 0:
                    return
                bb = j // 2
                act.wait_ge(bank_read, i * 2 * BQ + (CT + BQ * (bb + 1)))
                act.dma_start(g_dram[ds(i * 2 + bb, 1), :, :].rearrange("o p e -> p (o e)"),
                              gst[bb][:, :, :].rearrange("p e t -> p (e t)")).then_inc(g_stored[bb], 16)

            i0 = LOOP1 // 4
            def act_load(gg, g):
                act.dma_start(c_act[gg][:, :, :], a_dram[ds(g * E1G, E1G), :, :].rearrange("e p t -> p e t")
                              ).then_inc(c_in[gg], 16)

            for j in range(4):
                act.wait_ge(a_stored[j], 16 * (LOOP1 // 4 + 1))
            act_load(0, 0)
            act.sem_inc(c_in[0], 16)
            act.wait_ge(gparts_done, 2)
            for q in range(AHEAD - 1):
                gated(q, q)
            up_tiles(i0, i0 + LOOP2 - 1, gates_out, store_gates)
            up_tiles(i0 + LOOP2 - 1, i0 + LOOP2, lambda j, i: gates_out(j, i + (LOOP2 - 1), False),
                     lambda j, i: store_gates(j, i + (LOOP2 - 1)))

            def c_load(gg, g):
                act_load(gg, g)
                act.dma_start(c_gate[gg][:, :, :, :].rearrange("p b e t -> p b (e t)"),
                              g_dram[:, :, ds(g * (E1G * GB), E1G * GB)].rearrange("b p e -> p b e")
                              ).then_inc(c_in[gg], 16)

            def c_split(gg, g, experts=range(E1G)):
                for k in experts:
                    act.wait_ge(c_raw, g * E1G + (k + 1))
                    A(c_hi[gg][:, k, :], c_act[gg][:, k, :], ACT.Copy).then_inc(c_hi_done, 1)

            def first_split(j, i):
                if j == 0:
                    act.wait_ge(g_stored[0], 16 * (NGB // 2 + 1))
                    act.wait_ge(g_stored[1], 16 * (NGB // 2 + 1))
                c_split(0, 0, range(3 * j, min(3 * j + 3, E1G)))

            up_tiles(i0 + LOOP2, NK // 4, after=first_split)
            for j in range(4):
                act.wait_ge(a_stored[j], 16 * (NK // 4 + 1))
            act.wait_ge(tile_done, N_D)
            c_load(1, 1)
            with act.Fori(0, NGRP // 2 - 1) as i:
                for gg in range(2):
                    g = i * 2 + gg
                    act.wait_ge(c_lo_done, g * E1G + E1G)
                    c_load(gg, g + 2)
                    c_split(1 - gg, g + 1)
            c_split(1, NGRP - 1)
            norm(2, yraw, split=False)

        @b.vector
        def _(dve):
            V = nc.vector
            n_step = [0]

            def link(ins):
                n_step[0] += 1
                ins.then_inc(dve_step, 1)
                dve.wait_ge(dve_step, n_step[0])

            V.memset(small[:, 40:41], EPS)
            V.memset(ones[:, :], 1.0).then_inc(ones_set, 1)

            def squares(r, k):
                t0 = META if r else 0
                dve.wait_ge(sq_done, KT * r + k + 1)
                if k == 0:
                    V.tensor_copy(rstd[:, t0:], sq[:, t0:]).then_inc(sq_used, 1)
                    return
                dve.wait_ge(sq_used, KT * r + k)
                V.tensor_tensor(rstd[:, t0:], rstd[:, t0:], sq[:, t0:], ALU.add).then_inc(sq_used, 1)

            def lo(r, raw, k):
                dve.wait_ge(hi_done, 8 * r + k + 1)
                t0 = META if r else 0
                hi_, lo_ = (n_hi, n_lo) if r else (h_hi, h_lo)
                V.tensor_tensor(lo_[:, k, :], raw[:, k, :], f(hi_[:, k, :]), ALU.subtract
                                ).then_inc(lo_done, 1)

            dve.wait_ge(col_in, 16)
            for k in range(KT + 1):
                if k < KT:
                    dve.wait_ge(x_in[k // 2], 16)
                    V.tensor_scalar(hn_raw[:, k, :], x[:, k, :], c_("norm1", k), None, ALU.mult).then_inc(xg_done, 1)
                if k:
                    dve.wait_ge(xg_hi_done, k)
                    V.tensor_tensor(xg_lo[:, k - 1, :], hn_raw[:, k - 1, :], f(xg_hi[:, k - 1, :]), ALU.subtract
                                    ).then_inc(xg_lo_done, 1)
                    squares(0, k - 1)

            def queries_keys(n):
                dve.wait_ge(tile_done, n + 1)
                V.scalar_tensor_tensor(halves(qk[:, n, :]), pair(n % 2), DK ** -0.5 if n < 4 else 1.0,
                                       halves(rstd[:, :]), ALU.mult, ALU.mult).then_inc(pair_free[n % 2], 1)

            dve.wait_ge(rms_done, 1)
            link(V.reciprocal(rstd[:, :], rstd[:, :]))
            queries_keys(0)
            dve.wait_ge(xg_lo_done, KT)
            for k in range(KT):
                V.tensor_tensor(hn_raw[:, k, :], hn_raw[:, k, :], rstd[:, :], ALU.mult).then_inc(nrm_done, 1)
                if k:
                    lo(0, hn_raw, k - 1)
                if k in (0, 5):
                    queries_keys(1 + k // 5)
            lo(0, hn_raw, KT - 1)
            queries_keys(3)
            dve.wait_ge(const_in, CONSTS)
            V.tensor_copy(lmask[:, :, :], lmask_in[:, :, :]).then_inc(masks_in, 1)
            lam = col[:, COLS["lam"]:COLS["lam"] + KT]
            V.scalar_tensor_tensor(small[:, 16:24], lam, -1.0, lam, ALU.mult, ALU.max).then_inc(lam_abs, 1)
            dve.wait_ge(gl_done, 1)
            V.tensor_copy(halves(glT[:, :]), ps[0:RANK, 4:6, 0:H2]).then_inc(gl_copied, 1)
            for n in range(4, 8):
                queries_keys(n)
            dve.wait_ge(lsig, 1)
            link(V.scalar_tensor_tensor(gtmp[:, :, :].rearrange("p h t -> p (h t)"),
                                        cum[:, :, :].rearrange("p h t -> p (h t)"), 0.0,
                                        gtmp[:, :, :].rearrange("p h t -> p (h t)"), ALU.min, ALU.subtract))
            link(V.tensor_scalar(gtmp[:, :, :], gtmp[:, :, :], 1.0 / 16.0, None, ALU.mult))
            for h in range(HEADS):
                last = V.tensor_tensor_scan(cum[:, h, :], rst[:, :], gtmp[:, h, :], 0.0, ALU.mult, ALU.add)
            link(last)
            link(V.memset(attn[:, :, :, :], 0.0))
            V.memset(st_p[:, :, :], 0.0)
            for c in range(CT):
                w = P if c < CT - 1 else LAST
                dve.wait_ge(vt_done, c + 1)
                V.tensor_copy(v_nat[0:w, c, :].rearrange("p (a n) -> p a n", a=2),
                              ps[0:w, 4 + 2 * (c % 2):6 + 2 * (c % 2), :]).then_inc(vt_copied, 1)

            def level_views(buf, heads, lv):
                hs = HALF[lv - 1]
                span = level_span(lv)
                out = []
                if span == T:
                    v = buf[:, heads, :].rearrange("p h (n b) -> p (h n) b", b=2 * hs)
                    return [(v[:, :, 0:hs], v[:, :, hs:], v[:, :, hs - 1:hs])]
                for h in range(heads.start, heads.stop):
                    v = buf[:, h, 0:span].rearrange("p (n b) -> p n b", b=2 * hs)
                    out.append((v[:, :, 0:hs], v[:, :, hs:], v[:, :, hs - 1:hs]))
                return out

            all_h = slice(0, HEADS)

            def diffs(lv):
                hs = HALF[lv - 1]
                z = zed[lv % 2]
                for (z0, z1, _), (c0, c1, cm) in zip(level_views(z, all_h, lv), level_views(cum, all_h, lv)):
                    n = c0.shape[1]
                    V.tensor_tensor(z0, cm.to_broadcast([P, n, hs]), c0, ALU.subtract)
                    last = V.tensor_tensor(z1, c1, cm.to_broadcast([P, n, hs]), ALU.subtract)
                last.then_inc(diff_done, 1)

            def mults(lv):
                dve.wait_ge(exp_done, lv)
                z = zed[lv % 2]
                for (z0, z1, _), (_, q1, _), (k0, _, _) in zip(
                        level_views(z, all_h, lv), level_views(qk, all_h, lv),
                        level_views(qk, slice(HEADS, 2 * HEADS), lv)):
                    V.tensor_tensor(z0, z0, k0, ALU.mult)
                    last = V.tensor_tensor(z1, z1, q1, ALU.mult)
                last.then_inc(zed_done, 1)

            turn = [0]

            def keep(lv):
                for c, w in level_tiles(lv):
                    dve.wait_ge(a_done, turn[0] + 1)
                    bank = ps[0:w, 4 + turn[0] % 4, :].rearrange("p (h t) -> p h t", h=HEADS)[:, :, 0:w]
                    V.copy_predicated(attn[0:w, c, :, 0:w],
                                      lmask[0:w, lv, 0:w].unsqueeze(1).to_broadcast([w, HEADS, w]), bank
                                      ).then_inc(a_copied, 1)
                    turn[0] += 1

            for p in range(2):
                dve.wait_ge(pair_free[p], 5)
            dve.wait_ge(vt_done, CT)
            diffs(1)
            diffs(2)
            mults(1)
            mults(2)
            keep(0)
            for lv in range(3, 8):
                keep(lv - 2)
                dve.wait_ge(a_done, turns_to(lv - 2))
                diffs(lv)
                mults(lv)
            keep(6)
            for h in range(HEADS):
                V.tensor_copy(end_cum[:, h, 0:CT - 1], cum[:, h, 0:(CT - 1) * P].rearrange("p (c t) -> p c t", t=P)[:, :, P - 1])
                V.tensor_copy(end_cum[:, h, CT - 1:CT], cum[:, h, TP - 1:TP])
                last = V.tensor_copy(end_cum[:, h, CT:CT + NSEQ], cum[:, h, TP:].rearrange("p (s t) -> p s t", t=DEC)[:, :, DEC - 1])
            link(last)
            keep(7)
            for h in range(HEADS):
                for lo_, n, w, e in ((0, CT - 1, P, 0), ((CT - 1) * P, 1, PREST, CT - 1), (TP, NSEQ, DEC, CT)):
                    last = V.tensor_tensor(
                        zed[1][:, h, lo_:lo_ + n * w].rearrange("p (n t) -> p n t", t=w),
                        end_cum[:, h, e:e + n].unsqueeze(2).to_broadcast([P, n, w]),
                        cum[:, h, lo_:lo_ + n * w].rearrange("p (n t) -> p n t", t=w), ALU.subtract)
            last.then_inc(zed_done, 1)
            dve.wait_ge(qe_exp, 1)
            V.tensor_tensor(qk[:, 0:HEADS, :], qk[:, 0:HEADS, :], zed[0][:, :, :], ALU.mult).then_inc(qe_done, 1)
            dve.wait_ge(qe_exp, 2)
            V.tensor_tensor(qk[:, HEADS:, :], qk[:, HEADS:, :], zed[1][:, :, :], ALU.mult).then_inc(qe_done, 1)
            dve.wait_ge(end_done, 1)
            for c in range(CT):
                for hp in range(2):
                    dve.wait_ge(u_done, 2 * c + hp + 1)
                    if c:
                        dve.wait_ge(o_done, c + 1)
                        dve.wait_ge(s_done, 2 * c + hp)
                    for h in (2 * hp, 2 * hp + 1):
                        last = V.scalar_tensor_tensor(st_p[:, h, :], st_p[:, h, :], end_cum[:, h, c:c + 1],
                                                      ps[:, 7 - hp, (h % 2) * DV:(h % 2 + 1) * DV], ALU.mult, ALU.add)
                    last.then_inc(s_done, 1)
            dve.wait_ge(lam_exp, 1)
            e_, zz, z2, acc, rate = (small[:, 8 * q:8 * q + 8] for q in (2, 3, 4, 6, 0))
            link(V.tensor_scalar(zz, e_, 2.0, None, ALU.add))
            link(V.reciprocal(zz, zz))
            link(V.tensor_tensor(zz, zz, e_, ALU.mult))
            link(V.tensor_tensor(z2, zz, zz, ALU.mult))
            link(V.memset(acc, 1.0 / 17))
            for q in (15, 13, 11, 9, 7, 5, 3, 1):
                link(V.tensor_tensor(acc, acc, z2, ALU.mult))
                link(V.tensor_scalar(acc, acc, 1.0 / q, None, ALU.add))
            link(V.tensor_tensor(acc, acc, zz, ALU.mult))
            link(V.tensor_scalar(zz, lam, -1.0, 0.0, ALU.mult, ALU.max))
            link(V.scalar_tensor_tensor(acc, acc, 2.0, zz, ALU.mult, ALU.add))
            link(V.tensor_scalar(rate, acc, -8.0, None, ALU.mult))
            link(V.tensor_scalar(small[:, 8:16], acc, 8.0, None, ALU.mult))

            def conv_inputs():
                dve.wait_ge(rgw_in, 16 * 3)
                V.memset(xpad[:, :, 0:3], 0.0)
                link(V.tensor_copy(xpad[:, :, 3 + TP:].rearrange("p k (s c) -> p k s c", s=NSEQ)[:, :, :, 0:3],
                                   c0sb[:, :, :, :]))
                dve.sem_inc(w2_done, 1)

            def taps(k):
                xs = xpad[:, k, 3 + TP:].rearrange("p (s c) -> p s c", s=NSEQ)
                cs = xc(k)[:, TP:].rearrange("p (s c) -> p s c", s=NSEQ)
                dve.wait_ge(tap0, 2 * k + 2)
                for tap in (2, 1, 0):
                    w = c_(f"cw{tap}", k)
                    a_ = V.scalar_tensor_tensor(xc(k)[:, 0:TP], xpad[:, k, tap:tap + TP], w, xc(k)[:, 0:TP],
                                                ALU.mult, ALU.add)
                    if tap == 0:
                        a_.then_inc(conv_done, 1)
                    b_ = V.scalar_tensor_tensor(cs, xs[:, :, tap:tap + DEC], w, cs, ALU.mult, ALU.add)
                    if tap:
                        link(b_)
                b_.then_inc(conv_done, 1)

            for s in range(NSEQ):
                if s:
                    dve.wait_ge(u_done, 2 * (CT + s))
                else:
                    dve.wait_ge(k_nat_done, CT)
                if s == NSEQ - 2:
                    conv_inputs()
                V.tensor_scalar(k_seg[0:LAST, :], k_nat[0:LAST, :], segm[0:LAST, s:s + 1], None, ALU.mult
                                ).then_inc(kseg_done, 1)
                dve.wait_ge(si_done, s + 1)
                for hp in range(2):
                    dve.wait_ge(u_done, 2 * (CT + s) + hp + 1)
                    for h in (2 * hp, 2 * hp + 1):
                        last = V.scalar_tensor_tensor(st_s[s % SB][:, h, :], st_s[s % SB][:, h, :],
                                                      end_cum[:, h, CT + s:CT + s + 1],
                                                      ps[:, 7 - hp, (h % 2) * DV:(h % 2 + 1) * DV], ALU.mult, ALU.add)
                    last.then_inc(s_done, 1)
            dve.wait_ge(o_copied, CT)
            V.tensor_tensor(o[:, :, TP:], o[:, :, TP:], ps[:, 4, :].rearrange("p (g t) -> p g t", t=NSEQ * DEC),
                            ALU.add).then_inc(o_norm, 1)
            taps(0)
            V.tensor_copy(cfin[:, :, 0, :], xpad[:, :, TP:TP + 3])
            link(V.tensor_copy(cfin[:, :, 1:, :],
                               xpad[:, :, 3 + TP:].rearrange("p k (s c) -> p k s c", s=NSEQ)[:, :, :, DEC:]))
            dve.sem_inc(conv_kept, 1)
            for k in range(KT):
                if k < KT - 1:
                    taps(k + 1)
                dve.wait_ge(ri_done, 2 * k + 2)
                dve.wait_ge(conv_done, 2 * k + 2)
                link(V.tensor_tensor(ii[:, :], ii[:, :], xc(k), ALU.mult))
                dve.wait_ge(ae_done, 2 * k + 2)
                if k:
                    dve.wait_ge(ya_done, k)
                link(V.tensor_tensor(hh[:, :], aa[:, :], aa[:, :], ALU.mult))
                link(V.scalar_tensor_tensor(rr[:, :], hh[:, :], 1.0, rr[:, :], ALU.add, ALU.mult))
                V.tensor_scalar(rr[:, :], rr[:, :], 2.0 ** -100, None, ALU.max).then_inc(w2_done, 1)
                as_ = aa[:, TP:].rearrange("p (s c) -> p s c", s=NSEQ)[:, :, 0]
                us_ = ii[:, TP:].rearrange("p (s c) -> p s c", s=NSEQ)[:, :, 0]
                link(V.tensor_tensor(h0sb[:, k, :], h0sb[:, k, :], as_, ALU.mult))
                dve.wait_ge(sq2_done, k + 1)
                link(V.tensor_tensor(ii[:, :], ii[:, :], rr[:, :], ALU.mult))
                link(V.tensor_tensor(us_, us_, h0sb[:, k, :], ALU.add))
                link(V.memset(as_, 0.0))
                V.tensor_tensor_scan(hh[:, :], aa[:, :], ii[:, :], 0.0, ALU.mult, ALU.add).then_inc(w2_done, 1)
                dve.wait_ge(w2_done, 1 + 3 * k + 2)
                V.tensor_copy(hfin[:, k, 0:1], hh[:, TP - 1:TP])
                V.tensor_copy(hfin[:, k, 1:], hh[:, TP:].rearrange("p (s c) -> p s c", s=NSEQ)[:, :, DEC - 1]
                              ).then_inc(w2_done, 1)
                dve.wait_ge(pair_free[0], (N_GZ + 2 * k) // 2 + 2)
                V.tensor_tensor(ga[:, k, :], ga[:, k, :], hh[:, META:], ALU.mult).then_inc(ya_done, 1)
                dve.wait_ge(yhi_done, k + 1)
                V.tensor_tensor(y_lo[:, k, :], ga[:, k, :], f(y_hi[:, k, :]), ALU.subtract).then_inc(ylo_done, 1)
            dve.wait_ge(w2_done, 1 + 3 * KT)
            dve.sem_inc(states_done, 1)
            dve.wait_ge(zsa_in, 16)
            for m in range(KT):
                n = N_PA + m
                dve.wait_ge(tile_done, n + 1)
                V.tensor_tensor(halves(mix[:, m, :]), opair(n % 2), halves(zsa[:, m, :]), ALU.mult
                                ).then_inc(pair_free[n % 2], 1)
                if not m:
                    continue
                if m <= HEADS:
                    h = m - 1
                    dve.wait_ge(orms_done, h + 1)
                    link(V.reciprocal(rstd[:, META:], rstd[:, META:]))
                    for d in range(2):
                        oh = o[:, 2 * h + d, META:]
                        V.scalar_tensor_tensor(oh, oh, c_("gng", d), rstd[:, META:],
                                               ALU.mult, ALU.mult).then_inc(o_norm, 1)
                    dve.wait_ge(o_norm, 1 + 2 * (h + 1))
                    dve.wait_ge(sr_in, 16)
                    for k in (2 * h, 2 * h + 1):
                        V.tensor_tensor(o[:, k, META:], o[:, k, META:], sr[:, k, :], ALU.mult).then_inc(ya_done, 1)
                if m >= HEADS:
                    for k in (2 * (m - HEADS), 2 * (m - HEADS) + 1):
                        dve.wait_ge(yhi_done, KT + k + 1)
                        V.tensor_tensor(y2_lo[:, k, :], o[:, k, META:], f(y2_hi[:, k, :]), ALU.subtract
                                        ).then_inc(ylo_done, 1)
            dve.wait_ge(zsb_in, 16)
            for m in range(KT):
                n = N_PB + m
                dve.wait_ge(tile_done, n + 1)
                V.tensor_tensor(halves(prod), opair(n % 2), halves(zsb[:, m, :]), ALU.mult
                                ).then_inc(pair_free[n % 2], 1)
                dve.wait_ge(pair_free[n % 2], n // 2 + 2)
                V.tensor_tensor(mix[:, m, :], mix[:, m, :], prod, ALU.add).then_inc(mix_done, 1)
                dve.wait_ge(yhi_done, 2 * KT + m + 1)
                V.tensor_tensor(y_lo[:, m, :], mix[:, m, :], f(y_hi[:, m, :]), ALU.subtract).then_inc(ylo_done, 1)
            def split_xg(k):
                dve.wait_ge(xg_hi_done, KT + k + 1)
                V.tensor_tensor(h_lo[:, k, META:], xg2[:, k, :], f(h_hi[:, k, META:]), ALU.subtract
                                ).then_inc(xg_lo_done, 1)
                squares(1, k)

            def queries(hb, side, n):
                dve.wait_ge(tile_done, n + 1)
                V.tensor_tensor(halves(qh[hb][:, side, :]), opair(side), halves(rstd[:, META:]), ALU.mult
                                ).then_inc(pair_free[side], 1)

            for m in range(KT):
                n = N_OUT + m
                dve.wait_ge(tile_done, n + 1)
                V.tensor_tensor(halves(x[:, m, META:]), halves(x[:, m, META:]), opair(m % 2), ALU.add
                                ).then_inc(pair_free[m % 2], 1)
                dve.wait_ge(pair_free[m % 2], (N_OUT + m) // 2 + 2)
                V.tensor_scalar(xg2[:, m, :], x[:, m, META:], c_("norm2", m), None, ALU.mult).then_inc(xg_done, 1)
                if m:
                    split_xg(m - 1)
            split_xg(KT - 1)
            dve.wait_ge(rms_done, 2)
            link(V.reciprocal(rstd[:, META:], rstd[:, META:]))
            queries(0, 0, N_WQ)
            dve.wait_ge(xg_lo_done, 2 * KT)
            for k in range(KT):
                V.tensor_tensor(xg2[:, k, :], xg2[:, k, :], rstd[:, META:], ALU.mult).then_inc(nrm_done, 1)
                if k:
                    lo(1, xg2, k - 1)
                if k == 2:
                    queries(0, 1, N_WQ + 1)
            lo(1, xg2, KT - 1)
            V.memset(scores[:, CT - 1, :, :], 0.0).then_inc(sc_copied, 1)
            dve.wait_ge(sc_copied, 1)

            def copy_scores(h):
                dve.wait_ge(sc_done, h + 1)
                for part in range(3):
                    nt = 2 if part < 2 else 1
                    w = P if part < 2 else OLAST
                    V.tensor_copy(
                        scores[0:w, 2 * part:2 * part + nt, ds(h * 2, 2), :],
                        ps[0:w, 4 + part, 0:nt * 2 * P].rearrange("p (c s k) -> p c s k", c=nt, s=2)
                    ).then_inc(sc_copied, 1)

            queries(1, 0, N_WQ + 2)
            copy_scores(0)
            with dve.Fori(0, PH // 2 - 1) as i:
                for hb in (1, 2):
                    queries(hb % 2, 1, i * 4 + (N_WQ + 2 * hb + 1))
                    queries(1 - hb % 2, 0, i * 4 + (N_WQ + 2 * hb + 2))
                    copy_scores(i * 2 + hb)
            queries(1, 1, N_U - 1)
            copy_scores(PH - 1)
            dve.wait_ge(sc_copied, 3 * PH + 1)
            LOWEST = -3.4028235e38
            STEPS = 21

            with dve.Fori(0, CT) as i:
                n_top = [0]

                def then(ins):
                    n_top[0] += 1
                    ins.then_inc(top_step, 1)
                    dve.wait_ge(top_step, i * STEPS + n_top[0])
                    dve.sem_inc(passed, 1)

                def best(n, vals, best_v, best_i):
                    for q in range(n):
                        last = V.max(best_v(q, 0), vals(q))
                    then(last)
                    for q in range(n):
                        last = V.max_index(best_i(q, 0), best_v(q, 0), vals(q))
                    then(last)
                    for q in range(n):
                        last = V.match_replace(vals(q), best_v(q, 0), vals(q), LOWEST)
                    then(last)
                    for q in range(n):
                        last = V.max(best_v(q, 8), vals(q))
                    then(last)
                    for q in range(n):
                        last = V.max_index(best_i(q, 8), best_v(q, 8), vals(q))
                    then(last)

                then(V.tensor_copy(work[:, :, :], scores[:, ds(i, 1), :, :].rearrange("p o q k -> p (o q) k")))
                best(2 * PH, lambda q: work[:, q, :], lambda q, s: tv[:, q, s:s + 8], lambda q, s: ti[:, q, s:s + 8])
                V.tensor_copy(tif[:, :, :], ti[:, :, :])
                tvs = tv[:, :, :].rearrange("p (h s) k -> p h s k", s=2)
                then(V.tensor_tensor(cand[:, :, :, :],
                                     tvs[:, :, 0, :].unsqueeze(3).to_broadcast([P, PH, TOPK, TOPK]),
                                     tvs[:, :, 1, :].unsqueeze(2).to_broadcast([P, PH, TOPK, TOPK]), ALU.add))
                best(PH, lambda q: cand[:, q, :, :].rearrange("p a b -> p (a b)"),
                     lambda q, s: cv[:, q, s:s + 8], lambda q, s: ci[:, q, s:s + 8])
                V.tensor_scalar(ca[:, 0, :, :], ci[:, :, :], 4, None, ALU.logical_shift_right)
                then(V.tensor_scalar(ca[:, 1, :, :], ci[:, :, :], 15, None, ALU.bitwise_and))
                then(V.tensor_copy(caf[:, :, :, :], ca[:, :, :, :]))
                tifs = tif[:, :, :].rearrange("p (h s) k -> p h s k", s=2)
                for side in range(2):
                    then(V.tensor_tensor(pick[:, :, :, :],
                                         iot[:, 0:TOPK].unsqueeze(1).unsqueeze(1).to_broadcast([P, PH, TOPK, TOPK]),
                                         caf[:, side, :, :].unsqueeze(3).to_broadcast([P, PH, TOPK, TOPK]),
                                         ALU.is_equal))
                    then(V.tensor_tensor(pick[:, :, :, :], pick[:, :, :, :],
                                         tifs[:, :, side, :].unsqueeze(2).to_broadcast([P, PH, TOPK, TOPK]),
                                         ALU.mult))
                    then(V.tensor_reduce(chosen[:, ds(i, 1), side, :].rearrange("p o j -> p (o j)"),
                                         pick[:, :, :, :].rearrange("p h k a -> p (h k) a"), AX, ALU.add))
                then(V.tensor_tensor(chosen[:, ds(i, 1), 2, :].rearrange("p o (h k) -> p (o h) k", h=PH),
                                     cv[:, :, :], cv[:, :, 0:1].to_broadcast([P, PH, TOPK]), ALU.subtract))
            assert n_top[0] == STEPS, n_top
            dve.sem_inc(picked, 1)
            dve.wait_ge(gate_exp, 1)
            for c in range(CT):
                last = V.tensor_reduce(sm[:, c, :], chosen[:, c, 2, :].rearrange("p (h k) -> p h k", h=PH), AX, ALU.add)
            link(last)
            link(V.reciprocal(sm[:, :, :], sm[:, :, :]))
            for c in range(CT):
                cg = chosen[:, c, 2, :].rearrange("p (h k) -> p h k", h=PH)
                last = V.tensor_tensor(cg, cg, sm[:, c, :].unsqueeze(2).to_broadcast([P, PH, TOPK]), ALU.mult)
            last.then_inc(chosen_done, 1)

            dve.wait_ge(gparts_done, 1)
            V.tensor_tensor(g_lo[:, :], chT[:, 2, :], f(g_hi[:, :]), ALU.subtract).then_inc(gparts_done, 1)

            def one_hots(q, n, wait=True):
                if wait:
                    dve.wait_ge(g_mm, n - (RING - 1))
                for buf, side in ((oh2[q], 1), (row1[q], 0)):
                    last = V.tensor_tensor(buf[:, :, :], iot[:, :].unsqueeze(1).to_broadcast([P, QT, NK]),
                                           chT[:, side, ds(n * QT, QT)].unsqueeze(2).to_broadcast([P, QT, NK]),
                                           ALU.is_equal)
                last.then_inc(oh_done, 1)
                dve.wait_ge(oh_done, 2 * n + 1)
                V.tensor_tensor(oh1[q][:, :, 0, :], row1[q][:, :, :],
                                f(g_hi[:, ds(n * QT, QT)]).unsqueeze(2).to_broadcast([P, QT, NK]), ALU.mult
                                ).then_inc(oh_done, 1)

            def gather_gates(q, n, blkno):
                dve.wait_ge(g_part, n + 1)
                gates_, parts = quad_views(q)
                t0 = QT * (q % BQ)
                V.tensor_tensor(c_gate[0][:, ds(blkno, 1), :, t0:t0 + QT].rearrange("p o e t -> p (o t) e"),
                                gates_[:, :, 0:E1G], parts[:, :, 0, 0:E1G], ALU.add).then_inc(g_first, 1)
                dve.wait_ge(g_first, n + 1)
                V.tensor_tensor(gates_, gates_, parts[:, :, 0, :], ALU.add).then_inc(bank_read, 1)

            def gate_pass(i, more):
                for q in range(2 * BQ):
                    gather_gates(q, i * 2 * BQ + q, i * 2 + q // BQ)
                    if more or q + AHEAD < 2 * BQ:
                        one_hots((q + AHEAD) % RING, i * 2 * BQ + (q + AHEAD))

            for q in range(AHEAD):
                one_hots(q, q, wait=False)
            with dve.Fori(0, LOOP2 - 1) as i:
                gate_pass(i, True)
            gate_pass(LOOP2 - 1, False)

            def prepare(gg, g):
                dve.wait_ge(c_in[gg], (g - gg) * 16 + 32)
                for k in range(E1G + 1):
                    if k < E1G:
                        a3 = c_act[gg][:, k, :].rearrange("p (b t) -> p b t", t=GB)
                        V.tensor_tensor(a3, a3, c_gate[gg][:, :, k, :], ALU.mult).then_inc(c_raw, 1)
                    if k:
                        dve.wait_ge(c_hi_done, g * E1G + k)
                        V.tensor_tensor(c_lo[gg][:, k - 1, :], c_act[gg][:, k - 1, :], f(c_hi[gg][:, k - 1, :]),
                                        ALU.subtract).then_inc(c_lo_done, 1)

            def gather(g, feats=range(KT)):
                for d in feats:
                    dve.wait_ge(tile_done, g * 8 + (N_D + d + 1))
                    V.tensor_tensor(halves(x[:, d, META:]), halves(x[:, d, META:]), opair(d % 4), ALU.add
                                    ).then_inc(d_free[d % 4], 1)

            prepare(0, 0)
            for p in range(2):
                dve.wait_ge(pair_free[p], N_D // 2 + 1)
                dve.sem_inc(d_free[p], 1)
            dve.wait_ge(bank_read, CT + BQ * NGB)
            for p in range(2, 4):
                dve.sem_inc(d_free[p], 1)
            with dve.Fori(0, NGRP // 2 - 1) as i:
                for gg in range(2):
                    gather(i * 2 + gg, range(KT // 2))
                    prepare(1 - gg, i * 2 + (gg + 1))
                    gather(i * 2 + gg, range(KT // 2, KT))
            gather(NGRP - 2, range(KT // 2))
            prepare(1, NGRP - 1)
            gather(NGRP - 2, range(KT // 2, KT))
            for d in range(KT + 1):
                if d < KT:
                    gather(NGRP - 1, [d])
                if d:
                    squares(2, d - 1)
            dve.wait_ge(rms_done, 3)
            link(V.reciprocal(rstd[:, META:], rstd[:, META:]))
            for k in range(KT):
                V.scalar_tensor_tensor(yraw[:, k, :], x[:, k, META:], c_("normf", k), rstd[:, META:],
                                       ALU.mult, ALU.mult).then_inc(y_done, 1)


def _tiles(w):
    n = w.shape[1] // P
    return w.reshape(KT, P, n, P).transpose(2, 1, 0, 3).reshape(n, P, D)


def _blocks(v):
    return v.reshape(-1, P).T


def kernel(**inputs):
    import concourse.bacc as _bacc
    from concourse.bass_utils import run_bass_kernel_spmd as _run

    a = {k: np.asarray(v) for k, v in inputs.items()}
    f4 = np.float32
    tokens = np.concatenate([a["meta"], a["x_prompt"][0], a["x_sample"].reshape(NSEQ * DEC, D)], axis=0)
    feat = lambda t: t.T.reshape(KT, P, -1).transpose(1, 0, 2)
    win = a["w_in"][0]
    offs = np.cumsum([0, D, D, HEADS * DK, HEADS * DK, HEADS * DV, HEADS * DV, RANK, D, D])
    xa, ga, q, k, v, r, gl, za, zb = (win[:, offs[i]:offs[i + 1]] for i in range(9))
    inter = lambda p, q_: np.stack([_tiles(p), _tiles(q_)], axis=1).reshape(2 * KT, P, D)
    trunk = np.concatenate([_tiles(w) for w in (q, k, v, xa, za, r)] + [inter(ga, zb)] + [
        _tiles(a[n][0]) for n in ("w_pa", "w_pb", "w_out", "peer_wq")])
    up = a["peer_u"][0].reshape(NK, NK, KT, P).transpose(0, 3, 2, 1).reshape(NK, P, D)
    down = a["peer_v"][0].reshape(NGRP, E1G, NK, KT, P).transpose(0, 3, 2, 1, 4).reshape(NGRP * KT, P, D)
    vec = {"norm1": a["norm1_g"][0], "cw0": a["conv_w"][0, 0], "cw1": a["conv_w"][0, 1], "cw2": a["conv_w"][0, 2],
           "cw3": a["conv_w"][0, 3], "cb": a["conv_b"][0], "ba": a["rg_ba"][0], "bx": a["rg_bx"][0],
           "lam": a["rg_lam"][0], "norm2": a["norm2_g"][0], "normf": a["normf_g"], "bg": a["gla_bg"][0],
           "gng": a["gla_norm_g"][0]}
    cols = np.concatenate([_blocks(vec[n]) for n in COLS], axis=1)
    s_, t_ = np.arange(P)[:, None], np.arange(P)[None, :]
    masks = np.stack([s_ == t_] + [(s_ // (2 * h) == t_ // (2 * h)) & (s_ % (2 * h) < h) & (t_ % (2 * h) >= h)
                                   for h in HALF], axis=1).astype(f4)
    reset = np.ones((P, T), f4)
    reset[:, list(range(0, CT * P, P)) + list(range(TP, T, DEC))] = 0.0
    rows = np.arange(P)[:, None] - PREST
    segmask = ((rows // DEC == np.arange(NSEQ)[None, :]) & (rows >= 0)).astype(f4)
    iota = np.broadcast_to(np.arange(P, dtype=f4)[None, :], (P, P))
    gates = np.zeros((P, 2, KT, P), f4)
    for g, w in enumerate((a["rg_wa"][0], a["rg_wx"][0])):
        for n in range(16):
            e = 64 * (n % 2)
            gates[e:e + 64, g, n // 2, e:e + 64] = w[n]
    keys = np.stack([a["peer_k1"][0], a["peer_k2"][0]], axis=1).transpose(3, 0, 1, 2)
    arrays = {
        "xT": feat(tokens), "trunk": trunk, "up": up, "down": down, "cols": cols, "masks": masks,
        "ident": np.eye(P, dtype=f4), "reset": reset, "segmask": segmask, "iota": iota,
        "wgl": gl.reshape(KT, P, RANK).transpose(1, 0, 2), "wg": a["gla_wg"][0], "gates": gates, "keys": keys,
        "conv0": a["state_conv"][0].transpose(2, 0, 1).reshape(KT, P, NSEQ, 3).transpose(1, 0, 2, 3),
        "h0": a["state_rglru"][0].T.reshape(KT, P, NSEQ).transpose(1, 0, 2),
        "gla0": a["state_gla"][0],
    }
    outs = {"yT": (P, KT, TO), "conv_out": (P, KT, 1 + NSEQ, 3), "h_out": (P, KT, 1 + NSEQ),
            "gla_p": (HEADS, DK, DV), "gla_s": (NSEQ, HEADS, DK, DV)}
    nc = _bacc.Bacc("TRN2", target_bir_lowering=False, num_devices=1)
    feed, args = {}, {}
    for name, arr in arrays.items():
        arr = np.ascontiguousarray(arr)
        feed["in_" + name] = arr
        args[name] = nc.dram_tensor("in_" + name, arr.shape, mybir.dt.from_np(arr.dtype), kind="ExternalInput").ap()
    args["a_dram"] = nc.dram_tensor("act_scratch", (NK, P, TO), F32).ap()
    args["s_dram"] = nc.dram_tensor("sig_scratch", (3 * KT, P, TO), F32).ap()
    args["g_dram"] = nc.dram_tensor("gate_scratch", (NGB, P, NK * GB), F32).ap()
    for name, shape in outs.items():
        args[name] = nc.dram_tensor("out_" + name, shape, F32, kind="ExternalOutput").ap()
    build(nc, **args)
    res = _run(nc, [feed], core_ids=[0]).results[0]
    y = res["out_yT"].transpose(1, 0, 2).reshape(D, TO).T
    hs = res["out_h_out"].transpose(2, 1, 0).reshape(1 + NSEQ, D)
    cs = res["out_conv_out"].transpose(2, 3, 1, 0).reshape(1 + NSEQ, 3, D)
    return (np.ascontiguousarray(y[:SEQ])[None], np.ascontiguousarray(y[SEQ:]).reshape(NSEQ, DEC, D),
            cs[None, 0:1], hs[None, 0:1], res["out_gla_p"][None, None], cs[None, 1:], hs[None, 1:],
            res["out_gla_s"][None])
```
